# Optimizing a Trainium2 kernel written in Bass

```python
import math
import jax
import jax.numpy as jnp
from jax import lax
import numpy as np

D_MODEL = 1024
BATCH = 1
SEQ = 1024
DEPTH = 2
DEC_BATCH = 8
DEC_SEQ = 1
PAST_LEN = 2048
PAGE_SIZE = 128

D_A = D_MODEL // 2
HEAD_A = 64
H_A = D_A // HEAD_A
W_LORA = 32
A_LORA = 64
G_LORA = 96
RWKV_COLS = 3 * D_A + W_LORA + A_LORA + G_LORA
D_B = D_MODEL - D_A
HEAD_B = 64
H_B = D_B // HEAD_B
KV_HEADS = 2
Q_PER_KV = H_B // KV_HEADS
SWA_COLS = D_B + 2 * KV_HEADS * HEAD_B
PROJ_COLS = RWKV_COLS + SWA_COLS
WINDOW = 128
N_BUCKETS = 32
MAX_EXACT = 16
REL_MAX_DIST = 128
POOL_WINDOWS = (2, 4, 8, 16)
N_POOL_GROUPS = len(POOL_WINDOWS)
POOL_GROUP = D_MODEL // N_POOL_GROUPS
POOL_KEEP = max(POOL_WINDOWS) - 1
N_EXPERTS = 16
N_GROUPS = 4
EXPERTS_PER_GROUP = N_EXPERTS // N_GROUPS
TOP_K = 2
D_FF = 256
N_EVEN = (DEPTH + 1) // 2
N_ODD = DEPTH // 2
ALPHA = (2.0 * DEPTH) ** 0.25
BETA = (8.0 * DEPTH) ** -0.25
LN_EPS = 1e-5
LNX_EPS = 64e-5
NEG_INF = -1e30

kernel_name = 'hybrid_rwkv7_swa_pool_moe_step'

def layer_norm(x, g, b, eps=LN_EPS):
    xf = x.astype(jnp.float32)
    mu = xf.mean(-1, keepdims=True)
    var = jnp.square(xf - mu).mean(-1, keepdims=True)
    return ((xf - mu) * lax.rsqrt(var + eps) * g + b).astype(x.dtype)

def wkv7_scan(r, decay, k, v, a, b, S0):
    xs = tuple(jnp.moveaxis(t, 1, 0) for t in (r, decay, k, v, a, b))

    def step(S, inp):
        r_t, w_t, k_t, v_t, a_t, b_t = inp
        sa = jnp.einsum('bhij,bhj->bhi', S, a_t)
        S = S * w_t[:, :, None, :] + sa[..., None] * b_t[:, :, None, :] + v_t[..., None] * k_t[:, :, None, :]
        return S, jnp.einsum('bhij,bhj->bhi', S, r_t)

    S, ys = lax.scan(step, S0, xs)
    return jnp.moveaxis(ys, 0, 1), S

def rwkv7_mixer(m, S0, w0, w_w2, a0, w_a2, w_g2, k_k, k_a, r_k, lnx_g, lnx_b):
    Bn, T, _ = m.shape
    m = m.astype(jnp.float32)
    r, k, v, wd, ad, gd = jnp.split(m, [D_A, 2 * D_A, 3 * D_A, 3 * D_A + W_LORA, 3 * D_A + W_LORA + A_LORA], axis=-1)
    w_log = -jax.nn.softplus(-(w0 + jnp.tanh(wd) @ w_w2)) - 0.5
    decay = jnp.exp(-jnp.exp(w_log))
    a = jax.nn.sigmoid(a0 + ad @ w_a2)
    g = jax.nn.sigmoid(gd) @ w_g2
    heads = lambda t: t.reshape(Bn, T, H_A, HEAD_A)
    kk = heads(k * k_k)
    kk = kk / jnp.maximum(jnp.linalg.norm(kk, axis=-1, keepdims=True), 1e-12)
    k = k * (1.0 + (a - 1.0) * k_a)
    r, k, v, a, decay = heads(r), heads(k), heads(v), heads(a), heads(decay)
    y, S = wkv7_scan(r, decay, k, v, -kk, kk * a, S0.astype(jnp.float32))
    mu = y.mean(-1, keepdims=True)
    var = jnp.square(y - mu).mean(-1, keepdims=True)
    y = ((y - mu) * lax.rsqrt(var + LNX_EPS)).reshape(Bn, T, D_A) * lnx_g + lnx_b
    bonus = jnp.sum(r * k * r_k, axis=-1, keepdims=True) * v
    return (y + bonus.reshape(Bn, T, D_A)) * g, S

def t5_bucket(dist):
    n = jnp.maximum(dist, 0)
    scaled = jnp.log(jnp.maximum(n, MAX_EXACT).astype(jnp.float32) / MAX_EXACT) / math.log(REL_MAX_DIST / MAX_EXACT)
    large = jnp.minimum(MAX_EXACT + (scaled * (N_BUCKETS - MAX_EXACT)).astype(jnp.int32), N_BUCKETS - 1)
    return jnp.where(n < MAX_EXACT, n, large)

def window_attention(qb, kb, vb, q_pos, k_pos, sinks, rel_bias):
    s = jnp.einsum('bnqhgd,bnkhd->bnhgqk', qb, kb).astype(jnp.float32) * (HEAD_B ** -0.5)
    dist = q_pos[:, :, None] - k_pos[:, None, :]
    valid = (dist >= 0) & (dist <= WINDOW) & (k_pos[:, None, :] >= 0)
    nb, nq, nk = dist.shape
    bias = jnp.moveaxis(rel_bias.astype(jnp.float32)[t5_bucket(dist)], -1, 1).reshape(nb, KV_HEADS, Q_PER_KV, nq, nk)
    s = jnp.where(valid[None, :, None, None], s + bias[None], NEG_INF)
    sink = sinks.astype(jnp.float32).reshape(1, 1, KV_HEADS, Q_PER_KV, 1)
    m = jnp.maximum(s.max(-1), sink)
    p = jnp.exp(s - m[..., None])
    p = p / (p.sum(-1) + jnp.exp(sink - m))[..., None]
    return jnp.einsum('bnhgqk,bnkhd->bnqhgd', p, vb.astype(jnp.float32))

def swa_mixer(q, k, v, k_buf, v_buf, start_pos, sinks, rel_bias):
    Bn, T, _ = q.shape
    q = q.reshape(Bn, T, KV_HEADS, Q_PER_KV, HEAD_B)
    k = k.reshape(Bn, T, KV_HEADS, HEAD_B)
    v = v.reshape(Bn, T, KV_HEADS, HEAD_B)
    if k_buf is None:
        nb = T // WINDOW

        def band(t):
            cur = t.reshape(Bn, nb, WINDOW, KV_HEADS, HEAD_B)
            prev = jnp.concatenate([jnp.zeros_like(cur[:, :1]), cur[:, :-1]], axis=1)
            return jnp.concatenate([prev, cur], axis=2)

        qb = q.reshape(Bn, nb, WINDOW, KV_HEADS, Q_PER_KV, HEAD_B)
        kb, vb = band(k), band(v)
        q_pos = start_pos + jnp.arange(T).reshape(nb, WINDOW)
        k_pos = jnp.concatenate([q_pos - WINDOW, q_pos], axis=1)
        k_all, v_all = k, v
    else:
        w_buf = k_buf.shape[1]
        k_all = jnp.concatenate([k_buf.astype(k.dtype), k], axis=1)
        v_all = jnp.concatenate([v_buf.astype(v.dtype), v], axis=1)
        qb, kb, vb = q[:, None], k_all[:, None], v_all[:, None]
        q_pos = (start_pos + jnp.arange(T))[None]
        k_pos = (start_pos - w_buf + jnp.arange(w_buf + T))[None]
    o = window_attention(qb, kb, vb, q_pos, k_pos, sinks, rel_bias)
    return o.reshape(Bn, T, D_B), k_all[:, -WINDOW:], v_all[:, -WINDOW:]

def even_mixer(x, prev_row, S0, k_buf, v_buf, start_pos, prm, i):
    w_in = prm['w_in'][i]
    proj = x @ w_in
    pr = proj[..., :RWKV_COLS]
    prev = (prev_row.astype(x.dtype) @ w_in[:, :RWKV_COLS])[:, None]
    shifted = jnp.concatenate([prev, pr[:, :-1]], axis=1)
    mixed = pr + prm['tshift_mu'][i] * (shifted - pr)
    y_a, S = rwkv7_mixer(mixed, S0, prm['decay_w0'][i], prm['decay_w2'][i], prm['iclr_a0'][i], prm['iclr_a2'][i],
                         prm['gate_w2'][i], prm['k_k'][i], prm['k_a'][i], prm['r_k'][i], prm['lnx_g'][i], prm['lnx_b'][i])
    q, ks, vs = jnp.split(proj[..., RWKV_COLS:], [D_B, D_B + KV_HEADS * HEAD_B], axis=-1)
    y_b, k_new, v_new = swa_mixer(q, ks, vs, k_buf, v_buf, start_pos, prm['attn_sinks'][i], prm['rel_bias'])
    out = jnp.concatenate([y_a.astype(x.dtype), y_b.astype(x.dtype)], axis=-1) @ prm['w_out'][i]
    return out, x[:, -1], S, k_new, v_new

def pool_mixer(x, buf, start_pos, w_pool, pool_scale):
    Bn, T, D = x.shape
    xcat = x if buf is None else jnp.concatenate([buf.astype(x.dtype), x], axis=1)
    L = xcat.shape[1]
    base = start_pos - (L - T)
    cs = jnp.concatenate([jnp.zeros((Bn, 1, D), jnp.float32), jnp.cumsum(xcat.astype(jnp.float32), axis=1)], axis=1)
    t = jnp.arange(L - T, L)
    pos = base + t
    hi = cs[:, L - T + 1:]
    means = []
    for gi, w in enumerate(POOL_WINDOWS):
        cols = slice(gi * POOL_GROUP, (gi + 1) * POOL_GROUP)
        lo = jnp.take(cs[..., cols], jnp.maximum(t + 1 - w, 0), axis=1)
        cnt = jnp.minimum(w, pos + 1).astype(jnp.float32)[None, :, None]
        means.append((hi[..., cols] - lo) / cnt)
    pooled = jnp.concatenate(means, axis=-1) - x.astype(jnp.float32)
    mixed = jnp.einsum('btgc,gcd->btgd', pooled.reshape(Bn, T, N_POOL_GROUPS, POOL_GROUP),
                       w_pool.astype(jnp.float32)).reshape(Bn, T, D)
    return (mixed * pool_scale).astype(x.dtype), xcat[:, -POOL_KEEP:]

def moe_ffn(x, w_router, b_router, w_gate, w_up, w_down):
    Bn, T, D = x.shape
    xt = x.reshape(Bn * T, D)
    probs = jax.nn.softmax((xt @ w_router).astype(jnp.float32) + b_router, axis=-1)
    group_score = lax.top_k(probs.reshape(-1, N_GROUPS, EXPERTS_PER_GROUP), TOP_K)[0].sum(-1)
    best_group = jnp.argmax(group_score, axis=-1)
    in_group = (jnp.arange(N_EXPERTS) // EXPERTS_PER_GROUP)[None, :] == best_group[:, None]
    vals, idx = lax.top_k(jnp.where(in_group, probs, -1.0), TOP_K)
    gates = vals / vals.sum(-1, keepdims=True)
    dense_gate = jnp.sum(jax.nn.one_hot(idx, N_EXPERTS, dtype=jnp.float32) * gates[..., None], axis=1)
    y = jnp.zeros(xt.shape, jnp.float32)
    for e in range(N_EXPERTS):
        h = jax.nn.silu(xt @ w_gate[e]) * (xt @ w_up[e])
        y = y + dense_gate[:, e:e + 1] * (h @ w_down[e]).astype(jnp.float32)
    return y.astype(x.dtype).reshape(Bn, T, D)

def trunk(x, start_pos, st_rwkv, st_shift, c_k, c_v, st_pool, prm):
    Bn = x.shape[0]
    fresh = st_rwkv is None
    new_S, new_shift, new_k, new_v, new_pool = [], [], [], [], []
    for layer in range(DEPTH):
        i = layer // 2
        if layer % 2 == 0:
            S0 = jnp.zeros((Bn, H_A, HEAD_A, HEAD_A), jnp.float32) if fresh else st_rwkv[i]
            prev = jnp.zeros((Bn, D_MODEL), x.dtype) if fresh else st_shift[i]
            kb = None if fresh else c_k[i]
            vb = None if fresh else c_v[i]
            h, last, S, kn, vn = even_mixer(x, prev, S0, kb, vb, start_pos, prm, i)
            new_S.append(S)
            new_shift.append(last)
            new_k.append(kn)
            new_v.append(vn)
        else:
            h, pn = pool_mixer(x, None if fresh else st_pool[i], start_pos, prm['w_pool'][i], prm['pool_scale'][i])
            new_pool.append(pn)
        x = layer_norm(ALPHA * x + h, prm['ln_mix_g'][layer], prm['ln_mix_b'][layer])
        f = moe_ffn(x, prm['w_router'], prm['b_router'], prm['w_ex_gate'][layer], prm['w_ex_up'][layer], prm['w_ex_down'][layer])
        x = layer_norm(ALPHA * x + f, prm['ln_ffn_g'][layer], prm['ln_ffn_b'][layer])
    return x, jnp.stack(new_S), jnp.stack(new_shift), jnp.stack(new_k), jnp.stack(new_v), jnp.stack(new_pool)

def setup_inputs(seed: int = 0) -> dict:
    key = jax.random.key(seed)
    k = jax.random.split(key, 33)
    f32 = jnp.float32
    nrm = lambda kk, shape, s=1.0: s * jax.random.normal(kk, shape, f32)
    win_buf = min(WINDOW, PAST_LEN)
    head_profile = jnp.linspace(-6.0, 0.0, HEAD_A, dtype=f32)
    return {
        'x_prompt': nrm(k[0], (BATCH, SEQ, D_MODEL)),
        'x_sample': nrm(k[1], (DEC_BATCH, DEC_SEQ, D_MODEL)),
        'state_rwkv': nrm(k[2], (N_EVEN, DEC_BATCH, H_A, HEAD_A, HEAD_A), 0.3),
        'state_shift': nrm(k[3], (N_EVEN, DEC_BATCH, D_MODEL)),
        'cache_swa_k': nrm(k[4], (N_EVEN, DEC_BATCH, win_buf, KV_HEADS, HEAD_B)),
        'cache_swa_v': nrm(k[5], (N_EVEN, DEC_BATCH, win_buf, KV_HEADS, HEAD_B)),
        'state_pool': nrm(k[6], (N_ODD, DEC_BATCH, POOL_KEEP, D_MODEL)),
        'w_in': nrm(k[7], (N_EVEN, D_MODEL, PROJ_COLS), D_MODEL ** -0.5),
        'tshift_mu': jax.random.uniform(k[8], (N_EVEN, RWKV_COLS), f32),
        'decay_w0': jnp.tile(head_profile, (N_EVEN, H_A)) + nrm(k[9], (N_EVEN, D_A), 0.1),
        'decay_w2': nrm(k[10], (N_EVEN, W_LORA, D_A), 0.1),
        'iclr_a0': nrm(k[11], (N_EVEN, D_A), 0.2),
        'iclr_a2': nrm(k[12], (N_EVEN, A_LORA, D_A), A_LORA ** -0.5),
        'gate_w2': nrm(k[13], (N_EVEN, G_LORA, D_A), G_LORA ** -0.5),
        'k_k': 0.85 + nrm(k[14], (N_EVEN, D_A), 0.05),
        'k_a': 1.0 + nrm(k[15], (N_EVEN, D_A), 0.05),
        'r_k': nrm(k[16], (N_EVEN, H_A, HEAD_A), 0.1),
        'lnx_g': 1.0 + nrm(k[17], (N_EVEN, D_A), 0.1),
        'lnx_b': nrm(k[18], (N_EVEN, D_A), 0.1),
        'attn_sinks': nrm(k[19], (N_EVEN, H_B), 0.5),
        'rel_bias': nrm(k[20], (N_BUCKETS, H_B), 0.5),
        'w_out': nrm(k[21], (N_EVEN, D_MODEL, D_MODEL), D_MODEL ** -0.5 * BETA),
        'w_pool': nrm(k[22], (N_ODD, N_POOL_GROUPS, POOL_GROUP, POOL_GROUP), POOL_GROUP ** -0.5 * BETA),
        'pool_scale': 1.0 + nrm(k[23], (N_ODD, D_MODEL), 0.1),
        'ln_mix_g': 1.0 + nrm(k[24], (DEPTH, D_MODEL), 0.1),
        'ln_mix_b': nrm(k[25], (DEPTH, D_MODEL), 0.1),
        'ln_ffn_g': 1.0 + nrm(k[26], (DEPTH, D_MODEL), 0.1),
        'ln_ffn_b': nrm(k[27], (DEPTH, D_MODEL), 0.1),
        'w_router': nrm(k[28], (D_MODEL, N_EXPERTS), D_MODEL ** -0.5),
        'b_router': nrm(k[29], (N_EXPERTS,), 0.01),
        'w_ex_gate': nrm(k[30], (DEPTH, N_EXPERTS, D_MODEL, D_FF), D_MODEL ** -0.5),
        'w_ex_up': nrm(k[31], (DEPTH, N_EXPERTS, D_MODEL, D_FF), D_MODEL ** -0.5),
        'w_ex_down': nrm(k[32], (DEPTH, N_EXPERTS, D_FF, D_MODEL), D_FF ** -0.5 * BETA),
    }

def reference(x_prompt, x_sample, state_rwkv, state_shift, cache_swa_k, cache_swa_v, state_pool,
              w_in, tshift_mu, decay_w0, decay_w2, iclr_a0, iclr_a2, gate_w2, k_k, k_a, r_k, lnx_g, lnx_b,
              attn_sinks, rel_bias, w_out, w_pool, pool_scale, ln_mix_g, ln_mix_b, ln_ffn_g, ln_ffn_b,
              w_router, b_router, w_ex_gate, w_ex_up, w_ex_down):
    prm = dict(w_in=w_in, tshift_mu=tshift_mu, decay_w0=decay_w0, decay_w2=decay_w2, iclr_a0=iclr_a0,
               iclr_a2=iclr_a2, gate_w2=gate_w2, k_k=k_k, k_a=k_a, r_k=r_k, lnx_g=lnx_g, lnx_b=lnx_b,
               attn_sinks=attn_sinks, rel_bias=rel_bias, w_out=w_out, w_pool=w_pool, pool_scale=pool_scale,
               ln_mix_g=ln_mix_g, ln_mix_b=ln_mix_b, ln_ffn_g=ln_ffn_g, ln_ffn_b=ln_ffn_b,
               w_router=w_router, b_router=b_router, w_ex_gate=w_ex_gate, w_ex_up=w_ex_up, w_ex_down=w_ex_down)
    y_prompt, rwkv_p, shift_p, k_p, v_p, pool_p = trunk(x_prompt, 0, None, None, None, None, None, prm)
    y_sample, rwkv_s, shift_s, k_s, v_s, pool_s = trunk(x_sample, PAST_LEN, state_rwkv, state_shift,
                                                        cache_swa_k, cache_swa_v, state_pool, prm)
    return (y_prompt, y_sample, rwkv_p, rwkv_s, shift_p, shift_s, k_p, k_s, v_p, v_s, pool_p, pool_s)


_drawn_inputs = setup_inputs


def setup_inputs(seed=0):
    import zlib

    import numpy as np

    out = dict(_drawn_inputs(seed))
    spreads = {}
    factors = {'attn_sinks': 8.0}
    for name, (base, spread) in spreads.items():
        noise = np.random.default_rng([zlib.crc32(name.encode()), seed]).standard_normal(out[name].shape)
        drawn = base * np.exp(spread * noise) if base else spread * noise
        out[name] = jnp.asarray(drawn.astype(out[name].dtype))
    for name, factor in factors.items():
        out[name] = (out[name] * factor).astype(out[name].dtype)
    return out
```

```python
from contextlib import ExitStack
import math

import concourse.bass as bass
from concourse import mybir
import numpy as np

F32 = mybir.dt.float32
I32 = mybir.dt.int32
U32 = mybir.dt.uint32
ACT = mybir.ActivationFunctionType
ALU = mybir.AluOpType
AX = mybir.AxisListType.X

P = 128
D = 1024
KD = D // P
T = 1024
NT = T // P
NS = 8
TT = T + NS
TC = TT + NS
PC = TC + 1
S0C, V0C = T + 1, T + 1 + NS
DA = 512
HD = 64
HA = DA // HD
WL, AL, GL = 32, 64, 96
KVH = 2
QPK = 4
WIN = 128
NBUCK = 32
NEG = -1e30
POOLW = (2, 4, 8, 16)
KEEP = 15
E = 16
NG = 4
EPG = E // NG
FF = 256
ALPHA = (2.0 * 2) ** 0.25
LN_EPS = 1e-5
LNX_EPS = 64e-5
CH = 64
TILES = NT + 1
NBLK = (2 * TT + E * (P - 1)) // P
SLOTS = NBLK * P


def rows(i):
    return P if i < NT else NS


class Linked:

    def __init__(self, eng, sem):
        self.eng, self.sem, self.n = eng, sem, 0

    def __call__(self, ins):
        ins.then_inc(self.sem, 1)
        self.n += 1
        self.eng.wait_ge(self.sem, self.n)


class Memory:

    def __init__(self, nc, stage):
        self.nc, self.stage, self.ctx, self.sems = nc, stage, ExitStack(), []

    def __enter__(self):
        self.ctx.__enter__()
        return self

    def __exit__(self, *a):
        out = self.ctx.__exit__(*a)
        self.nc.clear_and_free_semaphores(self.sems)
        self.nc.all_engine_barrier()
        return out

    def sb(self, name, shape, dt=F32):
        return self.ctx.enter_context(self.nc.sbuf_tensor(f"{self.stage}_{name}", shape, dt))

    def psum(self, name, shape):
        return self.ctx.enter_context(self.nc.psum_tensor(f"{self.stage}_{name}", shape, F32))

    def sem(self, name):
        self.sems.append(self.nc.alloc_semaphore(f"{self.stage}_{name}"))
        return self.sems[-1]

    def block(self):
        return self.ctx.enter_context(self.nc.Block())


def by_partition(v, c):
    return v.rearrange("(c p) -> p c", c=c)


def project(nc, io, pr, pq, keep, const):
    w_in = io["w_in"][0]
    NR = 3 * DA
    slabs = [(0, 512), (512, 512), (1024, 512), (NR, WL + AL + GL), (NR + WL + AL + GL, 512),
             (NR + WL + AL + GL + 512, 256)]
    tiles = []
    for s in range(3):
        tiles += [(s, 128 * c, P, 4 * s + c) for c in range(4)]
    tiles += [(3, 0, WL + AL, 12), (3, WL + AL, GL, 13)]
    tiles += [(4, P * g, P, 14 + g) for g in range(QPK)]
    tiles += [(5, 0, P, 18), (5, 128, P, 19)]
    NW = 3
    QS = 4
    arrived = {s: 16 * sum((8 if z == QS else 1) for z in range(s % NW, s + 1, NW)) for s in range(len(slabs))}
    cols = [(0, 352), (352, 344), (696, 344)]
    with Memory(nc, "pj") as m:
        xt = m.sb("xt", [P, 3, D])
        xT = m.sb("xT", [P, KD, TC])
        w = m.sb("w", [P, NW, KD, 512])
        pb = m.psum("pb", [P, 8, 512])
        s_x = [m.sem(f"x{i}") for i in range(3)]
        s_w = [m.sem(f"w{i}") for i in range(NW)]
        s_id = m.sem("ident")
        s_tr = m.sem("transposed")
        s_xT = [m.sem(f"xT_copied{i}") for i in range(2)]
        s_mm = m.sem("product")
        s_ev = [m.sem(f"evacuated{i}") for i in range(2)]
        s_z = m.sem("zeroed")
        s_c = m.sem("consts")
        s_zero, s_slots, s_shift = m.sem("zero_tile"), m.sem("slots_zeroed"), m.sem("shift_out")
        zero = m.sb("zero", [P, D])
        block = m.block()
        xp = io["x_prompt"][0]
        n_out = len(tiles) * 3

        @block.sync
        def _(sp):
            def load_slab(s):
                c0, n = slabs[s]
                if s >= NW:
                    done = 3 * sum(t[0] <= s - NW for t in tiles)
                    sp.wait_ge(s_mm, done)
                src = w_in[:, c0:c0 + n].rearrange("(k p) n -> p k n", p=P)
                if s != QS:
                    sp.dma_start(w[:, s % NW, :, 0:n], src).then_inc(s_w[s % NW], 16)
                    return
                for h in range(KVH * QPK):
                    to = HD * (KVH * (h % QPK) + h // QPK)
                    sp.dma_start(w[:, s % NW, :, to:to + HD], src[:, :, HD * h:HD * h + HD]).then_inc(s_w[s % NW], 16)
            sp.dma_start(const["ident"][:, :], io["c_ident"]).then_inc(s_id, 16)
            for i in range(TILES):
                if i >= 3:
                    sp.wait_ge(s_tr, i - 2)
                if i < NT:
                    sp.dma_start(xt[:, i % 3, :], xp[P * i:P * i + P, :]).then_inc(s_x[i % 3], 16)
                else:
                    sp.dma_start(xt[0:NS, i % 3, :], io["x_sample"][:, 0, :]).then_inc(s_x[i % 3], 16)
                    sp.dma_start(xt[NS:2 * NS, i % 3, :], io["state_shift"][0]).then_inc(s_x[i % 3], 16)
                if i == 2:
                    load_slab(0)
                if i == 5:
                    load_slab(1)
            for s in range(2, len(slabs)):
                load_slab(s)

        @block.tensor
        def _(pe):
            pe.wait_ge(s_id, 16)
            for i in range(TILES):
                n = P if i < NT else 2 * NS
                pe.wait_ge(s_x[i % 3], 16 * (i // 3 + 1) if i < NT else 16 * (i // 3) + 32)
                if i >= 2:
                    pe.wait_ge(s_xT[i % 2], i // 2)
                for k in range(KD):
                    b = pb[:, 2 * (i % 2) + k // 4, 128 * (k % 4):128 * (k % 4) + n]
                    last = nc.tensor.transpose(b, xt[0:n, i % 3, 128 * k:128 * k + 128], const["ident"][0:n, 0:n])
                last.then_inc(s_tr, 1)
            pe.wait_ge(s_xT[0], 5)
            pe.wait_ge(s_xT[1], 4)
            at = 0
            seen = -1
            for (s, c0, mrows, _) in tiles:
                if s != seen:
                    pe.wait_ge(s_w[s % NW], arrived[s])
                    seen = s
                for (t0, tn) in cols:
                    if at >= 4:
                        pe.wait_ge(s_ev[at % 2], at // 2 - 1)
                    for k in range(KD):
                        last = nc.tensor.matmul(pb[0:mrows, 4 + at % 4, 0:tn], w[:, s % NW, k, c0:c0 + mrows], xT[:, k, t0:t0 + tn],
                                                start=(k == 0), stop=(k == KD - 1))
                    last.then_inc(s_mm, 1)
                    at += 1

        def evacuate(eng, copy, par):
            for i in range(par, TILES, 2):
                n = P if i < NT else 2 * NS
                eng.wait_ge(s_tr, i + 1)
                src = pb[:, 2 * par:2 * par + 2, :].rearrange("p b (k t) -> p (b k) t", k=4)[:, :, 0:n]
                copy(xT[:, :, P * i:P * i + n], src).then_inc(s_xT[par], 1)
            for at in range(par, n_out, 2):
                _, _, mrows, tile = tiles[at // 3]
                t0, tn = cols[at % 3]
                eng.wait_ge(s_mm, at + 1)
                dst = pr[0:mrows, tile, 1 + t0:1 + t0 + tn] if tile < 14 else pq[0:mrows, tile - 14, 1 + t0:1 + t0 + tn]
                copy(dst, pb[0:mrows, 4 + at % 4, 0:tn]).then_inc(s_ev[par], 1)

        @block.scalar
        def _(act):
            evacuate(act, nc.scalar.copy, 0)

        @block.vector
        def _(dve):
            nc.vector.memset(pr[:, :, 0:1], 0.0).then_inc(s_z, 1)
            evacuate(dve, nc.vector.tensor_copy, 1)

        @block.gpsimd
        def _(pool):
            nc.gpsimd.memset(zero[:, :], 0.0).then_inc(s_zero, 1)
            pool.wait_ge(s_zero, 1)
            pool.dma_start(io["slots_in"].rearrange("(b p) d -> p b d", p=P),
                           zero[:, :].unsqueeze(1).to_broadcast([P, NBLK, D])).then_inc(s_slots, 16)
            pool.dma_start(io["o_shift_prompt"][0], io["x_prompt"][0, T - 1:T, :]).then_inc(s_shift, 16)
            pool.dma_start(io["o_shift_sample"][0], io["x_sample"][:, 0, :]).then_inc(s_shift, 16)
            n = 0
            for name, (dst, src) in keep.items():
                pool.dma_start(dst, src, allow_slow_non_contiguous=True).then_inc(s_c, 16)
                n += 16
            pool.wait_ge(s_c, n)
            pool.wait_ge(s_slots, 16)
            pool.wait_ge(s_shift, 32)


def attend(nc, io, pq, yb, const):
    SC = HD ** -0.5
    H = KVH * QPK
    NB1 = NBUCK + 1
    VW = 384
    with Memory(nc, "at") as m:
        rb = m.sb("rel_bias_rows", [NB1, H])
        rbb = m.sb("rel_bias_wide", [NB1, H, P])
        oh = m.sb("bucket_onehot", [NB1, VW])
        bv = m.sb("bias_by_distance", [P, H, VW])
        bias = m.sb("bias", [P, H, 2 * WIN])
        sinks = m.sb("sinks", [P, H])
        vt = m.sb("v_rows", [P, NT + 1, P])
        s = m.sb("scores", [P, H, 2 * WIN])
        p = m.sb("probs", [P, H, 2 * WIN])
        pT = m.sb("probsT", [P, H, 2, P])
        st = m.sb("stats", [P, 6, H])
        kv_out = m.sb("kv_out", [P, 2, P])
        smp = m.sb("kv_sample", [NS, 2, P])
        pb = m.psum("pb", [P, 8, 512])
        names = ("in v_tr v_cp bias_ps bias_cp bias_wr bias_rd sc masked mx neg ex den prob ptr pcp o y out k0 chain"
                 " rbw rbw2 wr").split()
        q = {k: m.sem(k) for k in names}
        scr = io["bias_scratch"]
        block = m.block()

        @block.sync
        def _(sp):
            for v in range(KVH):
                sp.dma_start(rb[0:NBUCK, v::KVH], io["rel_bias"][:, QPK * v:QPK * v + QPK],
                             allow_slow_non_contiguous=True).then_inc(q["in"], 16)
                sp.dma_start(sinks[:, v::KVH], io["attn_sinks"][:, QPK * v:QPK * v + QPK].to_broadcast([P, QPK]),
                             allow_slow_non_contiguous=True)\
                    .then_inc(q["in"], 16)
            sp.dma_start(oh[:, :], io["c_onehot"]).then_inc(q["in"], 16)
            sp.dma_start(rb[NBUCK:NB1, :], io["c_neg"]).then_inc(q["in"], 16)
            sp.wait_ge(q["bias_cp"], H)
            sp.dma_start(scr.rearrange("h (p x) -> p h x", p=P), bv[:, :, :]).then_inc(q["bias_wr"], 16)
            sp.wait_ge(q["bias_wr"], 16)
            for h in range(H):
                src = scr[h, WIN - 1:WIN - 1 + P * (VW - 1)].rearrange("(p x) -> p x", x=VW - 1)[:, 0:2 * WIN]
                sp.dma_start(bias[:, h, :], src).then_inc(q["bias_rd"], 16)
            sp.wait_ge(q["k0"], 4)
            for j, name in enumerate(("k", "v")):
                sp.dma_start(io[f"o_{name}_prompt"][0, 0].rearrange("t h d -> t (h d)"), kv_out[:, j, :])\
                    .then_inc(q["out"], 16)
                dst = io[f"o_{name}_sample"][0].rearrange("b t h d -> b t (h d)")
                src = io[f"cache_swa_{name}"][0].rearrange("b t h d -> b t (h d)")
                sp.dma_start(dst[:, WIN - 1, :], smp[:, j, :]).then_inc(q["out"], 16)
                sp.dma_start(dst[:, 0:WIN - 1, :], src[:, 1:WIN, :]).then_inc(q["out"], 16)
            sp.wait_ge(q["out"], 96)

        @block.tensor
        def _(pe):
            ident = const["ident"]
            for n in range(NT):
                nc.tensor.transpose(pb[:, n // 4, 128 * (n % 4):128 * (n % 4) + 128],
                                    pq[:, 5, 1 + P * n:1 + P * n + P], ident[:, :])
            nc.tensor.transpose(pb[0:NS, 2, 0:P], pq[:, 5, S0C:S0C + NS], ident[:, :])
            nc.tensor.transpose(pb[:, 2, P:2 * P], pq[:, 4, 1 + T - P:1 + T], ident[:, :])
            nc.tensor.transpose(pb[0:NS, 2, 2 * P:3 * P], pq[:, 4, S0C:S0C + NS], ident[:, :]).then_inc(q["v_tr"], 1)
            pe.wait_ge(q["rbw"], 1)
            for h in range(H):
                if h >= 2:
                    pe.wait_ge(q["bias_cp"], h - 1)
                nc.tensor.matmul(pb[:, 6 + h % 2, 0:VW], rbb[:, h, :], oh[:, :], start=True, stop=True)\
                    .then_inc(q["bias_ps"], 1)
            pe.wait_ge(q["v_cp"], 1)
            pe.wait_ge(q["bias_cp"], H)
            for n in range(NT):
                if n >= 1:
                    pe.wait_ge(q["masked"], 4 * n)
                lo = 0 if n else P
                for mm in range(QPK):
                    for v in range(KVH):
                        c = 256 * (mm % 2)
                        last = nc.tensor.matmul(
                            pb[:, 2 * v + mm // 2, c + lo:c + 256],
                            pq[64 * v:64 * v + 64, mm, 1 + P * n:1 + P * n + P],
                            pq[64 * v:64 * v + 64, 4, 1 + P * (n - 1) + lo:1 + P * (n + 1)], start=True, stop=True)
                    last.then_inc(q["sc"], 1)
                pe.wait_ge(q["prob"], n + 1)
                for h in range(H):
                    if h % 4 == 0 and (n or h):
                        pe.wait_ge(q["pcp"], 2 * n + h // 4)
                    for j in (range(2) if n else (1,)):
                        last = nc.tensor.transpose(pb[:, 4 + (h % 4) // 2, 256 * (h % 2) + 128 * j:256 * (h % 2) + 128 * j + 128],
                                                   p[:, h, P * j:P * j + P], ident[:, :])
                    if h % 4 == 3:
                        last.then_inc(q["ptr"], 1)
                pe.wait_ge(q["pcp"], 2 * n + 2)
                if n:
                    pe.wait_ge(q["y"], n)
                for mm in range(QPK):
                    for v in range(KVH):
                        js = (0, 1) if n else (1,)
                        for j in js:
                            last = nc.tensor.matmul(pb[64 * v:64 * v + 64, 6, P * mm:P * mm + P],
                                                    vt[:, n - 1 + j, 64 * v:64 * v + 64], pT[:, 2 * mm + v, j, :],
                                                    start=(j == js[0]), stop=(j == 1))
                last.then_inc(q["o"], 1)

        @block.scalar
        def _(act):
            act.wait_ge(q["v_tr"], 1)
            nc.scalar.copy(kv_out[:, 0, :], pb[:, 2, P:2 * P]).then_inc(q["k0"], 1)
            nc.scalar.copy(smp[:, 0, :], pb[0:NS, 2, 2 * P:3 * P]).then_inc(q["k0"], 1)
            nc.scalar.copy(smp[:, 1, :], pb[0:NS, 2, 0:P]).then_inc(q["k0"], 1)
            act.wait_ge(q["v_cp"], 1)
            nc.scalar.copy(kv_out[:, 1, :], vt[:, NT - 1, :]).then_inc(q["k0"], 1)
            for h in range(H):
                act.wait_ge(q["bias_ps"], h + 1)
                nc.scalar.copy(bv[:, h, :], pb[:, 6 + h % 2, 0:VW]).then_inc(q["bias_cp"], 1)
            for n in range(NT):
                lo = 0 if n else P
                act.wait_ge(q["neg"], n + 1)
                if n:
                    act.wait_ge(q["ptr"], 2 * n)
                    act.wait_ge(q["prob"], n)
                for h in range(H):
                    nc.scalar.activation(p[:, h, lo:2 * WIN], s[:, h, lo:2 * WIN], ACT.Exp,
                                         bias=st[:, 1, h:h + 1], accum_out=st[:, 2, h:h + 1])
                nc.scalar.activation(st[:, 4, :], st[:, 3, :], ACT.Exp).then_inc(q["ex"], 1)
                for g in range(2):
                    act.wait_ge(q["ptr"], 2 * n + g + 1)
                    if n and g == 0:
                        act.wait_ge(q["o"], n)
                    for b in range(2):
                        h0 = 4 * g + 2 * b
                        src = pb[:, 4 + b, :].rearrange("p (h j t) -> p h j t", h=2, j=2)
                        j0 = 0 if n else 1
                        last = nc.scalar.copy(pT[:, h0:h0 + 2, j0:2, :], src[:, :, j0:2, :])
                    last.then_inc(q["pcp"], 1)
                act.wait_ge(q["o"], n + 1)
                nc.scalar.copy(yb[:, :, P * n:P * n + P],
                               pb[:, 6, :].rearrange("p (m t) -> p m t", m=QPK)).then_inc(q["y"], 1)

        @block.vector
        def _(dve):
            link = Linked(dve, q["chain"])
            dve.wait_ge(q["in"], 96)
            nc.vector.tensor_copy(rbb[:, :, :], rb[:, :].unsqueeze(2).to_broadcast([NB1, H, P])).then_inc(q["rbw"], 1)
            dve.wait_ge(q["v_tr"], 1)
            nc.vector.tensor_copy(vt[:, 0:NT, :], pb[:, 0:2, :].rearrange("p b (n d) -> p (b n) d", n=4))\
                .then_inc(q["v_cp"], 1)
            dve.wait_ge(q["bias_rd"], 16 * H)
            for n in range(NT):
                lo = 0 if n else P
                if n:
                    dve.wait_ge(q["ex"], n)
                for b in range(4):
                    v, half = b % 2, b // 2
                    dve.wait_ge(q["sc"], 4 * n + 2 * half + 2)
                    src = pb[:, 2 * v + half, :].rearrange("p (m k) -> p m k", m=2)
                    h0 = 4 * half + v
                    nc.vector.scalar_tensor_tensor(
                        out=s[:, h0:h0 + 3:2, lo:], in0=src[:, :, lo:], scalar=SC,
                        in1=bias[:, h0:h0 + 3:2, lo:], op0=ALU.mult, op1=ALU.add).then_inc(q["masked"], 1)
                dve.wait_ge(q["masked"], 4 * n + 4)
                link(nc.vector.tensor_reduce(st[:, 0, :], s[:, :, lo:], AX, ALU.max))
                link(nc.vector.tensor_tensor(st[:, 0, :], st[:, 0, :], sinks[:, :], ALU.max))
                nc.vector.tensor_tensor(st[:, 3, :], sinks[:, :], st[:, 0, :], ALU.subtract)
                nc.vector.tensor_scalar(st[:, 1, :], st[:, 0, :], -1.0, None, ALU.mult).then_inc(q["neg"], 1)
                dve.wait_ge(q["ex"], n + 1)
                link(nc.vector.tensor_tensor(st[:, 5, :], st[:, 2, :], st[:, 4, :], ALU.add))
                link(nc.vector.reciprocal(st[:, 5, :], st[:, 5, :]))
                nc.vector.tensor_tensor(p[:, :, lo:], p[:, :, lo:],
                                        st[:, 5, :].unsqueeze(2).to_broadcast([P, H, 2 * WIN - lo]), ALU.mult)\
                    .then_inc(q["prob"], 1)


def attend_samples(nc, io, pq, yb, const):
    SC = HD ** -0.5
    H = KVH * QPK
    R = NS * H
    with Memory(nc, "as") as m:
        kc = m.sb("k_cache", [P, NS, P])
        vc = m.sb("v_cache", [P, NS, P])
        kcT = m.sb("k_cacheT", [P, NS, P])
        qs = m.sb("q_cols", [P, NS, QPK])
        sT = m.sb("scoresT", [P, 2, R])
        s = m.sb("scores", [R, P + NS])
        p = m.sb("probs", [R, P + NS])
        pT = m.sb("probsT", [P, 2, R])
        vs = m.sb("v_own", [NS, P])
        extra = m.sb("bias", [R, P + NS])
        sink = m.sb("sink", [R, 1])
        sinks = m.sb("sinks", [R, H])
        pick = m.sb("pick", [R, H])
        st = m.sb("stats", [R, 8])
        pb = m.psum("pb", [P, 8, 512])
        names = "in kt ktc qc sc scc tr mx ex pr tr2 tr2c o y chain".split()
        q = {k: m.sem(k) for k in names}
        block = m.block()

        @block.sync
        def _(sp):
            for dst, name in ((kc, "k"), (vc, "v")):
                sp.dma_start(dst[:, :, :], io[f"cache_swa_{name}"][0].rearrange("b t h d -> t b (h d)"))\
                    .then_inc(q["in"], 16)
            sp.dma_start(extra[:, P:P + NS], io["c_own"]).then_inc(q["in"], 16)
            sp.dma_start(pick[:, :], io["c_rowhead"]).then_inc(q["in"], 16)
            for v in range(KVH):
                sp.dma_start(sinks[:, v::KVH], io["attn_sinks"][:, QPK * v:QPK * v + QPK].to_broadcast([R, QPK]),
                             allow_slow_non_contiguous=True)\
                    .then_inc(q["in"], 16)
            for b in range(NS):
                sp.dma_start(extra[H * b:H * b + H, 0:P], io["bias_scratch"][:, WIN - 1:2 * WIN - 1]).then_inc(q["in"], 16)
                sp.dma_start(st[H * b:H * b + H, 7:8], io["bias_scratch"][:, 2 * WIN - 1:2 * WIN],
                             allow_slow_non_contiguous=True).then_inc(q["in"], 16)

        @block.tensor
        def _(pe):
            ident = const["ident"]
            pe.wait_ge(q["in"], 16 * (6 + 2 * NS))
            for b in range(NS):
                last = nc.tensor.transpose(pb[:, b // 4, P * (b % 4):P * (b % 4) + P], kc[:, b, :], ident[:, :])
            nc.tensor.transpose(pb[0:NS, 4, 0:P], pq[:, 5, S0C:S0C + NS], ident[:, :]).then_inc(q["kt"], 1)
            pe.wait_ge(q["ktc"], 1)
            pe.wait_ge(q["qc"], 1)
            for v in range(KVH):
                for b in range(NS):
                    nc.tensor.matmul(pb[:, 2 + v, QPK * b:QPK * b + QPK], kcT[64 * v:64 * v + 64, b, :],
                                     qs[64 * v:64 * v + 64, b, :], start=True, stop=True)
                last = nc.tensor.matmul(pb[0:NS, 2 + v, 128:128 + NS * QPK],
                                        pq[64 * v:64 * v + 64, 4, S0C:S0C + NS],
                                        qs[64 * v:64 * v + 64, :, :].rearrange("p b g -> p (b g)"), start=True, stop=True)
            last.then_inc(q["sc"], 1)
            pe.wait_ge(q["scc"], 1)
            nc.tensor.transpose(pb[0:R, 5, 0:P], sT[:, 0, :], ident[:, :])
            nc.tensor.transpose(pb[0:R, 5, P:P + NS], sT[0:NS, 1, :], ident[0:NS, 0:NS]).then_inc(q["tr"], 1)
            pe.wait_ge(q["pr"], 1)
            nc.tensor.transpose(pb[:, 6, 0:R], p[:, 0:P], ident[0:R, 0:R])
            nc.tensor.transpose(pb[0:NS, 6, R:2 * R], p[:, P:P + NS], ident[0:R, 0:R]).then_inc(q["tr2"], 1)
            pe.wait_ge(q["tr2c"], 1)
            for v in range(KVH):
                for b in range(NS):
                    c = H * b + v
                    o = pb[64 * v:64 * v + 64, 7, QPK * b:QPK * b + QPK]
                    nc.tensor.matmul(o, vc[:, b, 64 * v:64 * v + 64], pT[:, 0, c:c + 7:2], start=True, stop=False)
                    last = nc.tensor.matmul(o, vs[:, 64 * v:64 * v + 64], pT[0:NS, 1, c:c + 7:2], start=False, stop=True)
            last.then_inc(q["o"], 1)

        @block.scalar
        def _(act):
            act.wait_ge(q["kt"], 1)
            nc.scalar.copy(kcT[:, :, :], pb[:, 0:2, :].rearrange("p c (b k) -> p (c b) k", b=4))
            nc.scalar.copy(vs[:, :], pb[0:NS, 4, 0:P]).then_inc(q["ktc"], 1)
            act.wait_ge(q["mx"], 1)
            nc.scalar.activation(p[:, :], s[:, :], ACT.Exp, bias=st[:, 2:3], accum_out=st[:, 3:4])
            nc.scalar.activation(st[:, 4:5], sink[:, :], ACT.Exp, bias=st[:, 2:3]).then_inc(q["ex"], 1)
            act.wait_ge(q["o"], 1)
            nc.scalar.copy(yb[:, :, T:TT].rearrange("p m b -> p b m"),
                           pb[:, 7, 0:QPK * NS].rearrange("p (b m) -> p b m", b=NS)).then_inc(q["y"], 1)

        @block.vector
        def _(dve):
            link = Linked(dve, q["chain"])
            nc.vector.tensor_copy(qs[:, :, :], pq[:, 0:QPK, S0C:S0C + NS].rearrange("p m b -> p b m")).then_inc(q["qc"], 1)
            dve.wait_ge(q["sc"], 1)
            for v in range(KVH):
                cols = pb[:, 2 + v, 0:NS * QPK].rearrange("p (b g) -> p b g", b=NS)
                own = pb[0:NS, 2 + v, 128:128 + NS * QPK].rearrange("p (b g) -> p b g", b=NS)
                nc.vector.tensor_copy(sT[:, 0, :].rearrange("p (b g v) -> p b g v", b=NS, v=KVH)[:, :, :, v], cols)
                last = nc.vector.tensor_copy(
                    sT[0:NS, 1, :].rearrange("p (b g v) -> p b g v", b=NS, v=KVH)[:, :, :, v], own)
            last.then_inc(q["scc"], 1)
            dve.wait_ge(q["in"], 16 * (6 + 2 * NS))
            link(nc.vector.tensor_tensor(sinks[:, :], sinks[:, :], pick[:, :], ALU.mult))
            link(nc.vector.tensor_reduce(sink[:, :], sinks[:, :], AX, ALU.add))
            link(nc.vector.tensor_scalar(extra[:, P:P + NS], extra[:, P:P + NS], st[:, 7:8], None, ALU.add))
            dve.wait_ge(q["tr"], 1)
            link(nc.vector.scalar_tensor_tensor(out=s[:, :], in0=pb[0:R, 5, 0:P + NS], scalar=SC, in1=extra[:, :],
                                                op0=ALU.mult, op1=ALU.add))
            link(nc.vector.tensor_reduce(st[:, 0:1], s[:, :], AX, ALU.max))
            link(nc.vector.tensor_tensor(st[:, 1:2], st[:, 0:1], sink[:, :], ALU.max))
            nc.vector.tensor_scalar(st[:, 2:3], st[:, 1:2], -1.0, None, ALU.mult).then_inc(q["mx"], 1)
            dve.wait_ge(q["ex"], 1)
            link(nc.vector.tensor_tensor(st[:, 5:6], st[:, 3:4], st[:, 4:5], ALU.add))
            link(nc.vector.reciprocal(st[:, 6:7], st[:, 5:6]))
            nc.vector.tensor_scalar(p[:, :], p[:, :], st[:, 6:7], None, ALU.mult).then_inc(q["pr"], 1)
            dve.wait_ge(q["tr2"], 1)
            nc.vector.tensor_copy(pT[:, 0, :], pb[:, 6, 0:R])
            nc.vector.tensor_copy(pT[0:NS, 1, :], pb[0:NS, 6, R:2 * R]).then_inc(q["tr2c"], 1)


def shift_mix(nc, io, pr, mx, cumx, vec, const):
    with Memory(nc, "sm") as m:
        w2 = m.sb("decay_w2", [WL, DA])
        a2 = m.sb("iclr_a2", [WL + AL, DA])
        d = m.sb("diff", [P, 2, TT])
        wt = m.sb("tanh_w", [WL, TT])
        sq = m.sb("squares", [P, 2, TT])
        rk = m.sb("raw_kk", [P, 2, TT])
        reset = m.sb("chunk_reset", [P, TT])
        pb = m.psum("pb", [P, 8, 512])
        names = "in dd mixed lor z zs a as sq n2 nr chain chain2 dfree zr kkr tn pl msk".split()
        q = {k: m.sem(k) for k in names}
        cols = [(0, 344), (344, 344), (688, 344)]
        block = m.block()
        order = [12, 13] + list(range(4, 8)) + list(range(0, 4)) + list(range(8, 12))

        def height(c):
            return {12: WL + AL, 13: GL}.get(c, P)

        def target(c):
            return pr[0:height(c), c, 0:TT] if c >= 12 else mx[:, c, :]

        @block.sync
        def _(sp):
            sp.dma_start(w2[:, :], io["decay_w2"][0]).then_inc(q["in"], 16)
            sp.dma_start(a2[WL:WL + AL, :], io["iclr_a2"][0]).then_inc(q["in"], 16)

        @block.gpsimd
        def _(pool):
            nc.gpsimd.memset(a2[0:WL, :], 0.0)
            nc.gpsimd.memset(reset[:, :], 1.0).then_inc(q["pl"], 1)
            pool.wait_ge(q["pl"], 1)
            nc.gpsimd.memset(reset[:, 0:T:CH], 0.0)
            nc.gpsimd.memset(reset[:, T:TT], 0.0).then_inc(q["pl"], 1)
            for i, c in enumerate(order):
                hgt = height(c)
                if i >= 2:
                    pool.wait_ge(q["mixed"], i - 1)
                o = d[0:hgt, i % 2, :]
                nc.gpsimd.tensor_tensor(o[:, 0:T], pr[0:hgt, c, 0:T], pr[0:hgt, c, 1:1 + T], ALU.subtract)
                nc.gpsimd.tensor_tensor(o[:, T:TT], pr[0:hgt, c, V0C:V0C + NS], pr[0:hgt, c, S0C:S0C + NS],
                                        ALU.subtract).then_inc(q["dd"], 1)

        @block.tensor
        def _(pe):
            pe.wait_ge(q["in"], 32)
            pe.wait_ge(q["pl"], 2)
            pe.wait_ge(q["lor"], 1)
            at = 0
            for t in range(4):
                for kind in range(2):
                    if at >= 2:
                        pe.wait_ge(q["zs"] if kind == 0 else q["as"], t)
                    for j, (t0, tn) in enumerate(cols):
                        bank = 3 * kind + j
                        if kind == 0:
                            last = nc.tensor.matmul(pb[:, bank, 0:tn], w2[:, P * t:P * t + P], wt[:, t0:t0 + tn],
                                                    start=True, stop=True)
                        else:
                            last = nc.tensor.matmul(pb[:, bank, 0:tn], a2[:, P * t:P * t + P],
                                                    pr[0:WL + AL, 12, t0:t0 + tn], start=True, stop=True)
                    last.then_inc(q["z"] if kind == 0 else q["a"], 1)
                    at += 1
            for t in range(4):
                pe.wait_ge(q["sq"], t + 1)
                if t >= 1:
                    pe.wait_ge(q["n2"], t)
                else:
                    pe.wait_ge(q["zs"], 4)
                for j, (t0, tn) in enumerate(cols):
                    last = nc.tensor.matmul(pb[:, j, 0:tn], const["head_ones"][:, :], sq[:, t % 2, t0:t0 + tn],
                                            start=True, stop=True)
                last.then_inc(q["nr"], 1)

        @block.scalar
        def _(act):
            act.wait_ge(q["mixed"], 1)
            nc.scalar.activation(wt[:, :], pr[0:WL, 12, 0:TT], ACT.Tanh).then_inc(q["lor"], 1)
            act.wait_ge(q["mixed"], 2)
            nc.scalar.activation(pr[0:GL, 13, 0:TT], pr[0:GL, 13, 0:TT], ACT.Sigmoid)
            act.wait_ge(q["mixed"], 6)
            for t in range(4):
                act.wait_ge(q["z"], t + 1)
                for j, (t0, tn) in enumerate(cols):
                    last = nc.scalar.activation(cumx[:, t, t0:t0 + tn], pb[:, j, 0:tn], ACT.Sigmoid,
                                                bias=vec["decay_w0"][:, t:t + 1])
                last.then_inc(q["zs"], 1)
                act.wait_ge(q["a"], t + 1)
                for j, (t0, tn) in enumerate(cols):
                    last = nc.scalar.activation(pr[:, 4 + t, t0:t0 + tn], pb[:, 3 + j, 0:tn], ACT.Sigmoid,
                                                bias=vec["iclr_a0"][:, t:t + 1])
                last.then_inc(q["as"], 1)
            for t in range(4):
                act.wait_ge(q["kkr"], t + 1)
                if t >= 2:
                    act.wait_ge(q["nr"], t - 1)
                nc.scalar.activation(sq[:, t % 2, :], rk[:, t % 2, :], ACT.Square).then_inc(q["sq"], 1)
                act.wait_ge(q["nr"], t + 1)
                for j, (t0, tn) in enumerate(cols):
                    last = nc.scalar.activation(sq[:, t % 2, t0:t0 + tn], pb[:, j, 0:tn], ACT.Sqrt)
                last.then_inc(q["n2"], 1)

        @block.vector
        def _(dve):
            link = Linked(dve, q["chain"])
            for i, c in enumerate(order):
                hgt = height(c)
                dve.wait_ge(q["dd"], i + 1)
                ins = nc.vector.scalar_tensor_tensor(
                    out=target(c), in0=d[0:hgt, i % 2, :], scalar=vec["mu"][0:hgt, c:c + 1],
                    in1=pr[0:hgt, c, 1:1 + TT], op0=ALU.mult, op1=ALU.add)
                ins.then_inc(q["mixed"], 1)
            dve.wait_ge(q["mixed"], len(order))
            dve.wait_ge(q["pl"], 2)
            for t in range(4):
                dve.wait_ge(q["zs"], t + 1)
                link(nc.vector.tensor_scalar(cumx[:, t, :], cumx[:, t, :], -math.exp(-0.5), None, ALU.mult))
                link(nc.vector.tensor_tensor_scan(pr[:, 8 + t, 0:TT], reset[:, :], cumx[:, t, :], 0.0, ALU.mult, ALU.add))
                nc.vector.tensor_tensor(cumx[:, t, :], pr[:, 8 + t, 0:TT], cumx[:, t, :], ALU.subtract)
            for t in range(4):
                if t >= 2:
                    dve.wait_ge(q["chain2"], t - 1)
                nc.vector.tensor_scalar(rk[:, t % 2, :], mx[:, 4 + t, :], vec["k_k"][:, t:t + 1], None, ALU.mult)\
                    .then_inc(q["kkr"], 1)
                dve.wait_ge(q["n2"], t + 1)
                link(nc.vector.tensor_scalar(sq[:, t % 2, :], sq[:, t % 2, :], 1e-12, None, ALU.max))
                link(nc.vector.reciprocal(sq[:, t % 2, :], sq[:, t % 2, :]))
                link(nc.vector.scalar_tensor_tensor(out=pr[:, t, 0:TT], in0=rk[:, t % 2, :], scalar=-1.0,
                                                    in1=sq[:, t % 2, :], op0=ALU.mult, op1=ALU.mult))
                dve.wait_ge(q["as"], t + 1)
                link(nc.vector.tensor_scalar(sq[:, t % 2, :], pr[:, 4 + t, 0:TT], -1.0, vec["k_a"][:, t:t + 1],
                                             ALU.add, ALU.mult))
                link(nc.vector.scalar_tensor_tensor(out=mx[:, 4 + t, :], in0=sq[:, t % 2, :], scalar=1.0,
                                                    in1=mx[:, 4 + t, :], op0=ALU.add, op1=ALU.mult))
                nc.vector.scalar_tensor_tensor(out=pr[:, 4 + t, 0:TT], in0=pr[:, t, 0:TT], scalar=-1.0,
                                               in1=pr[:, 4 + t, 0:TT], op0=ALU.mult, op1=ALU.mult).then_inc(q["chain2"], 1)


def rwkv_sample(nc, io, pr, mx, const):
    with Memory(nc, "rs") as m:
        HR = HD // 2
        R = 2 * NS * HA
        S = m.sb("state", [R, HR, HD])
        S2 = m.sb("work", [R, HR, HD])
        vrow = m.sb("vectors", [NS, 6, DA])
        vb = m.sb("vectors_by_head", [R, 5, HD])
        vv = m.sb("values", [R, HR])
        sa = m.sb("sa", [R, HR])
        y = m.sb("y", [R, HR])
        yr = m.sb("y_rows", [NS, DA])
        decay = m.sb("decay", [P, 4, NS])
        pb = m.psum("pb", [P, 8, 512])
        names = "st tr cp vw vr chain out y yd ydr ytr yc pre".split()
        q = {k: m.sem(k) for k in names}
        scr, yscr = io["sample_scratch"], io["sample_y"]
        block = m.block()
        def col(j, t):
            return [pr[:, t, T:TT], pr[:, 4 + t, T:TT], mx[:, 4 + t, T:TT], mx[:, t, T:TT], decay[:, t, :],
                    mx[:, 8 + t, T:TT]][j]

        @block.sync
        def _(sp):
            for half in range(2):
                sp.dma_start(S[64 * half:64 * half + 64, :, :],
                             io["state_rwkv"][0, :, :, HR * half:HR * half + HR, :].rearrange("b h i j -> (b h) i j"))\
                    .then_inc(q["st"], 16)
            sp.wait_ge(q["cp"], 6)
            sp.dma_start(scr.rearrange("v b c -> b v c"), vrow[:, :, :]).then_inc(q["vw"], 16)
            sp.wait_ge(q["vw"], 16)
            for half in range(2):
                sp.dma_start(vb[64 * half:64 * half + 64, :, :],
                             scr[0:5].rearrange("v b (h j) -> (b h) v j", h=HA)).then_inc(q["vr"], 16)
                sp.dma_start(vv[64 * half:64 * half + 64, :],
                             scr[5].rearrange("b (h i) -> (b h) i", h=HA)[:, HR * half:HR * half + HR]).then_inc(q["vr"], 16)
            sp.wait_ge(q["y"], 1)
            for half in range(2):
                sp.dma_start(yscr.rearrange("b (h i) -> (b h) i", h=HA)[:, HR * half:HR * half + HR],
                             y[64 * half:64 * half + 64, :]).then_inc(q["yd"], 16)
                sp.dma_start(io["o_rwkv_sample"][0, :, :, HR * half:HR * half + HR, :].rearrange("b h i j -> (b h) i j"),
                             S[64 * half:64 * half + 64, :, :]).then_inc(q["out"], 16)
            sp.wait_ge(q["yd"], 32)
            sp.dma_start(yr[:, :], yscr).then_inc(q["ydr"], 16)
            sp.wait_ge(q["out"], 32)

        @block.tensor
        def _(pe):
            pe.wait_ge(q["pre"], 1)
            for j in range(6):
                for t in range(4):
                    last = nc.tensor.transpose(pb[0:NS, j, P * t:P * t + P], col(j, t), const["ident"][:, :])
                last.then_inc(q["tr"], 1)
            pe.wait_ge(q["ydr"], 16)
            for t in range(4):
                last = nc.tensor.transpose(pb[:, 6, NS * t:NS * t + NS], yr[:, P * t:P * t + P], const["ident"][0:NS, 0:NS])
            last.then_inc(q["ytr"], 1)

        @block.scalar
        def _(act):
            nc.scalar.activation(decay[:, :, :], pr[:, 8:12, T:TT], ACT.Exp).then_inc(q["pre"], 1)
            for j in range(6):
                act.wait_ge(q["tr"], j + 1)
                nc.scalar.copy(vrow[:, j, :], pb[0:NS, j, :]).then_inc(q["cp"], 1)
            act.wait_ge(q["ytr"], 1)
            nc.scalar.copy(pr[:, 0:4, T:TT], pb[:, 6, 0:4 * NS].rearrange("p (t b) -> p t b", t=4)).then_inc(q["yc"], 1)

        @block.vector
        def _(dve):
            link = Linked(dve, q["chain"])
            dve.wait_ge(q["st"], 32)
            dve.wait_ge(q["vr"], 64)

            def over_i(j):
                return vb[:, j, :].unsqueeze(1).to_broadcast([R, HR, HD])

            def over_j(a):
                return a.unsqueeze(2).to_broadcast([R, HR, HD])

            link(nc.vector.tensor_tensor(S2[:, :, :], S[:, :, :], over_i(0), ALU.mult))
            link(nc.vector.tensor_reduce(sa[:, :], S2[:, :, :], AX, ALU.add))
            link(nc.vector.tensor_tensor(S[:, :, :], S[:, :, :], over_i(4), ALU.mult))
            link(nc.vector.tensor_tensor(S2[:, :, :], over_j(sa[:, :]), over_i(1), ALU.mult))
            link(nc.vector.tensor_tensor(S[:, :, :], S[:, :, :], S2[:, :, :], ALU.add))
            link(nc.vector.tensor_tensor(S2[:, :, :], over_j(vv[:, :]), over_i(2), ALU.mult))
            link(nc.vector.tensor_tensor(S[:, :, :], S[:, :, :], S2[:, :, :], ALU.add))
            link(nc.vector.tensor_tensor(S2[:, :, :], S[:, :, :], over_i(3), ALU.mult))
            nc.vector.tensor_reduce(y[:, :], S2[:, :, :], AX, ALU.add).then_inc(q["y"], 1)


def rwkv_chunks(nc, io, pr, mx, cumx, const):
    with Memory(nc, "rc") as m:
        ex = m.sb("exps", [P, 3, 4, P])
        ft = m.sb("scaled", [P, 6, 4, P])
        tok = m.sb("token_rows", [P, 4, DA])
        Lm = m.sb("L", [P, 2, 4, P])
        X = m.sb("X", [P, 2, 4, P])
        XT = m.sb("XT", [P, 2, 4, P])
        Z = m.sb("Z", [P, 2, 4, P])
        RB = m.sb("RBT", [P, 2, 4, P])
        RK = m.sb("RKT", [P, 2, 4, P])
        MV = m.sb("MV", [P, DA])
        U = m.sb("U", [P, DA])
        Uv = m.sb("Uv", [P, DA])
        WT = m.sb("WT", [P, 4, P])
        ST = m.sb("ST", [P, 2, 4, HD])
        SD = m.sb("ST_decayed", [P, 4, HD])
        So = m.sb("state_out", [HD, HA, HD])
        pb = m.psum("pb", [P, 8, 512])
        names = ("ex ft hat tr tc prod ev z zc x xe xt xc mt wt wtc uv uvc mv mvc sd u uc s sc y yc st chain stz so soc out"
                 " ys fin").split()
        q = {k: m.sem(k) for k in names}
        block = m.block()
        NLEV = 5
        ident = const["ident"]

        def hcol(par, t):
            return HD * (2 * t + par)

        def fr(par):
            return slice(64 * par, 64 * par + 64)

        @block.scalar
        def _(act):
            for n in range(NT):
                c = slice(P * n, P * n + P)
                if n:
                    act.wait_ge(q["hat"], 2 * n)
                    act.wait_ge(q["fin"], n)
                nc.scalar.activation(ex[:, 0, :, :], cumx[:, :, c], ACT.Exp)
                nc.scalar.activation(ex[:, 1, :, :], pr[:, 8:12, c], ACT.Exp)
                nc.scalar.activation(ex[:, 2, :, :], pr[:, 8:12, c], ACT.Exp, scale=-1.0).then_inc(q["ex"], 1)
                for j in range(4):
                    act.wait_ge(q["tr"], 4 * n + j + 1)
                    if n and j == 0:
                        act.wait_ge(q["s"], 2 * n)
                        act.wait_ge(q["y"], n)
                    nc.scalar.copy(tok[:, j, :], pb[:, j % 2, :]).then_inc(q["tc"], 1)
                for lev in range(NLEV - 1):
                    for par in range(2):
                        act.wait_ge(q["xt"], 2 * ((NLEV - 1) * n + lev) + par + 1)
                        nc.scalar.copy(X[:, par, :, :], pb[:, 6 + par, :]
                                       .rearrange("p (t s) -> p t s", t=4)).then_inc(q["xc"], 1)
                act.wait_ge(q["mt"], n + 1)
                nc.scalar.copy(MV[:, :], pb[:, 0, :]).then_inc(q["mvc"], 1)
                act.wait_ge(q["wt"], n + 1)
                if n:
                    act.wait_ge(q["u"], 2 * n)
                nc.scalar.copy(WT[:, :, :], pb[:, 1, :].rearrange("p (t s) -> p t s", t=4)).then_inc(q["wtc"], 1)
                act.wait_ge(q["uv"], n + 1)
                if n:
                    act.wait_ge(q["uc"], 2 * n)
                nc.scalar.copy(Uv[:, :], pb[:, 2, :]).then_inc(q["uvc"], 1)
                act.wait_ge(q["st"], 2 * n + 2)
                for par in range(2):
                    last = nc.scalar.copy(pr[fr(par), 0:4, c], pb[fr(par), 6 * par, :].rearrange("p (t s) -> p t s", t=4))
                last.then_inc(q["ys"], 1)
            act.wait_ge(q["so"], 1)
            nc.scalar.copy(So[:, :, :], pb[0:HD, 0, :].rearrange("p (h j) -> p h j", h=HA)).then_inc(q["soc"], 1)

        @block.gpsimd
        def _(pool):
            nc.gpsimd.memset(ST[:, 0, :, :], 0.0).then_inc(q["stz"], 1)
            for n in range(NT):
                c = slice(P * n, P * n + P)
                pool.wait_ge(q["ex"], n + 1)
                if n:
                    pool.wait_ge(q["y"], n)
                nc.gpsimd.tensor_tensor(ft[:, 0, :, :], pr[:, 0:4, c], ex[:, 0, :, :], ALU.mult)
                nc.gpsimd.tensor_tensor(ft[:, 2, :, :], pr[:, 4:8, c], ex[:, 2, :, :], ALU.mult).then_inc(q["ft"], 1)
                nc.gpsimd.tensor_tensor(ft[:, 3, :, :], mx[:, 4:8, c], ex[:, 2, :, :], ALU.mult)
                nc.gpsimd.tensor_tensor(ft[:, 1, :, :], mx[:, 0:4, c], ex[:, 1, :, :], ALU.mult).then_inc(q["ft"], 1)
                pool.wait_ge(q["ft"], 2 * n + 2)
                for j in (2, 3):
                    for ch in range(2):
                        src = ft[:, j, :, CH * ch:CH * ch + CH]
                        end = ex[:, 1, :, CH * ch + CH - 1:CH * ch + CH].to_broadcast([P, 4, CH])
                        last = nc.gpsimd.tensor_tensor(ft[:, j + 2, :, CH * ch:CH * ch + CH], src, end, ALU.mult)
                last.then_inc(q["fin"], 1)

        @block.tensor
        def _(pe):
            mm = nc.tensor.matmul
            for n in range(NT):
                c = slice(P * n, P * n + P)
                if n:
                    pe.wait_ge(q["yc"], n)
                    pe.wait_ge(q["sc"], 2 * n)
                for k, (lo, ro) in enumerate(((0, 2), (2, 0), (3, 0), (2, 1), (3, 1))):
                    pe.wait_ge(q["ft"], 2 * n + (1 if k < 2 else 2))
                    if k >= 4:
                        pe.wait_ge(q["ev"], 10 * n + 2 * (k - 4) + 2)
                    for t in range(4):
                        for par in range(2):
                            last = mm(pb[:, 2 * (k % 4) + par, P * t:P * t + P], ft[fr(par), lo, t, :],
                                      ft[fr(par), ro, t, :], start=True, stop=True)
                    last.then_inc(q["prod"], 1)
                pe.wait_ge(q["fin"], n + 1)
                for j, src in enumerate((ft[:, 0], ft[:, 4], ft[:, 5], mx[:, 8:12, c])):
                    if j == 0:
                        pe.wait_ge(q["ev"], 10 * n + 10)
                    if j >= 2:
                        pe.wait_ge(q["tc"], 4 * n + j - 1)
                    for t in range(4):
                        last = nc.tensor.transpose(pb[:, j % 2, P * t:P * t + P], src[:, t, :], ident[:, :])
                    last.then_inc(q["tr"], 1)
                pe.wait_ge(q["tc"], 4 * n + 4)
                for h in range(HA):
                    last = mm(pb[:, 0, HD * h:HD * h + HD], Z[:, h % 2, h // 2, :], tok[:, 3, HD * h:HD * h + HD],
                              start=True, stop=True)
                last.then_inc(q["mt"], 1)
                for lev in range(NLEV):
                    g = NLEV * n + lev
                    for par in range(2):
                        if lev:
                            pe.wait_ge(q["xe"], 2 * (g - 1) + par + 1)
                        for t in range(4):
                            last = mm(pb[:, 2 + par, P * t:P * t + P], Lm[:, par, t, :], XT[:, par, t, :],
                                      start=True, stop=True)
                        last.then_inc(q["z"], 1)
                    for par in range(2):
                        pe.wait_ge(q["zc"], 2 * g + par + 1)
                        if lev:
                            pe.wait_ge(q["xc"], 2 * ((NLEV - 1) * n + lev - 1) + par + 1)
                        for t in range(4):
                            last = mm(pb[:, 4 + par, P * t:P * t + P], X[:, par, t, :], Z[:, par, t, :],
                                      start=True, stop=True)
                        last.then_inc(q["x"], 1)
                    if lev < NLEV - 1:
                        for par in range(2):
                            pe.wait_ge(q["xe"], 2 * g + par + 1)
                            for t in range(4):
                                last = nc.tensor.transpose(pb[:, 6 + par, P * t:P * t + P], XT[:, par, t, :], ident[:, :])
                            last.then_inc(q["xt"], 1)
                pe.wait_ge(q["xe"], 2 * NLEV * (n + 1))
                for t in range(4):
                    for par in range(2):
                        last = mm(pb[fr(par), 1, P * t:P * t + P], tok[:, 0, hcol(par, t):hcol(par, t) + HD],
                                  XT[:, par, t, :], start=True, stop=True)
                last.then_inc(q["wt"], 1)
                pe.wait_ge(q["mvc"], n + 1)
                for h in range(HA):
                    last = mm(pb[:, 2, HD * h:HD * h + HD], XT[:, h % 2, h // 2, :], MV[:, HD * h:HD * h + HD],
                              start=True, stop=True)
                last.then_inc(q["uv"], 1)
                pe.wait_ge(q["wtc"], n + 1)
                for ch in range(2):
                    g = 2 * n + ch
                    cur = g % 2
                    tr = slice(CH * ch, CH * ch + CH)
                    if g:
                        pe.wait_ge(q["sc"], g)
                    else:
                        pe.wait_ge(q["stz"], 1)
                    for t in range(4):
                        for par in range(2):
                            last = mm(pb[tr, 3 + 2 * par, HD * t:HD * t + HD], WT[fr(par), t, tr], ST[fr(par), cur, t, :],
                                      start=True, stop=True)
                    last.then_inc(q["u"], 1)
                    if ch == 0:
                        pe.wait_ge(q["mvc"], n + 1)
                    for t in range(4):
                        for par in range(2):
                            last = mm(pb[fr(par), 6 * par, P * t + CH * ch:P * t + CH * ch + CH], ST[fr(par), cur, t, :],
                                      ft[fr(par), 1, t, tr], start=True, stop=True)
                    last.then_inc(q["st"], 1)
                    pe.wait_ge(q["uc"], g + 1)
                    bank = (4, 1)[ch]
                    for t in range(4):
                        for par in range(2):
                            hc = hcol(par, t)
                            o = pb[fr(par), bank, HD * t:HD * t + HD]
                            mm(o, tok[tr, 2, hc:hc + HD], tok[tr, 3, hc:hc + HD], start=True, stop=False)
                            last = mm(o, tok[tr, 1, hc:hc + HD], U[tr, hc:hc + HD], start=False, stop=True)
                    last.then_inc(q["s"], 1)
                for t in range(4):
                    for par in range(2):
                        hc = hcol(par, t)
                        o = pb[fr(par), 7, P * t:P * t + P]
                        mm(o, U[:, hc:hc + HD], RB[:, par, t, :], start=True, stop=False)
                        last = mm(o, tok[:, 3, hc:hc + HD], RK[:, par, t, :], start=False, stop=True)
                last.then_inc(q["y"], 1)
            pe.wait_ge(q["yc"], NT)
            pe.wait_ge(q["sc"], 2 * NT)
            for t in range(4):
                last = nc.tensor.transpose(pb[0:HD, 0, P * t:P * t + P], ST[:, 0, t, :], ident[:, :])
            last.then_inc(q["so"], 1)

        @block.vector
        def _(dve):
            link = Linked(dve, q["chain"])
            tt = nc.vector.tensor_tensor

            def bank(k):
                return pb[:, k, :].rearrange("p (t s) -> p t s", t=4)

            def wide(mask):
                return const[mask][:, :].unsqueeze(1).to_broadcast([P, 4, P])
            for n in range(NT):
                dst = (Lm, None, Z, RB, RK)
                masks = ("low", "up", "up", "up_incl", "up_incl")
                for k in range(5):
                    dve.wait_ge(q["prod"], 5 * n + k + 1)
                    for par in range(2):
                        src = bank(2 * (k % 4) + par)
                        if k == 1:
                            link(tt(XT[:, par, :, :], src, wide("lev0T"), ALU.mult))
                            last = tt(XT[:, par, :, :], XT[:, par, :, :], wide("ident"), ALU.add)
                        else:
                            last = tt(dst[k][:, par, :, :], src, wide(masks[k]), ALU.mult)
                        last.then_inc(q["ev"], 1)
                        if k == 0:
                            dve.wait_ge(q["ev"], 10 * n + par + 1)
                            link(tt(X[:, par, :, :], Lm[:, par, :, :], wide("lev0"), ALU.mult))
                            link(tt(X[:, par, :, :], X[:, par, :, :], wide("ident"), ALU.add))
                dve.wait_ge(q["mt"], n + 1)
                for lev in range(NLEV):
                    g = NLEV * n + lev
                    for par in range(2):
                        dve.wait_ge(q["z"], 2 * g + par + 1)
                        tt(Z[:, par, :, :], bank(2 + par), wide(f"lev{lev + 1}T"), ALU.mult).then_inc(q["zc"], 1)
                    for par in range(2):
                        dve.wait_ge(q["x"], 2 * g + par + 1)
                        tt(XT[:, par, :, :], XT[:, par, :, :], bank(4 + par), ALU.add).then_inc(q["xe"], 1)
                for ch in range(2):
                    g = 2 * n + ch
                    cur = g % 2
                    rr = slice(CH * ch, CH * ch + CH)
                    end = ex[:, 1, :, CH * ch + CH - 1:CH * ch + CH].to_broadcast([P, 4, HD])
                    if g == 0:
                        dve.wait_ge(q["stz"], 1)
                    else:
                        dve.wait_ge(q["sc"], g)
                    tt(SD[:, :, :], ST[:, cur, :, :], end, ALU.mult).then_inc(q["hat"], 1)
                    dve.wait_ge(q["u"], g + 1)
                    if ch == 0:
                        dve.wait_ge(q["uvc"], n + 1)
                    for par in range(2):
                        uu = U[rr, :].rearrange("p (t a d) -> p t a d", a=2, d=HD)[:, :, par, :]
                        vv = Uv[rr, :].rearrange("p (t a d) -> p t a d", a=2, d=HD)[:, :, par, :]
                        last = tt(uu, pb[rr, 3 + 2 * par, 0:256].rearrange("p (t d) -> p t d", t=4), vv, ALU.add)
                    last.then_inc(q["uc"], 1)
                    dve.wait_ge(q["s"], g + 1)
                    dve.wait_ge(q["hat"], g + 1)
                    dve.wait_ge(q["st"], g + 1)
                    tt(ST[:, 1 - cur, :, :], pb[:, (4, 1)[ch], 0:256].rearrange("p (t d) -> p t d", t=4), SD[:, :, :],
                       ALU.add).then_inc(q["sc"], 1)
                c = slice(P * n, P * n + P)
                dve.wait_ge(q["ys"], n + 1)
                dve.wait_ge(q["y"], n + 1)
                tt(pr[:, 0:4, c], pr[:, 0:4, c], bank(7), ALU.add).then_inc(q["yc"], 1)

        @block.sync
        def _(sp):
            sp.wait_ge(q["soc"], 1)
            sp.dma_start(io["o_rwkv_prompt"][0, 0].rearrange("h i j -> i h j"), So[:, :, :]).then_inc(q["out"], 16)
            sp.wait_ge(q["out"], 16)


def rwkv_norm(nc, io, pr, mx, vec, const):
    with Memory(nc, "rn") as m:
        g2 = m.sb("gate_w2", [GL, DA])
        sq = m.sb("squares", [P, 2, TT])
        bb = m.sb("bonus", [P, 2, TT])
        pb = m.psum("pb", [P, 8, 512])
        cols = [(0, 344), (344, 344), (688, 344)]
        names = "in mu d sq var rs rkk bo bv gt done chain eps".split()
        q = {k: m.sem(k) for k in names}
        block = m.block()

        @block.sync
        def _(sp):
            sp.dma_start(g2[:, :], io["gate_w2"][0]).then_inc(q["in"], 16)

        @block.tensor
        def _(pe):
            def product(b0, lhs, rhs):
                for j, (t0, tn) in enumerate(cols):
                    last = nc.tensor.matmul(pb[:, b0 + j, 0:tn], lhs, rhs[:, t0:t0 + tn], start=True, stop=True)
                return last
            pe.wait_ge(q["in"], 16)
            ones = const["head_ones"][:, :]
            for t in range(4):
                if t:
                    pe.wait_ge(q["bv"], t)
                product(0, ones, pr[:, t, 0:TT]).then_inc(q["mu"], 1)
                pe.wait_ge(q["sq"], t + 1)
                if t:
                    pe.wait_ge(q["done"], t)
                product(3, ones, sq[:, t % 2, :]).then_inc(q["var"], 1)
                pe.wait_ge(q["rkk"], t + 1)
                pe.wait_ge(q["d"], t + 1)
                product(0, ones, bb[:, t % 2, :]).then_inc(q["bo"], 1)
                pe.wait_ge(q["rs"], t + 1)
                product(3, g2[:, P * t:P * t + P], pr[0:GL, 13, 0:TT]).then_inc(q["gt"], 1)

        @block.gpsimd
        def _(pool):
            nc.gpsimd.memset(const["lnx_eps"][:, :], LNX_EPS).then_inc(q["eps"], 1)
            for t in range(4):
                if t >= 2:
                    pool.wait_ge(q["done"], t - 1)
                nc.gpsimd.tensor_tensor(bb[:, t % 2, :], mx[:, t, :], mx[:, 4 + t, :], ALU.mult).then_inc(q["chain"], 1)
                pool.wait_ge(q["chain"], t + 1)
                nc.gpsimd.tensor_scalar(bb[:, t % 2, :], bb[:, t % 2, :], vec["r_k"][:, t:t + 1], None, ALU.mult)\
                    .then_inc(q["rkk"], 1)

        @block.scalar
        def _(act):
            act.wait_ge(q["eps"], 1)
            for t in range(4):
                act.wait_ge(q["d"], t + 1)
                if t >= 2:
                    act.wait_ge(q["done"], t - 1)
                nc.scalar.activation(sq[:, t % 2, :], pr[:, t, 0:TT], ACT.Square).then_inc(q["sq"], 1)
                act.wait_ge(q["var"], t + 1)
                for j, (t0, tn) in enumerate(cols):
                    last = nc.scalar.activation(sq[:, t % 2, t0:t0 + tn], pb[:, 3 + j, 0:tn], ACT.Sqrt,
                                                scale=1.0 / HD, bias=const["lnx_eps"][:, :])
                last.then_inc(q["rs"], 1)

        @block.vector
        def _(dve):
            link = Linked(dve, m.sem("chain2"))
            for t in range(4):
                y = pr[:, t, :]
                dve.wait_ge(q["mu"], t + 1)
                for j, (t0, tn) in enumerate(cols):
                    last = nc.vector.scalar_tensor_tensor(out=y[:, t0:t0 + tn], in0=pb[:, j, 0:tn], scalar=-1.0 / HD,
                                                          in1=y[:, t0:t0 + tn], op0=ALU.mult, op1=ALU.add)
                last.then_inc(q["d"], 1)
                dve.wait_ge(q["rs"], t + 1)
                link(nc.vector.reciprocal(sq[:, t % 2, :], sq[:, t % 2, :]))
                link(nc.vector.tensor_tensor(y[:, 0:TT], y[:, 0:TT], sq[:, t % 2, :], ALU.mult))
                link(nc.vector.tensor_scalar(y[:, 0:TT], y[:, 0:TT], vec["lnx_g"][:, t:t + 1], vec["lnx_b"][:, t:t + 1],
                                             ALU.mult, ALU.add))
                dve.wait_ge(q["bo"], t + 1)
                for j, (t0, tn) in enumerate(cols):
                    last = nc.vector.tensor_tensor(bb[:, t % 2, t0:t0 + tn], pb[:, j, 0:tn], mx[:, 8 + t, t0:t0 + tn],
                                                   ALU.mult)
                last.then_inc(q["bv"], 1)
                dve.wait_ge(q["bv"], t + 1)
                link(nc.vector.tensor_tensor(y[:, 0:TT], y[:, 0:TT], bb[:, t % 2, :], ALU.add))
                dve.wait_ge(q["gt"], t + 1)
                for j, (t0, tn) in enumerate(cols):
                    last = nc.vector.tensor_tensor(y[:, t0:t0 + tn], y[:, t0:t0 + tn], pb[:, 3 + j, 0:tn], ALU.mult)
                last.then_inc(q["done"], 1)


def pool_features(nc, io, xr, feats, const):
    PAD = 16
    with Memory(nc, "pf") as m:
        xT = m.sb("xT", [P, KD, PAD + TT])
        a = m.sb("sums_a", [P, 2, PAD + T])
        b = m.sb("sums_b", [P, 2, PAD + T])
        hist = m.sb("history", [NS * KEEP, D])
        hT = m.sb("historyT", [P, KD, NS * KEEP])
        hs = m.sb("history_sums", [P, 2, NS])
        inv = m.sb("inverse_counts", [P, 4, 16])
        pb = m.psum("pb", [P, 8, 512])
        q = {k: m.sem(k) for k in "in tr cpa cpv pad chain out".split()}
        block = m.block()

        @block.sync
        def _(sp):
            sp.dma_start(hist[:, :], io["state_pool"][0].rearrange("b t d -> (b t) d")).then_inc(q["in"], 16)
            sp.dma_start(inv[:, :, :], io["c_invcnt"].rearrange("p (g t) -> p g t", g=4)).then_inc(q["in"], 16)
            sp.dma_start(io["o_pool_prompt"][0, 0], xr[P - KEEP:P, NT - 1, :]).then_inc(q["out"], 16)
            sp.dma_start(io["o_pool_sample"][0, :, 0:KEEP - 1, :], io["state_pool"][0, :, 1:KEEP, :]).then_inc(q["out"], 16)
            sp.dma_start(io["o_pool_sample"][0, :, KEEP - 1, :], xr[0:NS, NT, :]).then_inc(q["out"], 16)
            sp.wait_ge(q["out"], 48)

        @block.tensor
        def _(pe):
            for i in range(TILES + 1):
                if i >= 4:
                    pe.wait_ge(q["cpa"], i - 3)
                    pe.wait_ge(q["cpv"], i - 3)
                if i == TILES:
                    pe.wait_ge(q["in"], 32)
                n = NS * KEEP if i == TILES else rows(i)
                for k in range(KD):
                    src = hist[:, P * k:P * k + P] if i == TILES else xr[0:n, i, P * k:P * k + P]
                    last = nc.tensor.transpose(pb[:, 2 * (i % 4) + k // 4, P * (k % 4):P * (k % 4) + n], src,
                                               const["ident"][0:n, 0:n])
                last.then_inc(q["tr"], 1)

        def copy_out(eng, copy, half, sem):
            for i in range(TILES + 1):
                n = NS * KEEP if i == TILES else rows(i)
                eng.wait_ge(q["tr"], i + 1)
                src = pb[:, 2 * (i % 4) + half, :].rearrange("p (k t) -> p k t", k=4)[:, :, 0:n]
                ks = slice(4 * half, 4 * half + 4)
                dst = hT[:, ks, :] if i == TILES else xT[:, ks, PAD + P * i:PAD + P * i + n]
                copy(dst, src).then_inc(q[sem], 1)

        @block.scalar
        def _(act):
            copy_out(act, nc.scalar.copy, 0, "cpa")

        @block.gpsimd
        def _(pool):
            nc.gpsimd.memset(xT[:, :, 0:PAD], 0.0).then_inc(q["pad"], 1)
            nc.gpsimd.memset(a[:, :, 0:PAD], 0.0)
            nc.gpsimd.memset(b[:, :, 0:PAD], 0.0).then_inc(q["pad"], 1)

        @block.vector
        def _(dve):
            link = Linked(dve, q["chain"])
            copy_out(dve, nc.vector.tensor_copy, 1, "cpv")
            dve.wait_ge(q["cpa"], TILES + 1)
            dve.wait_ge(q["cpv"], TILES + 1)
            dve.wait_ge(q["pad"], 2)
            dve.wait_ge(q["in"], 32)
            for g, w in enumerate(POOLW):
                ks = slice(2 * g, 2 * g + 2)
                x = xT[:, ks, 0:PAD + T]
                src, step = x, 1
                for lev in range(g + 1):
                    dst = (a, b)[lev % 2][:, :, :]
                    link(nc.vector.tensor_tensor(dst[:, :, PAD:], src[:, :, PAD:], src[:, :, PAD - step:PAD + T - step],
                                                 ALU.add))
                    src, step = dst, 2 * step
                link(nc.vector.scalar_tensor_tensor(out=feats[:, ks, 0:T], in0=src[:, :, PAD:], scalar=1.0 / w,
                                                    in1=x[:, :, PAD:], op0=ALU.mult, op1=ALU.subtract))
                link(nc.vector.tensor_tensor(feats[:, ks, 0:16], src[:, :, PAD:PAD + 16],
                                             inv[:, g:g + 1, :].to_broadcast([P, 2, 16]), ALU.mult))
                link(nc.vector.tensor_tensor(feats[:, ks, 0:16], feats[:, ks, 0:16], x[:, :, PAD:PAD + 16], ALU.subtract))
                h = hT[:, ks, :].rearrange("p k (b t) -> p k b t", b=NS)[:, :, :, KEEP - (w - 1):KEEP]
                xs = xT[:, ks, PAD + T:PAD + TT]
                link(nc.vector.tensor_reduce(hs[:, :, :], h, AX, ALU.add))
                link(nc.vector.tensor_tensor(hs[:, :, :], hs[:, :, :], xs, ALU.add))
                link(nc.vector.scalar_tensor_tensor(out=feats[:, ks, T:TT], in0=hs[:, :, :], scalar=1.0 / w,
                                                    in1=xs, op0=ALU.mult, op1=ALU.subtract))


def mix_out(nc, io, layer, lhs, xr, lg, const):
    with Memory(nc, f"mo{layer}") as m:
        w = m.sb("w", [P, KD, D if layer == 0 else 256])
        wr = m.sb("w_router", [P, KD, E])
        g = m.sb("ln_g", [P, D])
        b = m.sb("ln_b", [P, D])
        xin = m.sb("x_in", [P, 2, D])
        xT = m.sb("xT", [P, KD, P])
        st = m.sb("stats", [P, 16])
        eps = m.sb("eps", [P, 1])
        scale = m.sb("pool_scale", [P, D]) if layer else None
        pb = m.psum("pb", [P, 8, 512])
        q = {k: m.sem(k) for k in "in w mm res ln lg var root tr cp rl ev eps sc zero".split()}
        s_x = [m.sem(f"x{i}") for i in range(2)]
        block = m.block()

        @block.sync
        def _(sp):
            if layer == 0:
                wo = io["w_out"][0]
                sp.dma_start(w[:, 0:4, :], wo[0:DA, :].rearrange("(k p) n -> p k n", p=P)).then_inc(q["w"], 16)
                for v in range(KVH):
                    sp.dma_start(w[HD * v:HD * v + HD, 4:8, :],
                                 wo[DA + 256 * v:DA + 256 * v + 256, :].rearrange("(m d) n -> d m n", d=HD)).then_inc(q["w"], 16)
            else:
                for gi in range(4):
                    sp.dma_start(w[:, 2 * gi:2 * gi + 2, :], io["w_pool"][0, gi].rearrange("(c p) n -> p c n", p=P))\
                        .then_inc(q["w"], 16)
            if layer == 0:
                for i in range(TILES):
                    if i >= 2:
                        sp.wait_ge(q["res"], i - 1)
                    src = io["x_prompt"][0, P * i:P * i + P, :] if i < NT else io["x_sample"][:, 0, :]
                    sp.dma_start(xin[0:rows(i), i % 2, :], src).then_inc(s_x[i % 2], 16)

        @block.gpsimd
        def _(pool):
            nc.gpsimd.memset(eps[:, :], LN_EPS).then_inc(q["eps"], 1)
            pool.dma_start(g[:, :], io["ln_mix_g"][layer:layer + 1, :].to_broadcast([P, D])).then_inc(q["in"], 16)
            pool.dma_start(b[:, :], io["ln_mix_b"][layer:layer + 1, :].to_broadcast([P, D])).then_inc(q["in"], 16)
            pool.dma_start(wr[:, :, :], io["w_router"].rearrange("(k p) e -> p k e", p=P)).then_inc(q["in"], 16)
            if layer:
                pool.dma_start(scale[:, :], io["pool_scale"].to_broadcast([P, D])).then_inc(q["in"], 16)
            nc.gpsimd.memset(lg[:, NT, :], 0.0).then_inc(q["zero"], 1)

        @block.tensor
        def _(pe):
            pe.wait_ge(q["w"], 48 if layer == 0 else 64)
            pe.wait_ge(q["in"], 48 if layer == 0 else 64)

            def products(i):
                n = rows(i)
                if i >= 2:
                    pe.wait_ge(q["res"], i - 1)
                for h in range(2):
                    if layer == 0:
                        for k in range(KD):
                            last = nc.tensor.matmul(pb[0:n, 2 * (i % 2) + h, :], lhs(k, i), w[:, k, 512 * h:512 * h + 512],
                                                    start=(k == 0), stop=(k == KD - 1))
                    else:
                        for gi in (2 * h, 2 * h + 1):
                            for k in range(2):
                                last = nc.tensor.matmul(pb[0:n, 2 * (i % 2) + h, 256 * (gi % 2):256 * (gi % 2) + 256],
                                                        lhs(2 * gi + k, i), w[:, 2 * gi + k, :], start=(k == 0), stop=(k == 1))
                last.then_inc(q["mm"], 1)

            def router(i):
                n = rows(i)
                pe.wait_ge(q["lg"], 2 * i + 2)
                for k in range(KD):
                    last = nc.tensor.transpose(pb[:, 4 + k // 4, P * (k % 4):P * (k % 4) + n], xr[0:n, i, P * k:P * k + P],
                                               const["ident"][0:n, 0:n])
                last.then_inc(q["tr"], 1)
                pe.wait_ge(q["cp"], i + 1)
                if i >= 1:
                    pe.wait_ge(q["ev"], i)
                for k in range(KD):
                    last = nc.tensor.matmul(pb[0:n, 6, 0:E], xT[:, k, 0:n], wr[:, k, :], start=(k == 0), stop=(k == KD - 1))
                last.then_inc(q["rl"], 1)
            products(0)
            for i in range(1, TILES):
                products(i)
                router(i - 1)
            router(TILES - 1)

        @block.scalar
        def _(act):
            act.wait_ge(q["eps"], 1)

            def copy_x(i):
                n = rows(i)
                act.wait_ge(q["tr"], i + 1)
                nc.scalar.copy(xT[:, :, 0:n], pb[:, 4:6, :].rearrange("p b (k t) -> p (b k) t", k=4)[:, :, 0:n])\
                    .then_inc(q["cp"], 1)
            for i in range(TILES):
                n = rows(i)
                act.wait_ge(q["var"], i + 1)
                nc.scalar.activation(st[0:n, 14:15], st[0:n, 13:14], ACT.Sqrt, bias=eps[0:n, :]).then_inc(q["root"], 1)
                if i:
                    copy_x(i - 1)
            copy_x(TILES - 1)

        @block.vector
        def _(dve):
            dve.wait_ge(q["in"], 48 if layer == 0 else 64)
            dve.wait_ge(q["zero"], 1)

            def take_logits(i):
                dve.wait_ge(q["rl"], i + 1)
                nc.vector.tensor_copy(lg[0:rows(i), i, :], pb[0:rows(i), 6, 0:E]).then_inc(q["ev"], 1)
            for i in range(TILES):
                n = rows(i)
                x = xr[0:n, i, :]
                dve.wait_ge(q["mm"], i + 1)
                banks = pb[0:n, 2 * (i % 2):2 * (i % 2) + 2, :].rearrange("p b n -> p (b n)")
                if layer == 0:
                    dve.wait_ge(s_x[i % 2], 16 * (i // 2 + 1))
                    nc.vector.scalar_tensor_tensor(out=x, in0=xin[0:n, i % 2, :], scalar=ALPHA, in1=banks,
                                                   op0=ALU.mult, op1=ALU.add).then_inc(q["res"], 1)
                else:
                    nc.vector.tensor_tensor(xin[0:n, i % 2, :], banks, scale[0:n, :], ALU.mult).then_inc(q["sc"], 1)
                    dve.wait_ge(q["sc"], i + 1)
                    nc.vector.scalar_tensor_tensor(out=x, in0=x, scalar=ALPHA, in1=xin[0:n, i % 2, :],
                                                   op0=ALU.mult, op1=ALU.add).then_inc(q["res"], 1)
                dve.wait_ge(q["res"], i + 1)
                for h in range(2):
                    last = nc.vector.bn_stats(st[0:n, 6 * h:6 * h + 6], x[:, 512 * h:512 * h + 512])
                last.then_inc(q["ln"], 1)
                dve.wait_ge(q["ln"], 3 * i + 1)
                nc.vector.bn_aggr(st[0:n, 12:14], st[0:n, 0:12]).then_inc(q["var"], 1)
                if i:
                    take_logits(i - 1)
                dve.wait_ge(q["root"], i + 1)
                nc.vector.reciprocal(st[0:n, 15:16], st[0:n, 14:15]).then_inc(q["ln"], 1)
                dve.wait_ge(q["ln"], 3 * i + 2)
                nc.vector.tensor_scalar(x, x, st[0:n, 12:13], st[0:n, 15:16], ALU.subtract, ALU.mult).then_inc(q["ln"], 1)
                dve.wait_ge(q["ln"], 3 * i + 3)
                nc.vector.tensor_tensor(x, x, g[0:n, :], ALU.mult).then_inc(q["lg"], 1)
                dve.wait_ge(q["lg"], 2 * i + 1)
                nc.vector.tensor_tensor(x, x, b[0:n, :], ALU.add).then_inc(q["lg"], 1)
            take_logits(TILES - 1)


def route(nc, io, layer, xr, lg, gates, slots, table, const):
    with Memory(nc, f"ro{layer}") as m:
        br = m.sb("b_router", [P, E])
        valid = m.sb("valid", [P, TILES])
        earlier = m.sb("earlier", [P, P])
        ones = m.sb("ones", [P, P])
        blocks = m.sb("blocks", [P, NBLK])
        p = m.sb("probs", [P, TILES, E])
        w = m.sb("work", [P, TILES, E])
        best = m.sb("best", [P, 2, TILES, E])
        A = m.sb("assigned", [P, TILES, E])
        slot = m.sb("slot", [P, TILES, E])
        base = m.sb("counts_before", [P, TILES + 1, E])
        t9 = m.sb("per_token", [P, 6, TILES])
        gs = m.sb("group", [P, 6, TILES, NG])
        rank_e = m.sb("descending_experts", [P, E])
        rank_g = m.sb("descending_groups", [P, NG])
        thr = m.sb("thresholds", [P, TILES, E])
        nb = m.sb("blocks_per_expert", [P, 3, E])
        cmpb = m.sb("block_compare", [P, NBLK, E])
        tf = m.sb("table_f", [P, NBLK])
        one = m.sb("one", [P, E])
        pb = m.psum("pb", [P, 8, 512])
        q = {k: m.sem(k) for k in "in io mx ex as rk chain slots sc tab".split()}
        block = m.block()
        N3 = [P, TILES, E]

        def per_token(a):
            return a.unsqueeze(2).to_broadcast(N3)

        @block.sync
        def _(sp):
            sp.dma_start(br[:, :], io["b_router"].rearrange("(a e) -> a e", a=1).to_broadcast([P, E])).then_inc(q["in"], 16)
            for dst, name in ((valid, "valid"), (earlier, "earlier"), (ones, "ones"), (blocks, "blocks")):
                sp.dma_start(dst[:, :], io[f"c_{name}"]).then_inc(q["in"], 16)

        @block.tensor
        def _(pe):
            pe.wait_ge(q["in"], 80)
            pe.wait_ge(q["as"], 1)
            a = A[:, :, :].rearrange("p t e -> p (t e)")
            nc.tensor.matmul(pb[:, 0, 0:TILES * E], earlier[:, :], a, start=True, stop=True)
            nc.tensor.matmul(pb[:, 1, 0:TILES * E], ones[:, :], a, start=True, stop=True).then_inc(q["rk"], 1)

        @block.scalar
        def _(act):
            act.wait_ge(q["mx"], 1)
            nc.scalar.activation(p[:, :, :], p[:, :, :], ACT.Exp).then_inc(q["ex"], 1)

        @block.gpsimd
        def _(pool):
            nc.gpsimd.iota(rank_e[:, :], [[-1, E]], base=E, channel_multiplier=0,
                           allow_small_or_imprecise_dtypes=True)
            nc.gpsimd.iota(rank_g[:, :], [[-1, NG]], base=NG, channel_multiplier=0,
                           allow_small_or_imprecise_dtypes=True)
            nc.gpsimd.memset(one[:, :], 1.0)
            nc.gpsimd.iota(thr[:, :, :], [[P, TILES], [0, E]], base=0, channel_multiplier=0,
                           allow_small_or_imprecise_dtypes=True).then_inc(q["io"], 1)
            pool.wait_ge(q["slots"], 1)
            for i in range(TILES):
                n = rows(i)
                for c in range(2):
                    pool.indirect_dma_start(io["slots_in"], bass.IndirectOffsetOnAxis(ap=slots[0:n, i, c:c + 1], axis=0),
                                            xr[0:n, i, :], None).then_inc(q["sc"], 16)
            pool.wait_ge(q["sc"], 32 * TILES)

        @block.vector
        def _(dve):
            link = Linked(dve, q["chain"])
            tt, ts, red = nc.vector.tensor_tensor, nc.vector.tensor_scalar, nc.vector.tensor_reduce
            dve.wait_ge(q["in"], 80)
            dve.wait_ge(q["io"], 1)
            link(tt(p[:, :, :], lg[:, :, :], br[:, :].unsqueeze(1).to_broadcast(N3), ALU.add))
            link(red(t9[:, 0, :], p[:, :, :], AX, ALU.max))
            tt(p[:, :, :], p[:, :, :], per_token(t9[:, 0, :]), ALU.subtract).then_inc(q["mx"], 1)
            dve.wait_ge(q["ex"], 1)
            link(red(t9[:, 0, :], p[:, :, :], AX, ALU.add))
            link(nc.vector.reciprocal(t9[:, 0, :], t9[:, 0, :]))
            link(tt(p[:, :, :], p[:, :, :], per_token(t9[:, 0, :]), ALU.mult))
            pv = p[:, :, :].rearrange("p t (g e) -> p t g e", g=NG)
            e0, e1, e2, e3 = (pv[:, :, :, k] for k in range(EPG))
            tt(gs[:, 0], e0, e1, ALU.max)
            tt(gs[:, 1], e0, e1, ALU.min)
            tt(gs[:, 2], e2, e3, ALU.max)
            link(tt(gs[:, 3], e2, e3, ALU.min))
            tt(gs[:, 4], gs[:, 0], gs[:, 2], ALU.max)
            tt(gs[:, 5], gs[:, 0], gs[:, 2], ALU.min)
            link(tt(gs[:, 1], gs[:, 1], gs[:, 3], ALU.max))
            link(tt(gs[:, 5], gs[:, 5], gs[:, 1], ALU.max))
            link(tt(gs[:, 4], gs[:, 4], gs[:, 5], ALU.add))
            link(red(t9[:, 0, :], gs[:, 4], AX, ALU.max))
            G3 = [P, TILES, NG]
            link(tt(gs[:, 0], gs[:, 4], t9[:, 0, :].unsqueeze(2).to_broadcast(G3), ALU.is_equal))
            link(tt(gs[:, 0], gs[:, 0], rank_g[:, :].unsqueeze(1).to_broadcast(G3), ALU.mult))
            link(red(t9[:, 0, :], gs[:, 0], AX, ALU.max))
            link(tt(gs[:, 0], gs[:, 0], t9[:, 0, :].unsqueeze(2).to_broadcast(G3), ALU.is_equal))
            for k in range(EPG):
                last = tt(pv[:, :, :, k], pv[:, :, :, k], gs[:, 0], ALU.mult)
            link(last)
            link(ts(gs[:, 1], gs[:, 0], -1.0, None, ALU.add))
            for k in range(EPG):
                last = tt(pv[:, :, :, k], pv[:, :, :, k], gs[:, 1], ALU.add)
            link(last)
            for c in range(2):
                link(red(t9[:, 1 + c, :], p[:, :, :], AX, ALU.max))
                link(tt(w[:, :, :], p[:, :, :], per_token(t9[:, 1 + c, :]), ALU.is_equal))
                link(tt(w[:, :, :], w[:, :, :], rank_e[:, :].unsqueeze(1).to_broadcast(N3), ALU.mult))
                link(red(t9[:, 0, :], w[:, :, :], AX, ALU.max))
                link(tt(best[:, c], w[:, :, :], per_token(t9[:, 0, :]), ALU.is_equal))
                if c == 0:
                    link(nc.vector.scalar_tensor_tensor(out=p[:, :, :], in0=best[:, 0], scalar=-4.0, in1=p[:, :, :],
                                                        op0=ALU.mult, op1=ALU.add))
            link(tt(A[:, :, :], best[:, 0], best[:, 1], ALU.add))
            tt(A[:, :, :], A[:, :, :], per_token(valid[:, :]), ALU.mult).then_inc(q["as"], 1)
            link(tt(t9[:, 3, :], t9[:, 1, :], t9[:, 2, :], ALU.add))
            link(nc.vector.reciprocal(t9[:, 3, :], t9[:, 3, :]))
            for c in range(2):
                link(tt(gates[:, :, c], t9[:, 1 + c, :], t9[:, 3, :], ALU.mult))
            dve.wait_ge(q["rk"], 1)
            link(nc.vector.memset(base[:, 0, :], 0.0))
            for i in range(TILES):
                link(tt(base[:, i + 1, :], base[:, i, :], pb[:, 1, E * i:E * i + E], ALU.add))
            link(tt(slot[:, :, :], base[:, 0:TILES, :], pb[:, 0, 0:TILES * E].rearrange("p (t e) -> p t e", t=TILES), ALU.add))
            link(tt(w[:, :, :], base[:, TILES, :].unsqueeze(1).to_broadcast(N3), thr[:, :, :], ALU.is_gt))
            link(red(nb[:, 0, :], w[:, :, :].rearrange("p t e -> p e t"), AX, ALU.add))
            link(nc.vector.tensor_tensor_scan(nb[:, 1, :], one[:, :], nb[:, 0, :], 0.0, ALU.mult, ALU.add))
            link(tt(nb[:, 2, :], nb[:, 1, :], nb[:, 0, :], ALU.subtract))
            link(ts(nb[:, 2, :], nb[:, 2, :], float(P), None, ALU.mult))
            link(tt(slot[:, :, :], slot[:, :, :], nb[:, 2, :].unsqueeze(1).to_broadcast(N3), ALU.add))
            for c in range(2):
                link(tt(w[:, :, :], slot[:, :, :], best[:, c], ALU.mult))
                link(red(t9[:, 4 + c, :], w[:, :, :], AX, ALU.add))
            for c in range(2):
                last = nc.vector.tensor_copy(slots[:, :, c], t9[:, 4 + c, :])
            last.then_inc(q["slots"], 1)
            B3 = [P, NBLK, E]
            link(tt(cmpb[:, :, :], blocks[:, :].unsqueeze(2).to_broadcast(B3), nb[:, 1, :].unsqueeze(1).to_broadcast(B3),
                    ALU.is_ge))
            link(red(tf[:, :], cmpb[:, :, :], AX, ALU.add))
            link(ts(tf[:, :], tf[:, :], float(E - 1), None, ALU.min))
            nc.vector.tensor_copy(table[:, :], tf[0:1, :]).then_inc(q["tab"], 1)
            dve.wait_ge(q["tab"], 1)


def experts(nc, io, layer, table, const):
    with Memory(nc, f"ex{layer}") as m:
        wgu = m.sb("w_gate_up", [P, 2, KD, 2 * FF])
        wd = m.sb("w_down", [P, 2, 2, D])
        xs = m.sb("x_rows", [P, 2, D])
        xT = m.sb("xT", [P, 2, KD, P])
        h = m.sb("hidden", [P, 2, FF])
        hT = m.sb("hiddenT", [P, 2, 2, P])
        y = m.sb("y_rows", [P, 2, D])
        pb = m.psum("pb", [P, 8, 512])
        q = {k: m.sem(k) for k in "gu xt dn ht silu h xca xcv hc ya yv".split()}
        s_wgu = [m.sem(f"w_gate_up{u}") for u in range(2)]
        s_wd = [m.sem(f"w_down{u}") for u in range(2)]
        s_xs = [m.sem(f"x_rows{u}") for u in range(2)]
        s_st = [m.sem(f"stored{u}") for u in range(2)]
        block = m.block()
        pairs = NBLK // 2

        def steps(eng, body):
            for u in range(2):
                body(0, u, True, False)
            with eng.Fori(1, pairs - 1) as i:
                for u in range(2):
                    body(i, u, False, False)
            for u in range(2):
                body(pairs - 1, u, False, True)

        @block.sync
        def _(sp):
            def body(i, u, first, last):
                j = 2 * i + u
                e = sp.value_load(table[0:1, bass.ds(j, 1)], min_val=0, max_val=E - 1)
                if not first:
                    sp.wait_ge(q["xt"], j - 1)
                sp.dma_start(xs[:, u, :], io["slots_in"][bass.ds(j * P, P), :]).then_inc(s_xs[u], 16)
                if not first:
                    sp.wait_ge(q["gu"], j - 1)
                for half, name in enumerate(("w_ex_gate", "w_ex_up")):
                    sp.dma_start(wgu[:, u, :, FF * half:FF * half + FF],
                                 io[name][layer][bass.ds(e, 1)].rearrange("a (k p) f -> p (a k) f", p=P)).then_inc(s_wgu[u], 16)
                if not first:
                    sp.wait_ge(q["dn"], j - 1)
                sp.dma_start(wd[:, u, :, :], io["w_ex_down"][layer][bass.ds(e, 1)].rearrange("a (k p) n -> p (a k) n", p=P))\
                    .then_inc(s_wd[u], 16)
            steps(sp, body)

        @block.tensor
        def _(pe):
            mm = nc.tensor.matmul

            def transpose_x(i, u):
                pe.wait_ge(s_xs[u], 16 * i + 16)
                for k in range(KD):
                    t = nc.tensor.transpose(pb[:, k // 4, P * (k % 4):P * (k % 4) + P], xs[:, u, P * k:P * k + P],
                                            const["ident"][:, :])
                t.then_inc(q["xt"], 1)

            def down(i, u):
                j = 2 * i + u
                pe.wait_ge(q["hc"], j + 1)
                pe.wait_ge(s_wd[u], 16 * i + 16)
                for half in range(2):
                    for k in range(2):
                        t = mm(pb[:, 5 + half, :], hT[:, u, k, :], wd[:, u, k, 512 * half:512 * half + 512],
                               start=(k == 0), stop=(k == 1))
                t.then_inc(q["dn"], 1)

            def body(i, u, first, last):
                j = 2 * i + u
                pe.wait_ge(q["xca"], j + 1)
                pe.wait_ge(q["xcv"], j + 1)
                pe.wait_ge(s_wgu[u], 32 * i + 32)
                if not first:
                    pe.wait_ge(q["h"], j - 1)
                for k in range(KD):
                    t = mm(pb[:, 2 + u, :], xT[:, u, k, :], wgu[:, u, k, :], start=(k == 0), stop=(k == KD - 1))
                t.then_inc(q["gu"], 1)
                if not (last and u == 1):
                    transpose_x(i + u, 1 - u)
                if not (first and u == 0):
                    if not (first and u == 1):
                        pe.wait_ge(q["ya"], j - 1)
                        pe.wait_ge(q["yv"], j - 1)
                    down(i - 1 + u, 1 - u)
                pe.wait_ge(q["h"], j + 1)
                if not (first and u == 0):
                    pe.wait_ge(q["hc"], j)
                for k in range(2):
                    t = nc.tensor.transpose(pb[:, 4, P * k:P * k + P], h[:, u, P * k:P * k + P], const["ident"][:, :])
                t.then_inc(q["ht"], 1)
            transpose_x(0, 0)
            steps(pe, body)
            pe.wait_ge(q["ya"], NBLK - 1)
            pe.wait_ge(q["yv"], NBLK - 1)
            down(pairs - 1, 1)

        def copy_x(eng, copy, u, half, sem, j):
            eng.wait_ge(q["xt"], j + 1)
            copy(xT[:, u, 4 * half:4 * half + 4, :], pb[:, half, :].rearrange("p (k t) -> p k t", k=4)).then_inc(q[sem], 1)

        @block.scalar
        def _(act):
            def out(i, u, first):
                j = 2 * i + u
                act.wait_ge(q["dn"], j + 1)
                if not first:
                    act.wait_ge(s_st[u], 16 * i)
                nc.scalar.copy(y[:, u, 0:512], pb[:, 5, :]).then_inc(q["ya"], 1)
                act.wait_ge(q["ya"], j + 1)
                act.wait_ge(q["yv"], j + 1)
                act.dma_start(io["slots_out"][bass.ds(j * P, P), :], y[:, u, :]).then_inc(s_st[u], 16)

            def body(i, u, first, last):
                j = 2 * i + u
                act.wait_ge(q["gu"], j + 1)
                if not first:
                    act.wait_ge(q["ht"], j - 1)
                nc.scalar.activation(h[:, u, :], pb[:, 2 + u, 0:FF], ACT.Silu).then_inc(q["silu"], 1)
                if not (last and u == 1):
                    copy_x(act, nc.scalar.copy, 1 - u, 0, "xca", j + 1)
                if not (first and u == 0):
                    out(i - 1 + u, 1 - u, first)
                act.wait_ge(q["ht"], j + 1)
                nc.scalar.copy(hT[:, u, :, :], pb[:, 4, 0:2 * P].rearrange("p (k t) -> p k t", k=2)).then_inc(q["hc"], 1)
            copy_x(act, nc.scalar.copy, 0, 0, "xca", 0)
            steps(act, body)
            out(pairs - 1, 1, False)
            for u in range(2):
                act.wait_ge(s_st[u], 16 * pairs)

        @block.vector
        def _(dve):
            def out(i, u, first):
                j = 2 * i + u
                dve.wait_ge(q["dn"], j + 1)
                if not first:
                    dve.wait_ge(s_st[u], 16 * i)
                nc.vector.tensor_copy(y[:, u, 512:1024], pb[:, 6, :]).then_inc(q["yv"], 1)

            def body(i, u, first, last):
                j = 2 * i + u
                dve.wait_ge(q["silu"], j + 1)
                nc.vector.tensor_tensor(h[:, u, :], h[:, u, :], pb[:, 2 + u, FF:2 * FF], ALU.mult).then_inc(q["h"], 1)
                if not (last and u == 1):
                    copy_x(dve, nc.vector.tensor_copy, 1 - u, 1, "xcv", j + 1)
                if not (first and u == 0):
                    out(i - 1 + u, 1 - u, first)
            copy_x(dve, nc.vector.tensor_copy, 0, 1, "xcv", 0)
            steps(dve, body)
            out(pairs - 1, 1, False)


def combine(nc, io, layer, xr, gates, slots, const):
    with Memory(nc, f"cb{layer}") as m:
        r = m.sb("expert_rows", [P, 2, 2, D])
        g = m.sb("ln_g", [P, D])
        b = m.sb("ln_b", [P, D])
        st = m.sb("stats", [P, 16])
        eps = m.sb("eps", [P, 1])
        q = {k: m.sem(k) for k in "in eps a1 a2 a3 ln lg var root done out".split()}
        s_r = [m.sem(f"rows{u}") for u in range(2)]
        block = m.block()

        @block.gpsimd
        def _(pool):
            nc.gpsimd.memset(eps[:, :], LN_EPS).then_inc(q["eps"], 1)
            for i in range(TILES):
                n = rows(i)
                if i >= 2:
                    pool.wait_ge(q["a3"], i - 1)
                for c in range(2):
                    pool.indirect_dma_start(r[0:n, i % 2, c, :], None, io["slots_out"],
                                            bass.IndirectOffsetOnAxis(ap=slots[0:n, i, c:c + 1], axis=0)).then_inc(s_r[i % 2], 16)

        @block.sync
        def _(sp):
            sp.dma_start(g[:, :], io["ln_ffn_g"][layer:layer + 1, :].to_broadcast([P, D])).then_inc(q["in"], 16)
            sp.dma_start(b[:, :], io["ln_ffn_b"][layer:layer + 1, :].to_broadcast([P, D])).then_inc(q["in"], 16)
            if layer == 1:
                for i in range(TILES):
                    sp.wait_ge(q["lg"], 2 * i + 2)
                    dst = io["o_y_prompt"][0, P * i:P * i + P, :] if i < NT else io["o_y_sample"][:, 0, :]
                    sp.dma_start(dst, xr[0:rows(i), i, :]).then_inc(q["out"], 16)
                sp.wait_ge(q["out"], 16 * TILES)

        @block.scalar
        def _(act):
            act.wait_ge(q["eps"], 1)
            for i in range(TILES):
                n = rows(i)
                act.wait_ge(q["var"], i + 1)
                nc.scalar.activation(st[0:n, 14:15], st[0:n, 13:14], ACT.Sqrt, bias=eps[0:n, :]).then_inc(q["root"], 1)

        @block.vector
        def _(dve):
            stt = nc.vector.scalar_tensor_tensor
            dve.wait_ge(q["in"], 32)
            for i in range(TILES):
                n = rows(i)
                x = xr[0:n, i, :]
                dve.wait_ge(s_r[i % 2], 32 * (i // 2 + 1))
                r1, r2 = r[0:n, i % 2, 0, :], r[0:n, i % 2, 1, :]
                nc.vector.tensor_scalar(r1, r1, gates[0:n, i, 0:1], None, ALU.mult).then_inc(q["a1"], 1)
                dve.wait_ge(q["a1"], i + 1)
                stt(out=r1, in0=r2, scalar=gates[0:n, i, 1:2], in1=r1, op0=ALU.mult, op1=ALU.add).then_inc(q["a2"], 1)
                dve.wait_ge(q["a2"], i + 1)
                stt(out=x, in0=x, scalar=ALPHA, in1=r1, op0=ALU.mult, op1=ALU.add).then_inc(q["a3"], 1)
                dve.wait_ge(q["a3"], i + 1)
                for h in range(2):
                    last = nc.vector.bn_stats(st[0:n, 6 * h:6 * h + 6], x[:, 512 * h:512 * h + 512])
                last.then_inc(q["ln"], 1)
                dve.wait_ge(q["ln"], 3 * i + 1)
                nc.vector.bn_aggr(st[0:n, 12:14], st[0:n, 0:12]).then_inc(q["var"], 1)
                dve.wait_ge(q["root"], i + 1)
                nc.vector.reciprocal(st[0:n, 15:16], st[0:n, 14:15]).then_inc(q["ln"], 1)
                dve.wait_ge(q["ln"], 3 * i + 2)
                nc.vector.tensor_scalar(x, x, st[0:n, 12:13], st[0:n, 15:16], ALU.subtract, ALU.mult).then_inc(q["ln"], 1)
                dve.wait_ge(q["ln"], 3 * i + 3)
                nc.vector.tensor_tensor(x, x, g[0:n, :], ALU.mult).then_inc(q["lg"], 1)
                dve.wait_ge(q["lg"], 2 * i + 1)
                nc.vector.tensor_tensor(x, x, b[0:n, :], ALU.add).then_inc(q["lg"], 1)
            dve.wait_ge(q["lg"], 2 * TILES)




def constants():
    i = np.arange(P)
    same = (i[:, None] // CH) == (i[None, :] // CH)
    up = (i[:, None] < i[None, :]) & same
    tabs = {"ident": np.eye(P), "low": up.T, "up": up, "up_incl": up | np.eye(P, dtype=bool),
            "head_ones": (i[:, None] // HD) == (i[None, :] // HD),
            "earlier": i[:, None] < i[None, :], "ones": np.ones((P, P))}
    for lev in range(6):
        b = 1 << lev
        off = ((i[:, None] // (2 * b)) == (i[None, :] // (2 * b))) & ((i[:, None] // b) % 2 == 1) & ((i[None, :] // b) % 2 == 0)
        if lev == 0:
            tabs["lev0"] = off
        tabs[f"lev{lev}T"] = off.T
    dist = 2 * WIN - 1 - np.arange(384)
    n = np.maximum(dist, 0)
    scaled = np.log(np.maximum(n, 16).astype(np.float32) / np.float32(16)) / np.float32(math.log(128 / 16))
    large = np.minimum(16 + (scaled * np.float32(16)).astype(np.int32), NBUCK - 1)
    bucket = np.where(n < 16, n, large)
    valid = (dist >= 0) & (dist <= WIN)
    onehot = np.zeros((NBUCK + 1, 384))
    onehot[np.where(valid, bucket, NBUCK), np.arange(384)] = 1
    r = np.arange(NS * 8)
    own = np.where((r[:, None] // 8) == np.arange(NS)[None, :], 0.0, NEG)
    cnt = np.minimum(np.array(POOLW)[:, None], np.arange(16)[None, :] + 1)
    tok = i[:, None] + P * np.arange(TILES)[None, :]
    out = {**{k: v for k, v in tabs.items()}, "onehot": onehot, "neg": np.full((1, 8), NEG), "own": own,
           "rowhead": np.tile(np.eye(8), (NS, 1)),
           "invcnt": np.tile((1.0 / cnt.astype(np.float32)).reshape(1, 64), (P, 1)),
           "valid": tok < TT, "blocks": np.tile(np.arange(NBLK)[None, :], (P, 1))}
    return {f"c_{k}": np.ascontiguousarray(np.asarray(v).astype(np.float32)) for k, v in out.items()}


SQUARE = ("ident", "low", "up", "up_incl", "head_ones", "earlier", "ones", "lev0", "lev0T", "lev1T", "lev2T", "lev3T", "lev4T", "lev5T")

_INS = ['x_prompt', 'x_sample', 'state_rwkv', 'state_shift', 'cache_swa_k', 'cache_swa_v', 'state_pool', 'w_in',
        'tshift_mu', 'decay_w0', 'decay_w2', 'iclr_a0', 'iclr_a2', 'gate_w2', 'k_k', 'k_a', 'r_k', 'lnx_g', 'lnx_b',
        'attn_sinks', 'rel_bias', 'w_out', 'w_pool', 'pool_scale', 'ln_mix_g', 'ln_mix_b', 'ln_ffn_g', 'ln_ffn_b',
        'w_router', 'b_router', 'w_ex_gate', 'w_ex_up', 'w_ex_down']
_OUTS = [('y_prompt', (1, T, D)), ('y_sample', (NS, 1, D)), ('rwkv_prompt', (1, 1, HA, HD, HD)),
         ('rwkv_sample', (1, NS, HA, HD, HD)), ('shift_prompt', (1, 1, D)), ('shift_sample', (1, NS, D)),
         ('k_prompt', (1, 1, WIN, KVH, HD)), ('k_sample', (1, NS, WIN, KVH, HD)),
         ('v_prompt', (1, 1, WIN, KVH, HD)), ('v_sample', (1, NS, WIN, KVH, HD)),
         ('pool_prompt', (1, 1, KEEP, D)), ('pool_sample', (1, NS, KEEP, D))]


def build(nc, io):
    with ExitStack() as whole:
        sb = lambda ctx, name, shape, dt=F32: ctx.enter_context(nc.sbuf_tensor(name, shape, dt))
        const = {"ident": sb(whole, "k_ident", [P, P])}
        lg = sb(whole, "logits", [P, TILES, E])
        gates = sb(whole, "gates", [P, TILES, 2])
        slots = sb(whole, "slots", [P, TILES, 2], U32)
        table = sb(whole, "block_experts", [1, NBLK], I32)
        with ExitStack() as layer0:
            yb = sb(layer0, "attention_out", [P, 4, TT])
            mix_const = {k: sb(layer0, f"k_{k}", [P, P]) for k in SQUARE if k not in ("ident", "earlier", "ones")}
            const.update(mix_const)
            const["lnx_eps"] = sb(layer0, "lnx_eps", [P, 1])
            pr = sb(layer0, "projected", [P, 14, PC])
            vec = {k: sb(layer0, f"v_{k}", [P, 4]) for k in ("decay_w0", "iclr_a0", "k_k", "k_a", "r_k", "lnx_g", "lnx_b")}
            vec["mu"] = sb(layer0, "v_mu", [P, 14])
            loads = {k: (t[:, :], io[f"c_{k}"]) for k, t in mix_const.items()}
            for k in ("decay_w0", "iclr_a0", "k_k", "k_a", "lnx_g", "lnx_b"):
                loads[k] = (vec[k][:, :], by_partition(io[k][0], 4))
            loads["r_k"] = (vec["r_k"][:, :], by_partition(io["r_k"][0].rearrange("h d -> (h d)"), 4))
            mu = io["tshift_mu"][0]
            loads["mu"] = (vec["mu"][:, 0:12], by_partition(mu[0:3 * DA], 12))
            lo = 3 * DA
            loads["mu_lora"] = (vec["mu"][0:WL + AL, 12:13], mu[lo:lo + WL + AL].rearrange("(p a) -> p a", a=1))
            loads["mu_gate"] = (vec["mu"][0:GL, 13:14], mu[lo + WL + AL:lo + WL + AL + GL].rearrange("(p a) -> p a", a=1))
            with ExitStack() as attention:
                pq = sb(attention, "projected_qkv", [P, 6, PC])
                project(nc, io, pr, pq, loads, const)
                attend(nc, io, pq, yb, const)
                attend_samples(nc, io, pq, yb, const)
            with ExitStack() as rwkv:
                mx = sb(rwkv, "mixed", [P, 12, TT])
                cumx = sb(rwkv, "log_decay_before", [P, 4, TT])
                shift_mix(nc, io, pr, mx, cumx, vec, const)
                rwkv_sample(nc, io, pr, mx, const)
                rwkv_chunks(nc, io, pr, mx, cumx, const)
                rwkv_norm(nc, io, pr, mx, vec, const)
            xr = whole.enter_context(nc.sbuf_tensor("x_rows", [P, TILES, D], F32, side="right"))
            mix_out(nc, io, 0, lambda k, i: (pr if k < 4 else yb)[:, k % 4, P * i:P * i + rows(i)], xr, lg, const)
        for layer in range(2):
            if layer == 1:
                with ExitStack() as pooled:
                    feats = sb(pooled, "pooled", [P, KD, TT])
                    pool_features(nc, io, xr, feats, const)
                    mix_out(nc, io, 1, lambda k, i: feats[:, k, P * i:P * i + rows(i)], xr, lg, const)
            route(nc, io, layer, xr, lg, gates, slots, table, const)
            experts(nc, io, layer, table, const)
            combine(nc, io, layer, xr, gates, slots, const)


def declare(nc, inputs):
    arrays, io = {}, {}
    for name in _INS:
        a = np.ascontiguousarray(inputs[name])
        arrays[f"in_{name}"] = a
        io[name] = nc.dram_tensor(f"in_{name}", a.shape, F32, kind="ExternalInput").ap()
    for name, a in constants().items():
        arrays[f"in_{name}"] = a
        io[name] = nc.dram_tensor(f"in_{name}", a.shape, F32, kind="ExternalInput").ap()
    for name, shape in _OUTS:
        io["o_" + name] = nc.dram_tensor(f"out_{name}", shape, F32, kind="ExternalOutput").ap()
    for name, shape in (("bias_scratch", (8, P * 384)), ("sample_scratch", (6, NS, DA)), ("sample_y", (NS, DA)),
                        ("slots_in", (SLOTS, D)), ("slots_out", (SLOTS, D))):
        io[name] = nc.dram_tensor(f"scratch_{name}", shape, F32, kind="Internal").ap()
    return arrays, io


def kernel(**inputs):
    import concourse.bacc as bacc
    from concourse.bass_utils import run_bass_kernel_spmd

    nc = bacc.Bacc("TRN2", target_bir_lowering=False, num_devices=1)
    arrays, io = declare(nc, inputs)
    build(nc, io)
    r = run_bass_kernel_spmd(nc, [arrays], core_ids=[0])
    return tuple(r.results[0][f"out_{name}"] for name, _ in _OUTS)
```

```python
from contextlib import ExitStack
import math

import concourse.bass as bass
from concourse import mybir
import numpy as np

F32 = mybir.dt.float32
I32 = mybir.dt.int32
U32 = mybir.dt.uint32
ACT = mybir.ActivationFunctionType
ALU = mybir.AluOpType
AX = mybir.AxisListType.X

P = 128
D = 1024
KD = D // P
T = 1024
NT = T // P
NS = 8
TT = T + NS
TC = TT + NS
PC = TC + 1
S0C, V0C = T + 1, T + 1 + NS
DA = 512
HD = 64
HA = DA // HD
WL, AL, GL = 32, 64, 96
KVH = 2
QPK = 4
WIN = 128
NBUCK = 32
NEG = -1e30
POOLW = (2, 4, 8, 16)
KEEP = 15
E = 16
NG = 4
EPG = E // NG
FF = 256
ALPHA = (2.0 * 2) ** 0.25
LN_EPS = 1e-5
LNX_EPS = 64e-5
CH = 64
TILES = NT + 1
NBLK = (2 * TT + E * (P - 1)) // P
SLOTS = (NBLK + 1) * P
EARLY = 2
SETS = 4
T_SETS = NBLK
T_ENDS = 2 * NBLK
T_LAST = 2 * NBLK + E
T_LEN = T_LAST + 1


def rows(i):
    return P if i < NT else NS


class Linked:

    def __init__(self, eng, sem):
        self.eng, self.sem, self.n = eng, sem, 0

    def __call__(self, ins):
        ins.then_inc(self.sem, 1)
        self.n += 1
        self.eng.wait_ge(self.sem, self.n)


class Memory:

    def __init__(self, nc, stage):
        self.nc, self.stage, self.ctx, self.sems = nc, stage, ExitStack(), []

    def __enter__(self):
        self.ctx.__enter__()
        return self

    def __exit__(self, *a):
        out = self.ctx.__exit__(*a)
        self.nc.clear_and_free_semaphores(self.sems)
        self.nc.all_engine_barrier()
        return out

    def sb(self, name, shape, dt=F32):
        return self.ctx.enter_context(self.nc.sbuf_tensor(f"{self.stage}_{name}", shape, dt))

    def psum(self, name, shape):
        return self.ctx.enter_context(self.nc.psum_tensor(f"{self.stage}_{name}", shape, F32))

    def sem(self, name):
        self.sems.append(self.nc.alloc_semaphore(f"{self.stage}_{name}"))
        return self.sems[-1]

    def block(self):
        return self.ctx.enter_context(self.nc.Block())


def by_partition(v, c):
    return v.rearrange("(c p) -> p c", c=c)


def project(nc, io, pr, pq, keep, const):
    w_in = io["w_in"][0]
    NR = 3 * DA
    slabs = [(0, 512), (512, 512), (1024, 512), (NR, WL + AL + GL), (NR + WL + AL + GL, 512),
             (NR + WL + AL + GL + 512, 256)]
    tiles = []
    for s in range(3):
        tiles += [(s, 128 * c, P, 4 * s + c) for c in range(4)]
    tiles += [(3, 0, WL + AL, 12), (3, WL + AL, GL, 13)]
    tiles += [(4, P * g, P, 14 + g) for g in range(QPK)]
    tiles += [(5, 0, P, 18), (5, 128, P, 19)]
    NW = 3
    QS = 4
    arrived = {s: 16 * sum((8 if z == QS else 1) for z in range(s % NW, s + 1, NW)) for s in range(len(slabs))}
    cols = [(0, 352), (352, 344), (696, 344)]
    with Memory(nc, "pj") as m:
        xt = m.sb("xt", [P, 3, D])
        xT = m.sb("xT", [P, KD, TC])
        w = m.sb("w", [P, NW, KD, 512])
        zero = m.sb("zero", [P, D])
        pb = m.psum("pb", [P, 8, 512])
        s_x = [m.sem(f"x{i}") for i in range(3)]
        s_w = [m.sem(f"w{i}") for i in range(NW)]
        s_id = m.sem("ident")
        s_tr = m.sem("transposed")
        s_xT = [m.sem(f"xT_copied{i}") for i in range(2)]
        s_mm = m.sem("product")
        s_ev = [m.sem(f"evacuated{i}") for i in range(2)]
        s_z = m.sem("zeroed")
        s_c = m.sem("consts")
        s_shift = m.sem("shift_out")
        s_slots = m.sem("slots_zeroed")
        block = m.block()
        xp = io["x_prompt"][0]
        n_out = len(tiles) * 3

        @block.sync
        def _(sp):
            def load_slab(s):
                c0, n = slabs[s]
                if s >= NW:
                    done = 3 * sum(t[0] <= s - NW for t in tiles)
                    sp.wait_ge(s_mm, done)
                src = w_in[:, c0:c0 + n].rearrange("(k p) n -> p k n", p=P)
                if s != QS:
                    sp.dma_start(w[:, s % NW, :, 0:n], src).then_inc(s_w[s % NW], 16)
                    return
                for h in range(KVH * QPK):
                    to = HD * (KVH * (h % QPK) + h // QPK)
                    sp.dma_start(w[:, s % NW, :, to:to + HD], src[:, :, HD * h:HD * h + HD]).then_inc(s_w[s % NW], 16)
            sp.dma_start(const["ident"][:, :], io["c_ident"]).then_inc(s_id, 16)
            for i in range(TILES):
                if i >= 3:
                    sp.wait_ge(s_tr, i - 2)
                if i < NT:
                    sp.dma_start(xt[:, i % 3, :], xp[P * i:P * i + P, :]).then_inc(s_x[i % 3], 16)
                else:
                    sp.dma_start(xt[0:NS, i % 3, :], io["x_sample"][:, 0, :]).then_inc(s_x[i % 3], 16)
                    sp.dma_start(xt[NS:2 * NS, i % 3, :], io["state_shift"][0]).then_inc(s_x[i % 3], 16)
                if i == 5:
                    load_slab(0)
            for s in range(1, len(slabs)):
                load_slab(s)

        @block.tensor
        def _(pe):
            pe.wait_ge(s_id, 16)
            for i in range(TILES):
                n = P if i < NT else 2 * NS
                pe.wait_ge(s_x[i % 3], 16 * (i // 3 + 1) if i < NT else 16 * (i // 3) + 32)
                if i >= 2:
                    pe.wait_ge(s_xT[i % 2], i // 2)
                for k in range(KD):
                    b = pb[:, 2 * (i % 2) + k // 4, 128 * (k % 4):128 * (k % 4) + n]
                    last = nc.tensor.transpose(b, xt[0:n, i % 3, 128 * k:128 * k + 128], const["ident"][0:n, 0:n])
                last.then_inc(s_tr, 1)
            pe.wait_ge(s_xT[0], 5)
            pe.wait_ge(s_xT[1], 4)
            at = 0
            seen = -1
            for (s, c0, mrows, _) in tiles:
                if s != seen:
                    pe.wait_ge(s_w[s % NW], arrived[s])
                    seen = s
                for (t0, tn) in cols:
                    if at >= 4:
                        pe.wait_ge(s_ev[at % 2], at // 2 - 1)
                    for k in range(KD):
                        last = nc.tensor.matmul(pb[0:mrows, 4 + at % 4, 0:tn], w[:, s % NW, k, c0:c0 + mrows], xT[:, k, t0:t0 + tn],
                                                start=(k == 0), stop=(k == KD - 1))
                    last.then_inc(s_mm, 1)
                    at += 1

        def evacuate(eng, copy, par):
            for i in range(par, TILES, 2):
                n = P if i < NT else 2 * NS
                eng.wait_ge(s_tr, i + 1)
                src = pb[:, 2 * par:2 * par + 2, :].rearrange("p b (k t) -> p (b k) t", k=4)[:, :, 0:n]
                copy(xT[:, :, P * i:P * i + n], src).then_inc(s_xT[par], 1)
            for at in range(par, n_out, 2):
                _, _, mrows, tile = tiles[at // 3]
                t0, tn = cols[at % 3]
                eng.wait_ge(s_mm, at + 1)
                dst = pr[0:mrows, tile, 1 + t0:1 + t0 + tn] if tile < 14 else pq[0:mrows, tile - 14, 1 + t0:1 + t0 + tn]
                copy(dst, pb[0:mrows, 4 + at % 4, 0:tn]).then_inc(s_ev[par], 1)

        @block.scalar
        def _(act):
            evacuate(act, nc.scalar.copy, 0)

        @block.vector
        def _(dve):
            nc.vector.memset(pr[:, :, 0:1], 0.0).then_inc(s_z, 1)
            evacuate(dve, nc.vector.tensor_copy, 1)

        @block.gpsimd
        def _(pool):
            pool.dma_start(io["o_shift_prompt"][0], io["x_prompt"][0, T - 1:T, :]).then_inc(s_shift, 16)
            pool.dma_start(io["o_shift_sample"][0], io["x_sample"][:, 0, :]).then_inc(s_shift, 16)
            n = 0
            for name, (dst, src) in keep.items():
                pool.dma_start(dst, src, allow_slow_non_contiguous=True).then_inc(s_c, 16)
                n += 16
            nc.gpsimd.memset(zero[:, :], 0.0).then_inc(s_z, 1)
            pool.wait_ge(s_z, 2)
            parts = [(name, b0, min(8, n_blk - b0)) for name, n_blk in (("slots_in", NBLK + 1), ("slots_out", NBLK))
                     for b0 in range(0, n_blk, 8)]
            for i, (name, b0, nb) in enumerate(parts):
                pool.wait_ge(s_mm, 3 + i * (n_out - 6) // len(parts))
                pool.dma_start(io[name][b0 * P:(b0 + nb) * P, :].rearrange("(b p) d -> p b d", p=P),
                               zero[:, :].unsqueeze(1).to_broadcast([P, nb, D])).then_inc(s_slots, 16)
            pool.wait_ge(s_c, n)
            pool.wait_ge(s_shift, 32)
            pool.wait_ge(s_slots, 16 * len(parts))


def attend(nc, io, pq, yb, const):
    SC = HD ** -0.5
    H = KVH * QPK
    NB1 = NBUCK + 1
    VW = 384
    with Memory(nc, "at") as m:
        rb = m.sb("rel_bias_rows", [NB1, H])
        rbb = m.sb("rel_bias_wide", [NB1, H, P])
        oh = m.sb("bucket_onehot", [NB1, VW])
        bias = m.sb("bias", [P, H, 2 * WIN])
        sinks = m.sb("sinks", [P, H])
        vt = m.sb("v_rows", [P, NT + 1, P])
        kz = m.sb("keys_by_head", [P, KVH, T])
        s = m.sb("scores", [P, 3, H, 2 * WIN])
        pT = m.sb("probsT", [P, H, 2, P])
        st = m.sb("stats", [P, 3, 6, H])
        kv_out = m.sb("kv_out", [P, 2, P])
        smp = m.sb("kv_sample", [NS, 2, P])
        pb = m.psum("pb", [P, 8, 512])
        names = ("in v_tr v_cp kz bias_ps bias_cp bias_wr bias_rd sc masked neg ex prob ptr pcp o y out k0 chain"
                 " rbw").split()
        q = {k: m.sem(k) for k in names}
        scr = io["bias_scratch"]
        bv = s[:, 0:2, :, :].rearrange("p a h k -> p (a h k)")[:, 0:H * VW].rearrange("p (h x) -> p h x", h=H)
        block = m.block()

        @block.gpsimd
        def _(pool):
            nc.gpsimd.memset(kz[:, :, :], 0.0).then_inc(q["kz"], 1)

        @block.sync
        def _(sp):
            for v in range(KVH):
                sp.dma_start(rb[0:NBUCK, v::KVH], io["rel_bias"][:, QPK * v:QPK * v + QPK],
                             allow_slow_non_contiguous=True).then_inc(q["in"], 16)
                sp.dma_start(sinks[:, v::KVH], io["attn_sinks"][:, QPK * v:QPK * v + QPK].to_broadcast([P, QPK]),
                             allow_slow_non_contiguous=True)\
                    .then_inc(q["in"], 16)
            sp.dma_start(oh[:, :], io["c_onehot"]).then_inc(q["in"], 16)
            sp.dma_start(rb[NBUCK:NB1, :], io["c_neg"]).then_inc(q["in"], 16)
            sp.wait_ge(q["bias_cp"], H)
            sp.dma_start(scr.rearrange("h (p x) -> p h x", p=P), bv).then_inc(q["bias_wr"], 16)
            sp.wait_ge(q["bias_wr"], 16)
            for h in range(H):
                src = scr[h, WIN - 1:WIN - 1 + P * (VW - 1)].rearrange("(p x) -> p x", x=VW - 1)[:, 0:2 * WIN]
                sp.dma_start(bias[:, h, :], src).then_inc(q["bias_rd"], 16)
            sp.wait_ge(q["k0"], 4)
            for j, name in enumerate(("k", "v")):
                sp.dma_start(io[f"o_{name}_prompt"][0, 0].rearrange("t h d -> t (h d)"), kv_out[:, j, :])\
                    .then_inc(q["out"], 16)
                dst = io[f"o_{name}_sample"][0].rearrange("b t h d -> b t (h d)")
                src = io[f"cache_swa_{name}"][0].rearrange("b t h d -> b t (h d)")
                sp.dma_start(dst[:, WIN - 1, :], smp[:, j, :]).then_inc(q["out"], 16)
                sp.dma_start(dst[:, 0:WIN - 1, :], src[:, 1:WIN, :]).then_inc(q["out"], 16)
            sp.wait_ge(q["out"], 96)

        @block.tensor
        def _(pe):
            ident = const["ident"]
            for n in range(NT):
                nc.tensor.transpose(pb[:, n // 4, 128 * (n % 4):128 * (n % 4) + 128],
                                    pq[:, 5, 1 + P * n:1 + P * n + P], ident[:, :])
            nc.tensor.transpose(pb[0:NS, 2, 0:P], pq[:, 5, S0C:S0C + NS], ident[:, :])
            nc.tensor.transpose(pb[:, 2, P:2 * P], pq[:, 4, 1 + T - P:1 + T], ident[:, :])
            nc.tensor.transpose(pb[0:NS, 2, 2 * P:3 * P], pq[:, 4, S0C:S0C + NS], ident[:, :]).then_inc(q["v_tr"], 1)
            pe.wait_ge(q["rbw"], 1)
            for h in range(H):
                if h >= 2:
                    pe.wait_ge(q["bias_cp"], h - 1)
                nc.tensor.matmul(pb[:, 6 + h % 2, 0:VW], rbb[:, h, :], oh[:, :], start=True, stop=True)\
                    .then_inc(q["bias_ps"], 1)
            pe.wait_ge(q["v_cp"], 1)
            pe.wait_ge(q["bias_cp"], H)
            pe.wait_ge(q["kz"], 1 + KVH)

            def scores(n):
                if n:
                    pe.wait_ge(q["masked"], 4 * n)
                lo = 0 if n else P
                for mm in range(QPK):
                    for v in range(KVH):
                        c = 256 * (mm % 2)
                        last = nc.tensor.matmul(pb[:, 2 * v + mm // 2, c + lo:c + 256], pq[:, mm, 1 + P * n:1 + P * n + P],
                                                kz[:, v, P * (n - 1) + lo:P * (n + 1)], start=True, stop=True)
                    last.then_inc(q["sc"], 1)

            def transposes(n, mm):
                if 4 * n + mm >= 2:
                    pe.wait_ge(q["pcp"], 4 * n + mm - 1)
                for v in range(KVH):
                    for j in (range(2) if n else (1,)):
                        last = nc.tensor.transpose(pb[:, 4 + mm % 2, 256 * v + 128 * j:256 * v + 128 * j + 128],
                                                   s[:, n % 3, 2 * mm + v, P * j:P * j + P], ident[:, :])
                last.then_inc(q["ptr"], 1)

            def output(n, mm):
                pe.wait_ge(q["pcp"], 4 * n + mm + 1)
                js = (0, 1) if n else (1,)
                for j in js:
                    for v in range(KVH):
                        last = nc.tensor.matmul(pb[64 * v:64 * v + 64, 6 + n % 2, P * mm:P * mm + P],
                                                vt[:, n - 1 + j, 64 * v:64 * v + 64], pT[:, 2 * mm + v, j, :],
                                                start=(j == js[0]), stop=(j == 1))
                return last
            scores(0)
            scores(1)
            for n in range(NT):
                if n + 2 < NT:
                    scores(n + 2)
                pe.wait_ge(q["prob"], n + 1)
                if n >= 2:
                    pe.wait_ge(q["y"], n - 1)
                transposes(n, 0)
                transposes(n, 1)
                for mm in range(QPK):
                    if mm + 2 < QPK:
                        transposes(n, mm + 2)
                    last = output(n, mm)
                last.then_inc(q["o"], 1)

        @block.scalar
        def _(act):
            act.wait_ge(q["v_tr"], 1)
            nc.scalar.copy(kv_out[:, 0, :], pb[:, 2, P:2 * P]).then_inc(q["k0"], 1)
            nc.scalar.copy(smp[:, 0, :], pb[0:NS, 2, 2 * P:3 * P]).then_inc(q["k0"], 1)
            nc.scalar.copy(smp[:, 1, :], pb[0:NS, 2, 0:P]).then_inc(q["k0"], 1)
            act.wait_ge(q["v_cp"], 1)
            nc.scalar.copy(kv_out[:, 1, :], vt[:, NT - 1, :]).then_inc(q["k0"], 1)
            for h in range(H):
                act.wait_ge(q["bias_ps"], h + 1)
                nc.scalar.copy(bv[:, h, :], pb[:, 6 + h % 2, 0:VW]).then_inc(q["bias_cp"], 1)
            act.wait_ge(q["kz"], 1)
            for v in range(KVH):
                own = slice(64 * v, 64 * v + 64)
                nc.scalar.copy(kz[own, v, :], pq[own, 4, 1:1 + T]).then_inc(q["kz"], 1)
            for n in range(NT + 1):
                if n < NT:
                    lo, u = (0 if n else P), n % 3
                    act.wait_ge(q["neg"], n + 1)
                    for h in range(H):
                        nc.scalar.activation(s[:, u, h, lo:2 * WIN], s[:, u, h, lo:2 * WIN], ACT.Exp,
                                             bias=st[:, u, 1, h:h + 1], accum_out=st[:, u, 2, h:h + 1])
                    nc.scalar.activation(st[:, u, 4, :], st[:, u, 3, :], ACT.Exp).then_inc(q["ex"], 1)
                if n:
                    if n >= 2:
                        act.wait_ge(q["o"], n - 1)
                    for mm in range(QPK):
                        act.wait_ge(q["ptr"], 4 * (n - 1) + mm + 1)
                        src = pb[:, 4 + mm % 2, :].rearrange("p (h j t) -> p h j t", h=2, j=2)
                        j0 = 0 if n > 1 else 1
                        nc.scalar.copy(pT[:, 2 * mm:2 * mm + 2, j0:2, :], src[:, :, j0:2, :]).then_inc(q["pcp"], 1)
                    act.wait_ge(q["o"], n)
                    nc.scalar.copy(yb[:, :, P * (n - 1):P * n],
                                   pb[:, 6 + (n - 1) % 2, :].rearrange("p (m t) -> p m t", m=QPK)).then_inc(q["y"], 1)

        @block.vector
        def _(dve):
            link = Linked(dve, q["chain"])
            dve.wait_ge(q["in"], 96)
            nc.vector.tensor_copy(rbb[:, :, :], rb[:, :].unsqueeze(2).to_broadcast([NB1, H, P])).then_inc(q["rbw"], 1)
            dve.wait_ge(q["v_tr"], 1)
            nc.vector.tensor_copy(vt[:, 0:NT, :], pb[:, 0:2, :].rearrange("p b (n d) -> p (b n) d", n=4))\
                .then_inc(q["v_cp"], 1)
            dve.wait_ge(q["bias_rd"], 16 * H)
            def masked_scores(n):
                lo, u = (0 if n else P), n % 3
                if n >= 3:
                    dve.wait_ge(q["ptr"], 4 * (n - 2))
                for b in range(4):
                    v, half = b % 2, b // 2
                    dve.wait_ge(q["sc"], 4 * n + 2 * half + 2)
                    src = pb[:, 2 * v + half, :].rearrange("p (m k) -> p m k", m=2)
                    h0 = 4 * half + v
                    nc.vector.scalar_tensor_tensor(
                        out=s[:, u, h0:h0 + 3:2, lo:], in0=src[:, :, lo:], scalar=SC,
                        in1=bias[:, h0:h0 + 3:2, lo:], op0=ALU.mult, op1=ALU.add).then_inc(q["masked"], 1)
                dve.wait_ge(q["masked"], 4 * n + 4)
                link(nc.vector.tensor_reduce(st[:, u, 0, :], s[:, u, :, lo:], AX, ALU.max))
                link(nc.vector.tensor_tensor(st[:, u, 0, :], st[:, u, 0, :], sinks[:, :], ALU.max))
                nc.vector.tensor_tensor(st[:, u, 3, :], sinks[:, :], st[:, u, 0, :], ALU.subtract)
                nc.vector.tensor_scalar(st[:, u, 1, :], st[:, u, 0, :], -1.0, None, ALU.mult).then_inc(q["neg"], 1)

            def normalise(n):
                lo, u = (0 if n else P), n % 3
                dve.wait_ge(q["ex"], n + 1)
                link(nc.vector.tensor_tensor(st[:, u, 5, :], st[:, u, 2, :], st[:, u, 4, :], ALU.add))
                link(nc.vector.reciprocal(st[:, u, 5, :], st[:, u, 5, :]))
                nc.vector.tensor_tensor(s[:, u, :, lo:], s[:, u, :, lo:],
                                        st[:, u, 5, :].unsqueeze(2).to_broadcast([P, H, 2 * WIN - lo]), ALU.mult)\
                    .then_inc(q["prob"], 1)
            masked_scores(0)
            for n in range(NT):
                if n + 1 < NT:
                    masked_scores(n + 1)
                normalise(n)


def attend_samples(nc, io, pq, yb, const):
    SC = HD ** -0.5
    H = KVH * QPK
    R = NS * H
    with Memory(nc, "as") as m:
        kc = m.sb("k_cache", [P, NS, P])
        vc = m.sb("v_cache", [P, NS, P])
        kcT = m.sb("k_cacheT", [P, NS, P])
        qs = m.sb("q_cols", [P, NS, QPK])
        sT = m.sb("scoresT", [P, 2, R])
        s = m.sb("scores", [R, P + NS])
        p = m.sb("probs", [R, P + NS])
        pT = m.sb("probsT", [P, 2, R])
        vs = m.sb("v_own", [NS, P])
        extra = m.sb("bias", [R, P + NS])
        sink = m.sb("sink", [R, 1])
        sinks = m.sb("sinks", [R, H])
        pick = m.sb("pick", [R, H])
        st = m.sb("stats", [R, 8])
        pb = m.psum("pb", [P, 8, 512])
        names = "in kt ktc qc sc scc tr mx ex pr tr2 tr2c o y chain".split()
        q = {k: m.sem(k) for k in names}
        block = m.block()

        @block.sync
        def _(sp):
            for dst, name in ((kc, "k"), (vc, "v")):
                sp.dma_start(dst[:, :, :], io[f"cache_swa_{name}"][0].rearrange("b t h d -> t b (h d)"))\
                    .then_inc(q["in"], 16)
            sp.dma_start(extra[:, P:P + NS], io["c_own"]).then_inc(q["in"], 16)
            sp.dma_start(pick[:, :], io["c_rowhead"]).then_inc(q["in"], 16)
            for v in range(KVH):
                sp.dma_start(sinks[:, v::KVH], io["attn_sinks"][:, QPK * v:QPK * v + QPK].to_broadcast([R, QPK]),
                             allow_slow_non_contiguous=True)\
                    .then_inc(q["in"], 16)
            for b in range(NS):
                sp.dma_start(extra[H * b:H * b + H, 0:P], io["bias_scratch"][:, WIN - 1:2 * WIN - 1]).then_inc(q["in"], 16)
                sp.dma_start(st[H * b:H * b + H, 7:8], io["bias_scratch"][:, 2 * WIN - 1:2 * WIN],
                             allow_slow_non_contiguous=True).then_inc(q["in"], 16)

        @block.tensor
        def _(pe):
            ident = const["ident"]
            pe.wait_ge(q["in"], 16 * (6 + 2 * NS))
            for b in range(NS):
                last = nc.tensor.transpose(pb[:, b // 4, P * (b % 4):P * (b % 4) + P], kc[:, b, :], ident[:, :])
            nc.tensor.transpose(pb[0:NS, 4, 0:P], pq[:, 5, S0C:S0C + NS], ident[:, :]).then_inc(q["kt"], 1)
            pe.wait_ge(q["ktc"], 1)
            pe.wait_ge(q["qc"], 1)
            for v in range(KVH):
                for b in range(NS):
                    nc.tensor.matmul(pb[:, 2 + v, QPK * b:QPK * b + QPK], kcT[64 * v:64 * v + 64, b, :],
                                     qs[64 * v:64 * v + 64, b, :], start=True, stop=True)
                last = nc.tensor.matmul(pb[0:NS, 2 + v, 128:128 + NS * QPK],
                                        pq[64 * v:64 * v + 64, 4, S0C:S0C + NS],
                                        qs[64 * v:64 * v + 64, :, :].rearrange("p b g -> p (b g)"), start=True, stop=True)
            last.then_inc(q["sc"], 1)
            pe.wait_ge(q["scc"], 1)
            nc.tensor.transpose(pb[0:R, 5, 0:P], sT[:, 0, :], ident[:, :])
            nc.tensor.transpose(pb[0:R, 5, P:P + NS], sT[0:NS, 1, :], ident[0:NS, 0:NS]).then_inc(q["tr"], 1)
            pe.wait_ge(q["pr"], 1)
            nc.tensor.transpose(pb[:, 6, 0:R], p[:, 0:P], ident[0:R, 0:R])
            nc.tensor.transpose(pb[0:NS, 6, R:2 * R], p[:, P:P + NS], ident[0:R, 0:R]).then_inc(q["tr2"], 1)
            pe.wait_ge(q["tr2c"], 1)
            for v in range(KVH):
                for b in range(NS):
                    c = H * b + v
                    o = pb[64 * v:64 * v + 64, 7, QPK * b:QPK * b + QPK]
                    nc.tensor.matmul(o, vc[:, b, 64 * v:64 * v + 64], pT[:, 0, c:c + 7:2], start=True, stop=False)
                    last = nc.tensor.matmul(o, vs[:, 64 * v:64 * v + 64], pT[0:NS, 1, c:c + 7:2], start=False, stop=True)
            last.then_inc(q["o"], 1)

        @block.scalar
        def _(act):
            act.wait_ge(q["kt"], 1)
            nc.scalar.copy(kcT[:, :, :], pb[:, 0:2, :].rearrange("p c (b k) -> p (c b) k", b=4))
            nc.scalar.copy(vs[:, :], pb[0:NS, 4, 0:P]).then_inc(q["ktc"], 1)
            act.wait_ge(q["mx"], 1)
            nc.scalar.activation(p[:, :], s[:, :], ACT.Exp, bias=st[:, 2:3], accum_out=st[:, 3:4])
            nc.scalar.activation(st[:, 4:5], sink[:, :], ACT.Exp, bias=st[:, 2:3]).then_inc(q["ex"], 1)
            act.wait_ge(q["o"], 1)
            nc.scalar.copy(yb[:, :, T:TT].rearrange("p m b -> p b m"),
                           pb[:, 7, 0:QPK * NS].rearrange("p (b m) -> p b m", b=NS)).then_inc(q["y"], 1)

        @block.vector
        def _(dve):
            link = Linked(dve, q["chain"])
            nc.vector.tensor_copy(qs[:, :, :], pq[:, 0:QPK, S0C:S0C + NS].rearrange("p m b -> p b m")).then_inc(q["qc"], 1)
            dve.wait_ge(q["sc"], 1)
            for v in range(KVH):
                cols = pb[:, 2 + v, 0:NS * QPK].rearrange("p (b g) -> p b g", b=NS)
                own = pb[0:NS, 2 + v, 128:128 + NS * QPK].rearrange("p (b g) -> p b g", b=NS)
                nc.vector.tensor_copy(sT[:, 0, :].rearrange("p (b g v) -> p b g v", b=NS, v=KVH)[:, :, :, v], cols)
                last = nc.vector.tensor_copy(
                    sT[0:NS, 1, :].rearrange("p (b g v) -> p b g v", b=NS, v=KVH)[:, :, :, v], own)
            last.then_inc(q["scc"], 1)
            dve.wait_ge(q["in"], 16 * (6 + 2 * NS))
            link(nc.vector.tensor_tensor(sinks[:, :], sinks[:, :], pick[:, :], ALU.mult))
            link(nc.vector.tensor_reduce(sink[:, :], sinks[:, :], AX, ALU.add))
            link(nc.vector.tensor_scalar(extra[:, P:P + NS], extra[:, P:P + NS], st[:, 7:8], None, ALU.add))
            dve.wait_ge(q["tr"], 1)
            link(nc.vector.scalar_tensor_tensor(out=s[:, :], in0=pb[0:R, 5, 0:P + NS], scalar=SC, in1=extra[:, :],
                                                op0=ALU.mult, op1=ALU.add))
            link(nc.vector.tensor_reduce(st[:, 0:1], s[:, :], AX, ALU.max))
            link(nc.vector.tensor_tensor(st[:, 1:2], st[:, 0:1], sink[:, :], ALU.max))
            nc.vector.tensor_scalar(st[:, 2:3], st[:, 1:2], -1.0, None, ALU.mult).then_inc(q["mx"], 1)
            dve.wait_ge(q["ex"], 1)
            link(nc.vector.tensor_tensor(st[:, 5:6], st[:, 3:4], st[:, 4:5], ALU.add))
            link(nc.vector.reciprocal(st[:, 6:7], st[:, 5:6]))
            nc.vector.tensor_scalar(p[:, :], p[:, :], st[:, 6:7], None, ALU.mult).then_inc(q["pr"], 1)
            dve.wait_ge(q["tr2"], 1)
            nc.vector.tensor_copy(pT[:, 0, :], pb[:, 6, 0:R])
            nc.vector.tensor_copy(pT[0:NS, 1, :], pb[0:NS, 6, R:2 * R]).then_inc(q["tr2c"], 1)


def shift_mix(nc, io, pr, mx, cumx, vec, const):
    with Memory(nc, "sm") as m:
        w2 = m.sb("decay_w2", [WL, DA])
        a2 = m.sb("iclr_a2", [WL + AL, DA])
        d = m.sb("diff", [P, 3, TT])
        wt = m.sb("tanh_w", [WL, TT])
        sq = m.sb("squares", [P, 2, TT])
        rk = m.sb("raw_kk", [P, 2, TT])
        reset = m.sb("chunk_reset", [P, TT])
        pb = m.psum("pb", [P, 8, 512])
        names = "in dd mixed lor z zs a as sq n2 nr chain chain2 dfree zr kkr tn pl msk".split()
        q = {k: m.sem(k) for k in names}
        cols = [(0, 344), (344, 344), (688, 344)]
        block = m.block()
        order = [12, 13] + list(range(4, 8)) + list(range(0, 4)) + list(range(8, 12))

        def height(c):
            return {12: WL + AL, 13: GL}.get(c, P)

        def difference(eng, i):
            c = order[i]
            hgt = height(c)
            o = d[0:hgt, (i // 2) % 2 if i % 2 == 0 else 2, :]
            eng.tensor_tensor(o[:, 0:T], pr[0:hgt, c, 0:T], pr[0:hgt, c, 1:1 + T], ALU.subtract)
            return eng.tensor_tensor(o[:, T:TT], pr[0:hgt, c, V0C:V0C + NS], pr[0:hgt, c, S0C:S0C + NS], ALU.subtract)

        def target(c):
            return pr[0:height(c), c, 0:TT] if c >= 12 else mx[:, c, :]

        @block.sync
        def _(sp):
            sp.dma_start(w2[:, :], io["decay_w2"][0]).then_inc(q["in"], 16)
            sp.dma_start(a2[WL:WL + AL, :], io["iclr_a2"][0]).then_inc(q["in"], 16)

        @block.gpsimd
        def _(pool):
            nc.gpsimd.memset(a2[0:WL, :], 0.0)
            nc.gpsimd.memset(reset[:, :], 1.0).then_inc(q["pl"], 1)
            pool.wait_ge(q["pl"], 1)
            nc.gpsimd.memset(reset[:, 0:T:CH], 0.0)
            nc.gpsimd.memset(reset[:, T:TT], 0.0).then_inc(q["pl"], 1)
            for i in range(0, len(order), 2):
                if i >= 4:
                    pool.wait_ge(q["mixed"], i - 3)
                difference(nc.gpsimd, i).then_inc(q["dd"], 1)

        @block.tensor
        def _(pe):
            pe.wait_ge(q["in"], 32)
            pe.wait_ge(q["pl"], 2)
            pe.wait_ge(q["lor"], 1)
            at = 0
            for t in range(4):
                for kind in range(2):
                    if at >= 2:
                        pe.wait_ge(q["zs"] if kind == 0 else q["as"], t)
                    for j, (t0, tn) in enumerate(cols):
                        bank = 3 * kind + j
                        if kind == 0:
                            last = nc.tensor.matmul(pb[:, bank, 0:tn], w2[:, P * t:P * t + P], wt[:, t0:t0 + tn],
                                                    start=True, stop=True)
                        else:
                            last = nc.tensor.matmul(pb[:, bank, 0:tn], a2[:, P * t:P * t + P],
                                                    pr[0:WL + AL, 12, t0:t0 + tn], start=True, stop=True)
                    last.then_inc(q["z"] if kind == 0 else q["a"], 1)
                    at += 1
            for t in range(4):
                pe.wait_ge(q["sq"], t + 1)
                if t >= 2:
                    pe.wait_ge(q["n2"], t - 1)
                elif t == 0:
                    pe.wait_ge(q["zs"], 4)
                    pe.wait_ge(q["as"], 4)
                for j, (t0, tn) in enumerate(cols):
                    last = nc.tensor.matmul(pb[:, 3 * (t % 2) + j, 0:tn], const["head_ones"][:, :], sq[:, t % 2, t0:t0 + tn],
                                            start=True, stop=True)
                last.then_inc(q["nr"], 1)

        @block.scalar
        def _(act):
            act.wait_ge(q["mixed"], 1)
            nc.scalar.activation(wt[:, :], pr[0:WL, 12, 0:TT], ACT.Tanh).then_inc(q["lor"], 1)
            act.wait_ge(q["mixed"], 2)
            nc.scalar.activation(pr[0:GL, 13, 0:TT], pr[0:GL, 13, 0:TT], ACT.Sigmoid)
            act.wait_ge(q["mixed"], 6)
            for t in range(4):
                act.wait_ge(q["z"], t + 1)
                for j, (t0, tn) in enumerate(cols):
                    last = nc.scalar.activation(cumx[:, t, t0:t0 + tn], pb[:, j, 0:tn], ACT.Sigmoid,
                                                bias=vec["decay_w0"][:, t:t + 1])
                last.then_inc(q["zs"], 1)
                act.wait_ge(q["a"], t + 1)
                for j, (t0, tn) in enumerate(cols):
                    last = nc.scalar.activation(pr[:, 4 + t, t0:t0 + tn], pb[:, 3 + j, 0:tn], ACT.Sigmoid,
                                                bias=vec["iclr_a0"][:, t:t + 1])
                last.then_inc(q["as"], 1)

            def square(t):
                act.wait_ge(q["kkr"], t + 1)
                if t >= 2:
                    act.wait_ge(q["chain2"], t - 1)
                nc.scalar.activation(sq[:, t % 2, :], rk[:, t % 2, :], ACT.Square).then_inc(q["sq"], 1)
            square(0)
            for t in range(4):
                if t == 0:
                    square(1)
                act.wait_ge(q["nr"], t + 1)
                for j, (t0, tn) in enumerate(cols):
                    last = nc.scalar.activation(sq[:, t % 2, t0:t0 + tn], pb[:, 3 * (t % 2) + j, 0:tn], ACT.Sqrt)
                last.then_inc(q["n2"], 1)
                if 1 <= t < 3:
                    square(t + 1)

        @block.vector
        def _(dve):
            link = Linked(dve, q["chain"])
            for i, c in enumerate(order):
                hgt = height(c)
                if i % 2:
                    if i > 1:
                        dve.wait_ge(q["mixed"], i - 1)
                    link(difference(nc.vector, i))
                    buf = 2
                else:
                    dve.wait_ge(q["dd"], i // 2 + 1)
                    buf = (i // 2) % 2
                ins = nc.vector.scalar_tensor_tensor(
                    out=target(c), in0=d[0:hgt, buf, :], scalar=vec["mu"][0:hgt, c:c + 1],
                    in1=pr[0:hgt, c, 1:1 + TT], op0=ALU.mult, op1=ALU.add)
                ins.then_inc(q["mixed"], 1)
            dve.wait_ge(q["mixed"], len(order))
            dve.wait_ge(q["pl"], 2)

            def raw_keys(t):
                nc.vector.tensor_scalar(rk[:, t % 2, :], mx[:, 4 + t, :], vec["k_k"][:, t:t + 1], None, ALU.mult)\
                    .then_inc(q["kkr"], 1)
            raw_keys(0)
            raw_keys(1)
            for t in range(4):
                dve.wait_ge(q["zs"], t + 1)
                link(nc.vector.tensor_scalar(cumx[:, t, :], cumx[:, t, :], -math.exp(-0.5), None, ALU.mult))
                link(nc.vector.tensor_tensor_scan(pr[:, 8 + t, 0:TT], reset[:, :], cumx[:, t, :], 0.0, ALU.mult, ALU.add))
                nc.vector.tensor_tensor(cumx[:, t, :], pr[:, 8 + t, 0:TT], cumx[:, t, :], ALU.subtract)
            for t in range(4):
                dve.wait_ge(q["n2"], t + 1)
                link(nc.vector.tensor_scalar(sq[:, t % 2, :], sq[:, t % 2, :], 1e-12, None, ALU.max))
                link(nc.vector.reciprocal(sq[:, t % 2, :], sq[:, t % 2, :]))
                link(nc.vector.scalar_tensor_tensor(out=pr[:, t, 0:TT], in0=rk[:, t % 2, :], scalar=-1.0,
                                                    in1=sq[:, t % 2, :], op0=ALU.mult, op1=ALU.mult))
                if t < 2:
                    raw_keys(t + 2)
                dve.wait_ge(q["as"], t + 1)
                link(nc.vector.tensor_scalar(sq[:, t % 2, :], pr[:, 4 + t, 0:TT], -1.0, vec["k_a"][:, t:t + 1],
                                             ALU.add, ALU.mult))
                link(nc.vector.scalar_tensor_tensor(out=mx[:, 4 + t, :], in0=sq[:, t % 2, :], scalar=1.0,
                                                    in1=mx[:, 4 + t, :], op0=ALU.add, op1=ALU.mult))
                nc.vector.scalar_tensor_tensor(out=pr[:, 4 + t, 0:TT], in0=pr[:, t, 0:TT], scalar=-1.0,
                                               in1=pr[:, 4 + t, 0:TT], op0=ALU.mult, op1=ALU.mult).then_inc(q["chain2"], 1)


def rwkv_sample(nc, io, pr, mx, const):
    with Memory(nc, "rs") as m:
        HR = HD // 2
        R = 2 * NS * HA
        S = m.sb("state", [R, HR, HD])
        S2 = m.sb("work", [R, HR, HD])
        vrow = m.sb("vectors", [NS, 6, DA])
        vb = m.sb("vectors_by_head", [R, 5, HD])
        vv = m.sb("values", [R, HR])
        sa = m.sb("sa", [R, HR])
        y = m.sb("y", [R, HR])
        yr = m.sb("y_rows", [NS, DA])
        decay = m.sb("decay", [P, 4, NS])
        pb = m.psum("pb", [P, 8, 512])
        names = "st tr cp vw vr chain out y yd ydr ytr yc pre".split()
        q = {k: m.sem(k) for k in names}
        scr, yscr = io["sample_scratch"], io["sample_y"]
        block = m.block()
        def col(j, t):
            return [pr[:, t, T:TT], pr[:, 4 + t, T:TT], mx[:, 4 + t, T:TT], mx[:, t, T:TT], decay[:, t, :],
                    mx[:, 8 + t, T:TT]][j]

        @block.sync
        def _(sp):
            for half in range(2):
                sp.dma_start(S[64 * half:64 * half + 64, :, :],
                             io["state_rwkv"][0, :, :, HR * half:HR * half + HR, :].rearrange("b h i j -> (b h) i j"))\
                    .then_inc(q["st"], 16)
            sp.wait_ge(q["cp"], 6)
            sp.dma_start(scr.rearrange("v b c -> b v c"), vrow[:, :, :]).then_inc(q["vw"], 16)
            sp.wait_ge(q["vw"], 16)
            for half in range(2):
                sp.dma_start(vb[64 * half:64 * half + 64, :, :],
                             scr[0:5].rearrange("v b (h j) -> (b h) v j", h=HA)).then_inc(q["vr"], 16)
                sp.dma_start(vv[64 * half:64 * half + 64, :],
                             scr[5].rearrange("b (h i) -> (b h) i", h=HA)[:, HR * half:HR * half + HR]).then_inc(q["vr"], 16)
            sp.wait_ge(q["y"], 1)
            for half in range(2):
                sp.dma_start(yscr.rearrange("b (h i) -> (b h) i", h=HA)[:, HR * half:HR * half + HR],
                             y[64 * half:64 * half + 64, :]).then_inc(q["yd"], 16)
                sp.dma_start(io["o_rwkv_sample"][0, :, :, HR * half:HR * half + HR, :].rearrange("b h i j -> (b h) i j"),
                             S[64 * half:64 * half + 64, :, :]).then_inc(q["out"], 16)
            sp.wait_ge(q["yd"], 32)
            sp.dma_start(yr[:, :], yscr).then_inc(q["ydr"], 16)
            sp.wait_ge(q["out"], 32)

        @block.tensor
        def _(pe):
            pe.wait_ge(q["pre"], 1)
            for j in range(6):
                for t in range(4):
                    last = nc.tensor.transpose(pb[0:NS, j, P * t:P * t + P], col(j, t), const["ident"][:, :])
                last.then_inc(q["tr"], 1)
            pe.wait_ge(q["ydr"], 16)
            for t in range(4):
                last = nc.tensor.transpose(pb[:, 6, NS * t:NS * t + NS], yr[:, P * t:P * t + P], const["ident"][0:NS, 0:NS])
            last.then_inc(q["ytr"], 1)

        @block.scalar
        def _(act):
            nc.scalar.activation(decay[:, :, :], pr[:, 8:12, T:TT], ACT.Exp).then_inc(q["pre"], 1)
            for j in range(6):
                act.wait_ge(q["tr"], j + 1)
                nc.scalar.copy(vrow[:, j, :], pb[0:NS, j, :]).then_inc(q["cp"], 1)
            act.wait_ge(q["ytr"], 1)
            nc.scalar.copy(pr[:, 0:4, T:TT], pb[:, 6, 0:4 * NS].rearrange("p (t b) -> p t b", t=4)).then_inc(q["yc"], 1)

        @block.vector
        def _(dve):
            link = Linked(dve, q["chain"])
            dve.wait_ge(q["st"], 32)
            dve.wait_ge(q["vr"], 64)

            def over_i(j):
                return vb[:, j, :].unsqueeze(1).to_broadcast([R, HR, HD])

            def over_j(a):
                return a.unsqueeze(2).to_broadcast([R, HR, HD])

            link(nc.vector.tensor_tensor(S2[:, :, :], S[:, :, :], over_i(0), ALU.mult))
            link(nc.vector.tensor_reduce(sa[:, :], S2[:, :, :], AX, ALU.add))
            link(nc.vector.tensor_tensor(S[:, :, :], S[:, :, :], over_i(4), ALU.mult))
            link(nc.vector.tensor_tensor(S2[:, :, :], over_j(sa[:, :]), over_i(1), ALU.mult))
            link(nc.vector.tensor_tensor(S[:, :, :], S[:, :, :], S2[:, :, :], ALU.add))
            link(nc.vector.tensor_tensor(S2[:, :, :], over_j(vv[:, :]), over_i(2), ALU.mult))
            link(nc.vector.tensor_tensor(S[:, :, :], S[:, :, :], S2[:, :, :], ALU.add))
            link(nc.vector.tensor_tensor(S2[:, :, :], S[:, :, :], over_i(3), ALU.mult))
            nc.vector.tensor_reduce(y[:, :], S2[:, :, :], AX, ALU.add).then_inc(q["y"], 1)


def rwkv_chunks(nc, io, pr, mx, cumx, const):
    with Memory(nc, "rc") as m:
        ends = m.sb("decay_at_ends", [P, 4, 2 * NT])
        inv = m.sb("inverse_decay", [P, 4, P])
        kt = m.sb("k_scaled", [P, 4, P])
        bh = m.sb("b_to_end", [P, 4, P])
        kh = m.sb("k_to_end", [P, 4, P])
        tok = m.sb("token_rows", [P, 4, DA])
        Lm = m.sb("L", [P, 2, 4, P])
        MT = m.sb("MT", [P, 2, 4, P])
        X = m.sb("X", [P, 2, 4, P])
        XT = m.sb("XT", [P, 2, 4, P])
        Z = m.sb("Z", [P, 2, 4, P])
        RT = m.sb("RBT_RKT", [P, 2, 2, 4, P])
        MV = m.sb("MV", [P, DA])
        U = m.sb("U", [P, DA])
        Uv = m.sb("Uv", [P, DA])
        WT = m.sb("WT", [P, 4, P])
        ST = m.sb("ST", [P, 2, 4, HD])
        SD = m.sb("ST_decayed", [P, 4, HD])
        So = MV[0:HD, :].rearrange("p (h j) -> p h j", h=HA)
        pb = m.psum("pb", [P, 8, 512])
        names = ("ex ft hat tr tc l lc m mc rr rrc x0 xt0 xt0c z zc x xe xt xc mv mvc wt wtc uv uvc sd u uc s sc y yc chain"
                 " start so soc out").split()
        q = {k: m.sem(k) for k in names}
        block = m.block()
        NLEV = 5
        ident = const["ident"]

        def hcol(par, t):
            return HD * (2 * t + par)

        def fr(par):
            return slice(64 * par, 64 * par + 64)

        def tile_cols(n):
            return slice(P * n, P * n + P)

        def mats(k):
            return pb[:, k, :].rearrange("p (t s) -> p t s", t=4)

        @block.scalar
        def _(act):
            def exps(n):
                c = tile_cols(n)
                if n:
                    act.wait_ge(q["ft"], 2 * n)
                nc.scalar.activation(inv[:, :, :], pr[:, 8:12, c], ACT.Exp, scale=-1.0).then_inc(q["ex"], 1)
                nc.scalar.activation(cumx[:, :, c], cumx[:, :, c], ACT.Exp)
                act.wait_ge(q["ex"], 2 * n + 2)
                nc.scalar.activation(pr[:, 8:12, c], pr[:, 8:12, c], ACT.Exp).then_inc(q["ex"], 1)

            def take_y(n):
                act.wait_ge(q["y"], n + 1)
                nc.scalar.copy(pr[:, 0:4, tile_cols(n)], mats(3)).then_inc(q["yc"], 1)

            def take_rows(n, j):
                act.wait_ge(q["tr"], 4 * n + j + 1)
                nc.scalar.copy(tok[:, j, :], pb[:, 2 + j % 2, :]).then_inc(q["tc"], 1)

            nc.scalar.activation(ends[:, :, :], pr[:, 8:12, CH - 1:T:CH], ACT.Exp).then_inc(q["ex"], 1)
            exps(0)
            for n in range(NT):
                for par in range(2):
                    act.wait_ge(q["xt0"], 2 * n + par + 1)
                    nc.scalar.copy(XT[:, par, :, :], mats(4 + par)).then_inc(q["xt0c"], 1)
                if n:
                    take_y(n - 1)
                if n + 1 < NT:
                    exps(n + 1)
                for lev in range(NLEV - 1):
                    if lev in (1, 2):
                        take_rows(n, 2 * lev - 2)
                        take_rows(n, 2 * lev - 1)
                    if lev == 3:
                        act.wait_ge(q["mv"], n + 1)
                        nc.scalar.copy(MV[:, :], pb[:, 2, :]).then_inc(q["mvc"], 1)
                    for par in range(2):
                        act.wait_ge(q["xt"], 2 * ((NLEV - 1) * n + lev) + par + 1)
                        nc.scalar.copy(X[:, par, :, :], mats(par)).then_inc(q["xc"], 1)
                act.wait_ge(q["wt"], n + 1)
                nc.scalar.copy(WT[:, :, :], mats(3)).then_inc(q["wtc"], 1)
                act.wait_ge(q["uv"], n + 1)
                nc.scalar.copy(Uv[:, :], pb[:, 2, :]).then_inc(q["uvc"], 1)
            take_y(NT - 1)
            act.wait_ge(q["so"], 1)
            nc.scalar.copy(So, pb[0:HD, 0, :].rearrange("p (h j) -> p h j", h=HA)).then_inc(q["soc"], 1)

        @block.gpsimd
        def _(pool):
            tt = nc.gpsimd.tensor_tensor

            def scaled(n):
                c = tile_cols(n)
                pool.wait_ge(q["ex"], 2 * n + 3)
                tt(cumx[:, :, c], pr[:, 0:4, c], cumx[:, :, c], ALU.mult)
                tt(pr[:, 4:8, c], pr[:, 4:8, c], inv[:, :, :], ALU.mult).then_inc(q["ft"], 1)
                if n:
                    pool.wait_ge(q["tr"], 4 * n - 2)
                    pool.wait_ge(q["hat"], n)
                tt(kt[:, :, :], mx[:, 4:8, c], inv[:, :, :], ALU.mult)
                tt(pr[:, 8:12, c], mx[:, 0:4, c], pr[:, 8:12, c], ALU.mult).then_inc(q["ft"], 1)
                pool.wait_ge(q["ft"], 2 * n + 2)
                for dst, src in ((bh[:, :, :], pr[:, 4:8, c]), (kh[:, :, :], kt[:, :, :])):
                    for ch in range(2):
                        cc = slice(CH * ch, CH * ch + CH)
                        end = ends[:, :, 2 * n + ch:2 * n + ch + 1].to_broadcast([P, 4, CH])
                        last = tt(dst[:, :, cc], src[:, :, cc], end, ALU.mult)
                last.then_inc(q["hat"], 1)

            for z in (ST[:, 0, :, :], Lm[:, :, :, :], MT[:, :, :, :], RT[:, :, :, :, :]):
                nc.gpsimd.memset(z, 0.0).then_inc(q["start"], 1)
            scaled(0)
            for n in range(NT):
                pool.wait_ge(q["lc"], 4 * n + 4)
                for i, (src, name, op) in enumerate(((Lm, "lev0", ALU.mult), (X, "ident", ALU.add))):
                    if i:
                        pool.wait_ge(q["chain"], n + 1)
                    tt(X[:, :, :, :].rearrange("p a t s -> p (a t) s"), src[:, :, :, :].rearrange("p a t s -> p (a t) s"),
                       const[name][:, :].unsqueeze(1).to_broadcast([P, 8, P]), op).then_inc(q[("chain", "x0")[i]], 1)
                if n + 1 < NT:
                    scaled(n + 1)

        @block.tensor
        def _(pe):
            mm = nc.tensor.matmul

            def masked(bank, at, lhs, rhs):
                for ch in range(2):
                    cc = slice(CH * ch, CH * ch + CH)
                    for t in range(4):
                        for par in range(2):
                            last = mm(pb[cc, bank + par, at + CH * t:at + CH * t + CH], lhs(t, cc)[fr(par)],
                                      rhs(t, cc)[fr(par)], start=True, stop=True)
                return last

            def state_terms(n, ch):
                g = 2 * n + ch
                cur = g % 2
                tr = slice(CH * ch, CH * ch + CH)
                c = slice(P * n + CH * ch, P * n + CH * ch + CH)
                if ch == 0:
                    pe.wait_ge(q["wtc"], n + 1)
                if g:
                    pe.wait_ge(q["sc"], g)
                for t in range(4):
                    for par in range(2):
                        last = mm(pb[tr, par, HD * t:HD * t + HD], WT[fr(par), t, tr], ST[fr(par), cur, t, :],
                                  start=True, stop=True)
                last.then_inc(q["u"], 1)
                if ch == 0:
                    pe.wait_ge(q["uvc"], n + 1)
                for t in range(4):
                    for par in range(2):
                        last = mm(pb[fr(par), 3, P * t + CH * ch:P * t + CH * ch + CH], ST[fr(par), cur, t, :],
                                  pr[fr(par), 8 + t, c], start=(ch == 0 and t == 0), stop=False)
                for t in range(4):
                    for par in range(2):
                        hc = hcol(par, t)
                        last = mm(pb[fr(par), 2, HD * t:HD * t + HD], tok[tr, 1, hc:hc + HD], tok[tr, 3, hc:hc + HD],
                                  start=(t == 0), stop=False)

            def state_update(n, ch):
                tr = slice(CH * ch, CH * ch + CH)
                pe.wait_ge(q["uc"], 2 * n + ch + 1)
                for t in range(4):
                    for par in range(2):
                        hc = hcol(par, t)
                        last = mm(pb[fr(par), 2, HD * t:HD * t + HD], tok[tr, 0, hc:hc + HD], U[tr, hc:hc + HD],
                                  start=False, stop=(t == 3))
                last.then_inc(q["s"], 1)

            def output(n):
                for t in range(4):
                    for par in range(2):
                        hc = hcol(par, t)
                        o = pb[fr(par), 3, P * t:P * t + P]
                        mm(o, U[:, hc:hc + HD], RT[:, par, 0, t, :], start=False, stop=False)
                        last = mm(o, tok[:, 3, hc:hc + HD], RT[:, par, 1, t, :], start=False, stop=(t == 3))
                last.then_inc(q["y"], 1)

            def token_rows(n, j):
                src = (bh[:, :, :], kh[:, :, :], cumx[:, :, tile_cols(n)], mx[:, 8:12, tile_cols(n)])[j]
                if j < 2:
                    pe.wait_ge(q["rrc"], 4 * n + 4)
                    pe.wait_ge(q["hat"], n + 1)
                else:
                    pe.wait_ge(q["tc"], 4 * n + j - 1)
                for t in range(4):
                    last = nc.tensor.transpose(pb[:, 2 + j % 2, P * t:P * t + P], src[:, t, :], ident[:, :])
                last.then_inc(q["tr"], 1)

            pe.wait_ge(q["start"], 4)
            for n in range(NT + 1):
                c0 = P * n

                def at(a, k0):
                    return lambda t, cc: a[:, k0 + t, c0 + cc.start:c0 + cc.stop]
                a_, b_, r_ = at(cumx, 0), at(pr, 4), at(pr, 8)

                def k_(t, cc):
                    return kt[:, t, cc]
                if n < NT:
                    pe.wait_ge(q["ft"], 2 * n + 1)
                    if n:
                        pe.wait_ge(q["xe"], 2 * NLEV * n)
                    masked(4, 0, a_, b_).then_inc(q["l"], 1)
                if n:
                    state_terms(n - 1, 0)
                if n < NT:
                    pe.wait_ge(q["ft"], 2 * n + 2)
                    masked(6, 0, k_, a_).then_inc(q["m"], 1)
                if n:
                    state_update(n - 1, 0)
                if n < NT:
                    pe.wait_ge(q["x0"], n + 1)
                    for par in range(2):
                        for t in range(4):
                            last = nc.tensor.transpose(pb[:, 4 + par, P * t:P * t + P], X[:, par, t, :], ident[:, :])
                        last.then_inc(q["xt0"], 1)
                if n:
                    state_terms(n - 1, 1)
                    state_update(n - 1, 1)
                    output(n - 1)
                if n == NT:
                    break
                for lev in range(NLEV):
                    g = NLEV * n + lev
                    for par in range(2):
                        if lev:
                            pe.wait_ge(q["xe"], 2 * (g - 1) + par + 1)
                        else:
                            pe.wait_ge(q["xt0c"], 2 * n + par + 1)
                            pe.wait_ge(q["mc"], 4 * n + 4)
                        for t in range(4):
                            last = mm(pb[:, 6 + par, P * t:P * t + P], Lm[:, par, t, :], XT[:, par, t, :],
                                      start=True, stop=True)
                        last.then_inc(q["z"], 1)
                    if lev == 0:
                        if n:
                            pe.wait_ge(q["sc"], 2 * n)
                            pe.wait_ge(q["yc"], n)
                        masked(2, 0, b_, r_)
                        masked(2, 256, k_, r_).then_inc(q["rr"], 1)
                    elif lev < 3:
                        token_rows(n, 2 * lev - 2)
                    elif lev == 3:
                        pe.wait_ge(q["tc"], 4 * n + 4)
                        for h in range(HA):
                            last = mm(pb[:, 2, HD * h:HD * h + HD], MT[:, h % 2, h // 2, :], tok[:, 3, HD * h:HD * h + HD],
                                      start=True, stop=True)
                        last.then_inc(q["mv"], 1)
                    for par in range(2):
                        pe.wait_ge(q["zc"], 2 * g + par + 1)
                        if lev:
                            pe.wait_ge(q["xc"], 2 * ((NLEV - 1) * n + lev - 1) + par + 1)
                        for t in range(4):
                            last = mm(pb[:, 4 + par, P * t:P * t + P], X[:, par, t, :], Z[:, par, t, :],
                                      start=True, stop=True)
                        last.then_inc(q["x"], 1)
                    if lev in (1, 2):
                        token_rows(n, 2 * lev - 1)
                    if lev < NLEV - 1:
                        for par in range(2):
                            pe.wait_ge(q["xe"], 2 * g + par + 1)
                            for t in range(4):
                                last = nc.tensor.transpose(pb[:, par, P * t:P * t + P], XT[:, par, t, :], ident[:, :])
                            last.then_inc(q["xt"], 1)
                pe.wait_ge(q["xe"], 2 * NLEV * (n + 1))
                for t in range(4):
                    for par in range(2):
                        last = mm(pb[fr(par), 3, P * t:P * t + P], tok[:, 2, hcol(par, t):hcol(par, t) + HD],
                                  XT[:, par, t, :], start=True, stop=True)
                last.then_inc(q["wt"], 1)
                pe.wait_ge(q["mvc"], n + 1)
                for h in range(HA):
                    last = mm(pb[:, 2, HD * h:HD * h + HD], XT[:, h % 2, h // 2, :], MV[:, HD * h:HD * h + HD],
                              start=True, stop=True)
                last.then_inc(q["uv"], 1)
            pe.wait_ge(q["sc"], 2 * NT)
            for t in range(4):
                last = nc.tensor.transpose(pb[0:HD, 0, P * t:P * t + P], ST[:, 0, t, :], ident[:, :])
            last.then_inc(q["so"], 1)

        @block.vector
        def _(dve):
            tt = nc.vector.tensor_tensor

            def take_masked(n, k, name, par, ch):
                cc = slice(CH * ch, CH * ch + CH)
                dst, bank, kinds, mask = {"l": (Lm, 4, 4, "low"), "m": (MT, 6, 4, "up"), "rr": (RT, 2, 8, "up_incl")}[name]
                out = dst[cc, par] if name != "rr" else dst[cc, par].rearrange("p k t s -> p (k t) s")
                tt(out[:, :, cc], pb[cc, bank + par, 0:CH * kinds].rearrange("p (t s) -> p t s", t=kinds),
                   const[mask][cc, cc].unsqueeze(1).to_broadcast([CH, kinds, CH]), ALU.mult).then_inc(q[name + "c"], 1)

            def take_all(n, name):
                dve.wait_ge(q[name], n + 1)
                for par in range(2):
                    for ch in range(2):
                        take_masked(n, 0, name, par, ch)

            def decay_state(g):
                if g:
                    dve.wait_ge(q["sc"], g)
                tt(SD[:, :, :], ST[:, g % 2, :, :], ends[:, :, g:g + 1].to_broadcast([P, 4, HD]), ALU.mult)\
                    .then_inc(q["sd"], 1)

            def take_u(n, ch):
                rr = slice(CH * ch, CH * ch + CH)
                dve.wait_ge(q["u"], 2 * n + ch + 1)
                if ch == 0:
                    dve.wait_ge(q["uvc"], n + 1)
                for par in range(2):
                    uu = U[rr, :].rearrange("p (t a d) -> p t a d", a=2, d=HD)[:, :, par, :]
                    vv = Uv[rr, :].rearrange("p (t a d) -> p t a d", a=2, d=HD)[:, :, par, :]
                    last = tt(uu, pb[rr, par, 0:256].rearrange("p (t d) -> p t d", t=4), vv, ALU.add)
                last.then_inc(q["uc"], 1)

            def take_state(n, ch):
                g = 2 * n + ch
                dve.wait_ge(q["s"], g + 1)
                dve.wait_ge(q["sd"], g + 1)
                tt(ST[:, 1 - g % 2, :, :], pb[:, 2, 0:256].rearrange("p (t d) -> p t d", t=4), SD[:, :, :], ALU.add)\
                    .then_inc(q["sc"], 1)

            dve.wait_ge(q["start"], 4)
            dve.wait_ge(q["ex"], 1)
            decay_state(0)
            for n in range(NT + 1):
                if n < NT:
                    take_all(n, "l")
                if n:
                    take_u(n - 1, 0)
                if n < NT:
                    take_all(n, "m")
                if n:
                    take_state(n - 1, 0)
                    decay_state(2 * n - 1)
                    take_u(n - 1, 1)
                    take_state(n - 1, 1)
                if n == NT:
                    break
                if n:
                    decay_state(2 * n)
                for lev in range(NLEV):
                    g = NLEV * n + lev
                    for par in range(2):
                        dve.wait_ge(q["z"], 2 * g + par + 1)
                        tt(Z[:, par, :, :], mats(6 + par), const[f"lev{lev + 1}T"][:, :].unsqueeze(1).to_broadcast([P, 4, P]),
                           ALU.mult).then_inc(q["zc"], 1)
                    for par in range(2):
                        dve.wait_ge(q["x"], 2 * g + par + 1)
                        tt(XT[:, par, :, :], XT[:, par, :, :], mats(4 + par), ALU.add).then_inc(q["xe"], 1)
                    if lev == 0:
                        take_all(n, "rr")

        @block.sync
        def _(sp):
            sp.wait_ge(q["soc"], 1)
            sp.dma_start(io["o_rwkv_prompt"][0, 0].rearrange("h i j -> i h j"), So).then_inc(q["out"], 16)
            sp.wait_ge(q["out"], 16)


def rwkv_norm(nc, io, pr, mx, vec, const):
    with Memory(nc, "rn") as m:
        g2 = m.sb("gate_w2", [GL, DA])
        sq = m.sb("squares", [P, 2, TT])
        bb = m.sb("bonus", [P, 2, TT])
        gate = m.sb("gate", [P, 2, TT])
        pb = m.psum("pb", [P, 8, 512])
        cols = [(0, 344), (344, 344), (688, 344)]
        names = "in mu d sq var rs rkk bo bv gt gc done chain eps".split()
        q = {k: m.sem(k) for k in names}
        block = m.block()

        @block.sync
        def _(sp):
            sp.dma_start(g2[:, :], io["gate_w2"][0]).then_inc(q["in"], 16)

        @block.tensor
        def _(pe):
            def product(b0, lhs, rhs):
                for j, (t0, tn) in enumerate(cols):
                    last = nc.tensor.matmul(pb[:, b0 + j, 0:tn], lhs, rhs[:, t0:t0 + tn], start=True, stop=True)
                return last
            pe.wait_ge(q["in"], 16)
            ones = const["head_ones"][:, :]
            product(0, ones, pr[:, 0, 0:TT]).then_inc(q["mu"], 1)
            for t in range(4):
                pe.wait_ge(q["rkk"], t + 1)
                pe.wait_ge(q["d"], t + 1)
                product(0, ones, bb[:, t % 2, :]).then_inc(q["bo"], 1)
                pe.wait_ge(q["sq"], t + 1)
                if t:
                    pe.wait_ge(q["gc"], t)
                product(3, ones, sq[:, t % 2, :]).then_inc(q["var"], 1)
                if t < 3:
                    pe.wait_ge(q["bv"], t + 1)
                    product(0, ones, pr[:, t + 1, 0:TT]).then_inc(q["mu"], 1)
                pe.wait_ge(q["rs"], t + 1)
                product(3, g2[:, P * t:P * t + P], pr[0:GL, 13, 0:TT]).then_inc(q["gt"], 1)

        @block.gpsimd
        def _(pool):
            nc.gpsimd.memset(const["lnx_eps"][:, :], LNX_EPS).then_inc(q["eps"], 1)
            for t in range(4):
                if t >= 2:
                    pool.wait_ge(q["done"], t - 1)
                nc.gpsimd.tensor_tensor(bb[:, t % 2, :], mx[:, t, :], mx[:, 4 + t, :], ALU.mult).then_inc(q["chain"], 1)
                pool.wait_ge(q["chain"], t + 1)
                nc.gpsimd.tensor_scalar(bb[:, t % 2, :], bb[:, t % 2, :], vec["r_k"][:, t:t + 1], None, ALU.mult)\
                    .then_inc(q["rkk"], 1)

        @block.scalar
        def _(act):
            act.wait_ge(q["eps"], 1)

            def square(t):
                act.wait_ge(q["d"], t + 1)
                if t >= 2:
                    act.wait_ge(q["done"], t - 1)
                nc.scalar.activation(sq[:, t % 2, :], pr[:, t, 0:TT], ACT.Square).then_inc(q["sq"], 1)
            square(0)
            for t in range(4):
                act.wait_ge(q["var"], t + 1)
                for j, (t0, tn) in enumerate(cols):
                    last = nc.scalar.activation(sq[:, t % 2, t0:t0 + tn], pb[:, 3 + j, 0:tn], ACT.Sqrt,
                                                scale=1.0 / HD, bias=const["lnx_eps"][:, :])
                last.then_inc(q["rs"], 1)
                if t < 3:
                    square(t + 1)
                act.wait_ge(q["gt"], t + 1)
                if t >= 2:
                    act.wait_ge(q["done"], t - 1)
                for j, (t0, tn) in enumerate(cols):
                    last = nc.scalar.copy(gate[:, t % 2, t0:t0 + tn], pb[:, 3 + j, 0:tn])
                last.then_inc(q["gc"], 1)

        @block.vector
        def _(dve):
            link = Linked(dve, m.sem("chain2"))
            stt, tt = nc.vector.scalar_tensor_tensor, nc.vector.tensor_tensor

            def centre(t):
                y = pr[:, t, :]
                dve.wait_ge(q["mu"], t + 1)
                for j, (t0, tn) in enumerate(cols):
                    last = stt(out=y[:, t0:t0 + tn], in0=pb[:, j, 0:tn], scalar=-1.0 / HD, in1=y[:, t0:t0 + tn],
                               op0=ALU.mult, op1=ALU.add)
                last.then_inc(q["d"], 1)

            def bonus(t):
                dve.wait_ge(q["bo"], t + 1)
                for j, (t0, tn) in enumerate(cols):
                    last = tt(bb[:, t % 2, t0:t0 + tn], pb[:, j, 0:tn], mx[:, 8 + t, t0:t0 + tn], ALU.mult)
                last.then_inc(q["bv"], 1)

            centre(0)
            for t in range(4):
                y = pr[:, t, :]
                bonus(t)
                if t < 3:
                    centre(t + 1)
                dve.wait_ge(q["rs"], t + 1)
                link(nc.vector.reciprocal(sq[:, t % 2, :], sq[:, t % 2, :]))
                link(tt(y[:, 0:TT], y[:, 0:TT], sq[:, t % 2, :], ALU.mult))
                link(nc.vector.tensor_scalar(y[:, 0:TT], y[:, 0:TT], vec["lnx_g"][:, t:t + 1], vec["lnx_b"][:, t:t + 1],
                                             ALU.mult, ALU.add))
                dve.wait_ge(q["bv"], t + 1)
                link(tt(y[:, 0:TT], y[:, 0:TT], bb[:, t % 2, :], ALU.add))
                dve.wait_ge(q["gc"], t + 1)
                tt(y[:, 0:TT], y[:, 0:TT], gate[:, t % 2, :], ALU.mult).then_inc(q["done"], 1)


def pool_features(nc, io, xr, feats, const):
    PAD = 16
    with Memory(nc, "pf") as m:
        xT = m.sb("xT", [P, KD, PAD + TT])
        a = m.sb("sums_a", [P, 2, PAD + T])
        b = m.sb("sums_b", [P, 2, PAD + T])
        hist = m.sb("history", [NS * KEEP, D])
        hT = m.sb("historyT", [P, KD, NS * KEEP])
        hs = m.sb("history_sums", [P, 2, NS])
        inv = m.sb("inverse_counts", [P, 4, 16])
        pb = m.psum("pb", [P, 8, 512])
        q = {k: m.sem(k) for k in "in tr cpa cpv pad chain out".split()}
        block = m.block()

        @block.sync
        def _(sp):
            sp.dma_start(hist[:, :], io["state_pool"][0].rearrange("b t d -> (b t) d")).then_inc(q["in"], 16)
            sp.dma_start(inv[:, :, :], io["c_invcnt"].rearrange("p (g t) -> p g t", g=4)).then_inc(q["in"], 16)
            sp.dma_start(io["o_pool_prompt"][0, 0], xr[P - KEEP:P, NT - 1, :]).then_inc(q["out"], 16)
            sp.dma_start(io["o_pool_sample"][0, :, 0:KEEP - 1, :], io["state_pool"][0, :, 1:KEEP, :]).then_inc(q["out"], 16)
            sp.dma_start(io["o_pool_sample"][0, :, KEEP - 1, :], xr[0:NS, NT, :]).then_inc(q["out"], 16)
            sp.wait_ge(q["out"], 48)

        @block.tensor
        def _(pe):
            for i in range(TILES + 1):
                if i >= 4:
                    pe.wait_ge(q["cpa"], i - 3)
                    pe.wait_ge(q["cpv"], i - 3)
                if i == TILES:
                    pe.wait_ge(q["in"], 32)
                n = NS * KEEP if i == TILES else rows(i)
                for k in range(KD):
                    src = hist[:, P * k:P * k + P] if i == TILES else xr[0:n, i, P * k:P * k + P]
                    last = nc.tensor.transpose(pb[:, 2 * (i % 4) + k // 4, P * (k % 4):P * (k % 4) + n], src,
                                               const["ident"][0:n, 0:n])
                last.then_inc(q["tr"], 1)

        def copy_out(eng, copy, half, sem):
            for i in range(TILES + 1):
                n = NS * KEEP if i == TILES else rows(i)
                eng.wait_ge(q["tr"], i + 1)
                src = pb[:, 2 * (i % 4) + half, :].rearrange("p (k t) -> p k t", k=4)[:, :, 0:n]
                ks = slice(4 * half, 4 * half + 4)
                dst = hT[:, ks, :] if i == TILES else xT[:, ks, PAD + P * i:PAD + P * i + n]
                copy(dst, src).then_inc(q[sem], 1)

        @block.scalar
        def _(act):
            copy_out(act, nc.scalar.copy, 0, "cpa")

        @block.gpsimd
        def _(pool):
            nc.gpsimd.memset(xT[:, :, 0:PAD], 0.0).then_inc(q["pad"], 1)
            nc.gpsimd.memset(a[:, :, 0:PAD], 0.0)
            nc.gpsimd.memset(b[:, :, 0:PAD], 0.0).then_inc(q["pad"], 1)

        @block.vector
        def _(dve):
            link = Linked(dve, q["chain"])
            copy_out(dve, nc.vector.tensor_copy, 1, "cpv")
            dve.wait_ge(q["cpa"], TILES + 1)
            dve.wait_ge(q["cpv"], TILES + 1)
            dve.wait_ge(q["pad"], 2)
            dve.wait_ge(q["in"], 32)
            for g, w in enumerate(POOLW):
                ks = slice(2 * g, 2 * g + 2)
                x = xT[:, ks, 0:PAD + T]
                src, step = x, 1
                for lev in range(g + 1):
                    dst = (a, b)[lev % 2][:, :, :]
                    link(nc.vector.tensor_tensor(dst[:, :, PAD:], src[:, :, PAD:], src[:, :, PAD - step:PAD + T - step],
                                                 ALU.add))
                    src, step = dst, 2 * step
                link(nc.vector.scalar_tensor_tensor(out=feats[:, ks, 0:T], in0=src[:, :, PAD:], scalar=1.0 / w,
                                                    in1=x[:, :, PAD:], op0=ALU.mult, op1=ALU.subtract))
                link(nc.vector.tensor_tensor(feats[:, ks, 0:16], src[:, :, PAD:PAD + 16],
                                             inv[:, g:g + 1, :].to_broadcast([P, 2, 16]), ALU.mult))
                link(nc.vector.tensor_tensor(feats[:, ks, 0:16], feats[:, ks, 0:16], x[:, :, PAD:PAD + 16], ALU.subtract))
                h = hT[:, ks, :].rearrange("p k (b t) -> p k b t", b=NS)[:, :, :, KEEP - (w - 1):KEEP]
                xs = xT[:, ks, PAD + T:PAD + TT]
                link(nc.vector.tensor_reduce(hs[:, :, :], h, AX, ALU.add))
                link(nc.vector.tensor_tensor(hs[:, :, :], hs[:, :, :], xs, ALU.add))
                link(nc.vector.scalar_tensor_tensor(out=feats[:, ks, T:TT], in0=hs[:, :, :], scalar=1.0 / w,
                                                    in1=xs, op0=ALU.mult, op1=ALU.subtract))


def norm_vector(nc, dve, q, i, xr, st, g, gain_after=1):
    n, s, x = rows(i), st[:, i % 2, :], xr[0:rows(i), i, :]
    dve.wait_ge(q["res"], i + 1)
    if i >= 2:
        dve.wait_ge(q["n"], i - 1)
    for h in range(2):
        last = nc.vector.bn_stats(s[0:n, 6 * h:6 * h + 6], x[:, 512 * h:512 * h + 512])
    last.then_inc(q["st"], 1)
    dve.wait_ge(q["st"], i + 1)
    nc.vector.bn_aggr(s[0:n, 12:14], s[0:n, 0:12]).then_inc(q["var"], 1)
    if i and gain_after:
        norm_gain(nc, dve, q, i - 1, xr, g)
    dve.wait_ge(q["root"], i + 1)
    nc.vector.reciprocal(s[0:n, 15:16], s[0:n, 14:15]).then_inc(q["rs"], 1)
    dve.wait_ge(q["rs"], i + 1)
    nc.vector.scalar_tensor_tensor(out=s[0:n, 16:17], in0=s[0:n, 12:13], scalar=-1.0, in1=s[0:n, 15:16],
                                   op0=ALU.mult, op1=ALU.mult).then_inc(q["nm"], 1)
    if not gain_after:
        norm_gain(nc, dve, q, i, xr, g)


def norm_gain(nc, dve, q, i, xr, g):
    n = rows(i)
    dve.wait_ge(q["n"], i + 1)
    nc.vector.tensor_tensor(xr[0:n, i, :], xr[0:n, i, :], g[0:n, :], ALU.mult).then_inc(q["g"], 1)


def norm_scalar(nc, act, q, i, xr, st, eps):
    n, s = rows(i), st[:, i % 2, :]
    act.wait_ge(q["var"], i + 1)
    nc.scalar.activation(s[0:n, 14:15], s[0:n, 13:14], ACT.Sqrt, bias=eps[0:n, :]).then_inc(q["root"], 1)
    act.wait_ge(q["nm"], i + 1)
    nc.scalar.activation(xr[0:n, i, :], xr[0:n, i, :], ACT.Identity, bias=s[0:n, 16:17], scale=s[0:n, 15:16])\
        .then_inc(q["n"], 1)


def norm_shift(nc, pool, q, i, xr, b):
    n = rows(i)
    pool.wait_ge(q["g"], i + 1)
    nc.gpsimd.tensor_tensor(xr[0:n, i, :], xr[0:n, i, :], b[0:n, :], ALU.add).then_inc(q["x"], 1)


def mix_out(nc, io, layer, lhs, xr, lg, const):
    LAG = 2 + layer
    with Memory(nc, f"mo{layer}") as m:
        w = m.sb("w", [P, KD, D if layer == 0 else 256])
        wr = m.sb("w_router", [P, KD, E])
        g = m.sb("ln_g", [P, D])
        b = m.sb("ln_b", [P, D])
        xin = m.sb("x_in", [P, 2, D])
        xT = m.sb("xT", [P, KD, P])
        st = m.sb("stats", [P, 2, 18])
        eps = m.sb("eps", [P, 1])
        scale = m.sb("pool_scale", [P, D]) if layer else None
        pb = m.psum("pb", [P, 8, 512])
        q = {k: m.sem(k) for k in "in w w_rwkv0 w_rwkv1 mm res st var root rs nm n g x tr cp rl ev eps sc zero".split()}
        s_x = [m.sem(f"x{i}") for i in range(2)]
        block = m.block()

        @block.sync
        def _(sp):
            if layer == 0:
                wo = io["w_out"][0]
                for j in range(2):
                    sp.dma_start(w[:, 2 * j:2 * j + 2, :], wo[256 * j:256 * j + 256, :].rearrange("(k p) n -> p k n", p=P))\
                        .then_inc(q[f"w_rwkv{j}"], 16)
                for v in range(KVH):
                    sp.dma_start(w[HD * v:HD * v + HD, 4:8, :],
                                 wo[DA + 256 * v:DA + 256 * v + 256, :].rearrange("(m d) n -> d m n", d=HD)).then_inc(q["w"], 16)
            else:
                for gi in range(4):
                    sp.dma_start(w[:, 2 * gi:2 * gi + 2, :], io["w_pool"][0, gi].rearrange("(c p) n -> p c n", p=P))\
                        .then_inc(q["w"], 16)
            if layer == 0:
                for i in range(TILES):
                    if i >= 2:
                        sp.wait_ge(q["res"], i - 1)
                    src = io["x_prompt"][0, P * i:P * i + P, :] if i < NT else io["x_sample"][:, 0, :]
                    sp.dma_start(xin[0:rows(i), i % 2, :], src).then_inc(s_x[i % 2], 16)

        @block.gpsimd
        def _(pool):
            nc.gpsimd.memset(eps[:, :], LN_EPS).then_inc(q["eps"], 1)
            pool.dma_start(g[:, :], io["ln_mix_g"][layer:layer + 1, :].to_broadcast([P, D])).then_inc(q["in"], 16)
            pool.dma_start(b[:, :], io["ln_mix_b"][layer:layer + 1, :].to_broadcast([P, D])).then_inc(q["in"], 16)
            pool.dma_start(wr[:, :, :], io["w_router"].rearrange("(k p) e -> p k e", p=P)).then_inc(q["in"], 16)
            if layer:
                pool.dma_start(scale[:, :], io["pool_scale"].to_broadcast([P, D])).then_inc(q["in"], 16)
            nc.gpsimd.memset(lg[:, NT, :], 0.0).then_inc(q["zero"], 1)
            pool.wait_ge(q["in"], 48 if layer == 0 else 64)
            for i in range(TILES):
                norm_shift(nc, pool, q, i, xr, b)

        @block.tensor
        def _(pe):
            if layer:
                pe.wait_ge(q["w"], 64)

            def products(i):
                n = rows(i)
                if i >= 2:
                    pe.wait_ge(q["res"], i - 1)
                if layer == 0:
                    for k in range(KD):
                        if i == 0 and k % 2 == 0 and k <= 4:
                            pe.wait_ge(q[("w_rwkv0", "w_rwkv1", "w")[k // 2]], 16 if k < 4 else 32)
                        for h in range(2):
                            last = nc.tensor.matmul(pb[0:n, 2 * (i % 2) + h, :], lhs(k, i), w[:, k, 512 * h:512 * h + 512],
                                                    start=(k == 0), stop=(k == KD - 1))
                else:
                    for h in range(2):
                        for gi in (2 * h, 2 * h + 1):
                            for k in range(2):
                                last = nc.tensor.matmul(pb[0:n, 2 * (i % 2) + h, 256 * (gi % 2):256 * (gi % 2) + 256],
                                                        lhs(2 * gi + k, i), w[:, 2 * gi + k, :], start=(k == 0), stop=(k == 1))
                last.then_inc(q["mm"], 1)

            def transpose_x(i):
                n = rows(i)
                pe.wait_ge(q["x"], i + 1)
                for k in range(KD):
                    last = nc.tensor.transpose(pb[:, 4 + k // 4, P * (k % 4):P * (k % 4) + n], xr[0:n, i, P * k:P * k + P],
                                               const["ident"][0:n, 0:n])
                last.then_inc(q["tr"], 1)

            def router(i):
                n = rows(i)
                pe.wait_ge(q["cp"], i + 1)
                if i == 0:
                    pe.wait_ge(q["in"], 48 if layer == 0 else 64)
                if i >= 1:
                    pe.wait_ge(q["ev"], i)
                for k in range(KD):
                    last = nc.tensor.matmul(pb[0:n, 6, 0:E], xT[:, k, 0:n], wr[:, k, :], start=(k == 0), stop=(k == KD - 1))
                last.then_inc(q["rl"], 1)
            for i in range(TILES + LAG):
                if i >= LAG:
                    transpose_x(i - LAG)
                if i < TILES:
                    products(i)
                if i >= LAG:
                    router(i - LAG)

        @block.scalar
        def _(act):
            act.wait_ge(q["eps"], 1)

            def copy_x(i):
                n = rows(i)
                act.wait_ge(q["tr"], i + 1)
                nc.scalar.copy(xT[:, :, 0:n], pb[:, 4:6, :].rearrange("p b (k t) -> p (b k) t", k=4)[:, :, 0:n])\
                    .then_inc(q["cp"], 1)
            for i in range(TILES + LAG):
                if i >= LAG:
                    copy_x(i - LAG)
                if i < TILES:
                    norm_scalar(nc, act, q, i, xr, st, eps)

        @block.vector
        def _(dve):
            dve.wait_ge(q["in"], 48 if layer == 0 else 64)
            dve.wait_ge(q["zero"], 1)

            def take_logits(i):
                dve.wait_ge(q["rl"], i + 1)
                nc.vector.tensor_copy(lg[0:rows(i), i, :], pb[0:rows(i), 6, 0:E]).then_inc(q["ev"], 1)
            for i in range(TILES):
                n = rows(i)
                x = xr[0:n, i, :]
                if i > LAG:
                    take_logits(i - LAG - 1)
                dve.wait_ge(q["mm"], i + 1)
                banks = pb[0:n, 2 * (i % 2):2 * (i % 2) + 2, :].rearrange("p b n -> p (b n)")
                if layer == 0:
                    dve.wait_ge(s_x[i % 2], 16 * (i // 2 + 1))
                    nc.vector.scalar_tensor_tensor(out=x, in0=xin[0:n, i % 2, :], scalar=ALPHA, in1=banks,
                                                   op0=ALU.mult, op1=ALU.add).then_inc(q["res"], 1)
                else:
                    nc.vector.tensor_tensor(xin[0:n, i % 2, :], banks, scale[0:n, :], ALU.mult).then_inc(q["sc"], 1)
                    dve.wait_ge(q["sc"], i + 1)
                    nc.vector.scalar_tensor_tensor(out=x, in0=x, scalar=ALPHA, in1=xin[0:n, i % 2, :],
                                                   op0=ALU.mult, op1=ALU.add).then_inc(q["res"], 1)
                norm_vector(nc, dve, q, i, xr, st, g, gain_after=layer)
            if layer:
                norm_gain(nc, dve, q, TILES - 1, xr, g)
            for i in range(TILES - LAG - 1, TILES):
                take_logits(i)


def route(nc, io, layer, xr, lg, gates, slots, table, weights, const):
    with Memory(nc, f"ro{layer}") as m:
        br = m.sb("b_router", [P, E])
        valid = m.sb("valid", [P, TILES])
        earlier = m.sb("earlier", [P, P])
        ones = m.sb("ones", [P, P])
        blocks = m.sb("blocks", [P, NBLK])
        p = m.sb("probs", [P, TILES, E])
        w = m.sb("work", [P, TILES, E])
        best = m.sb("best", [P, 2, TILES, E])
        A = m.sb("assigned", [P, TILES, E])
        slot = m.sb("slot", [P, TILES, E])
        base = m.sb("counts_before", [P, TILES + 1, E])
        t9 = m.sb("per_token", [P, 6, TILES])
        gs = m.sb("group", [P, 6, TILES, NG])
        rank_e = m.sb("descending_experts", [P, E])
        rank_g = m.sb("descending_groups", [P, NG])
        thr = m.sb("thresholds", [P, TILES, E])
        nb = m.sb("blocks_per_expert", [P, 3, E])
        cmpb = m.sb("block_compare", [P, NBLK, E])
        tf = m.sb("table_f", [P, T_LEN])
        alt = m.sb("set_steps", [P, E])
        one = m.sb("one", [P, E])
        pb = m.psum("pb", [P, 8, 512])
        q = {k: m.sem(k) for k in "in io mx ex as rk chain slots sc tab".split()}
        block = m.block()
        N3 = [P, TILES, E]

        def per_token(a):
            return a.unsqueeze(2).to_broadcast(N3)

        @block.sync
        def _(sp):
            sp.dma_start(br[:, :], io["b_router"].rearrange("(a e) -> a e", a=1).to_broadcast([P, E])).then_inc(q["in"], 16)
            for dst, name in ((valid, "valid"), (earlier, "earlier"), (ones, "ones"), (blocks, "blocks"), (alt, "set_steps")):
                sp.dma_start(dst[:, :], io[f"c_{name}"]).then_inc(q["in"], 16)
            for u in range(EARLY):
                load_expert(sp, io, layer, u, u, weights)

        @block.tensor
        def _(pe):
            pe.wait_ge(q["in"], 96)
            pe.wait_ge(q["as"], 1)
            a = A[:, :, :].rearrange("p t e -> p (t e)")
            nc.tensor.matmul(pb[:, 0, 0:TILES * E], earlier[:, :], a, start=True, stop=True)
            nc.tensor.matmul(pb[:, 1, 0:TILES * E], ones[:, :], a, start=True, stop=True).then_inc(q["rk"], 1)

        @block.scalar
        def _(act):
            act.wait_ge(q["mx"], 1)
            nc.scalar.activation(p[:, :, :], p[:, :, :], ACT.Exp).then_inc(q["ex"], 1)

        @block.gpsimd
        def _(pool):
            nc.gpsimd.iota(rank_e[:, :], [[-1, E]], base=E, channel_multiplier=0,
                           allow_small_or_imprecise_dtypes=True)
            nc.gpsimd.iota(rank_g[:, :], [[-1, NG]], base=NG, channel_multiplier=0,
                           allow_small_or_imprecise_dtypes=True)
            nc.gpsimd.memset(one[:, :], 1.0)
            nc.gpsimd.iota(thr[:, :, :], [[P, TILES], [0, E]], base=0, channel_multiplier=0,
                           allow_small_or_imprecise_dtypes=True).then_inc(q["io"], 1)
            pool.wait_ge(q["slots"], 1)
            for i in range(TILES):
                n = rows(i)
                for c in range(2):
                    pool.indirect_dma_start(io["slots_in"], bass.IndirectOffsetOnAxis(ap=slots[0:n, i, c:c + 1], axis=0),
                                            xr[0:n, i, :], None).then_inc(q["sc"], 16)
            pool.wait_ge(q["sc"], 32 * TILES)

        @block.vector
        def _(dve):
            link = Linked(dve, q["chain"])
            tt, ts, red = nc.vector.tensor_tensor, nc.vector.tensor_scalar, nc.vector.tensor_reduce
            dve.wait_ge(q["in"], 96)
            dve.wait_ge(q["io"], 1)
            link(tt(p[:, :, :], lg[:, :, :], br[:, :].unsqueeze(1).to_broadcast(N3), ALU.add))
            link(red(t9[:, 0, :], p[:, :, :], AX, ALU.max))
            tt(p[:, :, :], p[:, :, :], per_token(t9[:, 0, :]), ALU.subtract).then_inc(q["mx"], 1)
            dve.wait_ge(q["ex"], 1)
            link(red(t9[:, 0, :], p[:, :, :], AX, ALU.add))
            link(nc.vector.reciprocal(t9[:, 0, :], t9[:, 0, :]))
            link(tt(p[:, :, :], p[:, :, :], per_token(t9[:, 0, :]), ALU.mult))
            pv = p[:, :, :].rearrange("p t (g e) -> p t g e", g=NG)
            e0, e1, e2, e3 = (pv[:, :, :, k] for k in range(EPG))
            tt(gs[:, 0], e0, e1, ALU.max)
            tt(gs[:, 1], e0, e1, ALU.min)
            tt(gs[:, 2], e2, e3, ALU.max)
            link(tt(gs[:, 3], e2, e3, ALU.min))
            tt(gs[:, 4], gs[:, 0], gs[:, 2], ALU.max)
            tt(gs[:, 5], gs[:, 0], gs[:, 2], ALU.min)
            link(tt(gs[:, 1], gs[:, 1], gs[:, 3], ALU.max))
            link(tt(gs[:, 5], gs[:, 5], gs[:, 1], ALU.max))
            link(tt(gs[:, 4], gs[:, 4], gs[:, 5], ALU.add))
            link(red(t9[:, 0, :], gs[:, 4], AX, ALU.max))
            G3 = [P, TILES, NG]
            link(tt(gs[:, 0], gs[:, 4], t9[:, 0, :].unsqueeze(2).to_broadcast(G3), ALU.is_equal))
            link(tt(gs[:, 0], gs[:, 0], rank_g[:, :].unsqueeze(1).to_broadcast(G3), ALU.mult))
            link(red(t9[:, 0, :], gs[:, 0], AX, ALU.max))
            link(tt(gs[:, 0], gs[:, 0], t9[:, 0, :].unsqueeze(2).to_broadcast(G3), ALU.is_equal))
            for k in range(EPG):
                last = tt(pv[:, :, :, k], pv[:, :, :, k], gs[:, 0], ALU.mult)
            link(last)
            link(ts(gs[:, 1], gs[:, 0], -1.0, None, ALU.add))
            for k in range(EPG):
                last = tt(pv[:, :, :, k], pv[:, :, :, k], gs[:, 1], ALU.add)
            link(last)
            for c in range(2):
                link(red(t9[:, 1 + c, :], p[:, :, :], AX, ALU.max))
                link(tt(w[:, :, :], p[:, :, :], per_token(t9[:, 1 + c, :]), ALU.is_equal))
                link(tt(w[:, :, :], w[:, :, :], rank_e[:, :].unsqueeze(1).to_broadcast(N3), ALU.mult))
                link(red(t9[:, 0, :], w[:, :, :], AX, ALU.max))
                link(tt(best[:, c], w[:, :, :], per_token(t9[:, 0, :]), ALU.is_equal))
                if c == 0:
                    link(nc.vector.scalar_tensor_tensor(out=p[:, :, :], in0=best[:, 0], scalar=-4.0, in1=p[:, :, :],
                                                        op0=ALU.mult, op1=ALU.add))
            link(tt(A[:, :, :], best[:, 0], best[:, 1], ALU.add))
            tt(A[:, :, :], A[:, :, :], per_token(valid[:, :]), ALU.mult).then_inc(q["as"], 1)
            link(tt(t9[:, 3, :], t9[:, 1, :], t9[:, 2, :], ALU.add))
            link(nc.vector.reciprocal(t9[:, 3, :], t9[:, 3, :]))
            for c in range(2):
                link(tt(gates[:, :, c], t9[:, 1 + c, :], t9[:, 3, :], ALU.mult))
            dve.wait_ge(q["rk"], 1)
            link(nc.vector.memset(base[:, 0, :], 0.0))
            for i in range(TILES):
                link(tt(base[:, i + 1, :], base[:, i, :], pb[:, 1, E * i:E * i + E], ALU.add))
            link(tt(slot[:, :, :], base[:, 0:TILES, :], pb[:, 0, 0:TILES * E].rearrange("p (t e) -> p t e", t=TILES), ALU.add))
            link(tt(w[:, :, :], base[:, TILES, :].unsqueeze(1).to_broadcast(N3), thr[:, :, :], ALU.is_gt))
            link(red(nb[:, 0, :], w[:, :, :].rearrange("p t e -> p e t"), AX, ALU.add))
            link(nc.vector.tensor_tensor_scan(nb[:, 1, :], one[:, :], nb[:, 0, :], 0.0, ALU.mult, ALU.add))
            link(tt(nb[:, 2, :], nb[:, 1, :], nb[:, 0, :], ALU.subtract))
            link(ts(nb[:, 2, :], nb[:, 2, :], float(P), None, ALU.mult))
            link(tt(slot[:, :, :], slot[:, :, :], nb[:, 2, :].unsqueeze(1).to_broadcast(N3), ALU.add))
            for c in range(2):
                link(tt(w[:, :, :], slot[:, :, :], best[:, c], ALU.mult))
                link(red(t9[:, 4 + c, :], w[:, :, :], AX, ALU.add))
            for c in range(2):
                last = nc.vector.tensor_copy(slots[:, :, c], t9[:, 4 + c, :])
            last.then_inc(q["slots"], 1)
            B3 = [P, NBLK, E]
            link(tt(cmpb[:, :, :], blocks[:, :].unsqueeze(2).to_broadcast(B3), nb[:, 1, :].unsqueeze(1).to_broadcast(B3),
                    ALU.is_ge))
            link(red(tf[:, 0:NBLK], cmpb[:, :, :], AX, ALU.add))
            link(ts(tf[:, 0:NBLK], tf[:, 0:NBLK], float(E - 1), None, ALU.min))
            link(tt(cmpb[:, :, :], cmpb[:, :, :], alt[:, :].unsqueeze(1).to_broadcast(B3), ALU.mult))
            link(red(tf[:, T_SETS:T_SETS + NBLK], cmpb[:, :, :], AX, ALU.add))
            ts(tf[:, T_ENDS:T_ENDS + E], nb[:, 1, :], 1.0, None, ALU.add)
            link(ts(cmpb[:, 0, :], blocks[:, 0:NBLK:2], nb[:, 1, E - 1:E], None, ALU.is_lt))
            link(red(tf[:, T_LAST:T_LAST + 1], cmpb[:, 0, :], AX, ALU.add))
            link(ts(tf[:, T_LAST:T_LAST + 1], tf[:, T_LAST:T_LAST + 1], -1.0, None, ALU.add))
            nc.vector.tensor_copy(table[:, :], tf[0:1, :]).then_inc(q["tab"], 1)
            dve.wait_ge(q["tab"], 1)


def load_expert(sp, io, layer, e, u, weights):
    wgu, wd, s_w = weights
    for half, name in enumerate(("w_ex_gate", "w_ex_up")):
        sp.dma_start(wgu[:, u, :, FF * half:FF * half + FF],
                     io[name][layer][bass.ds(e, 1)].rearrange("a (k p) f -> p (a k) f", p=P)).then_inc(s_w[u], 16)
    sp.dma_start(wd[:, u, :, :], io["w_ex_down"][layer][bass.ds(e, 1)].rearrange("a (k p) n -> p (a k) n", p=P))\
        .then_inc(s_w[u], 16)


def experts(nc, io, layer, table, weights, const):
    with Memory(nc, f"ex{layer}") as m:
        wgu, wd, s_w = weights
        xs = m.sb("x_rows", [P, 2, D])
        xT = m.sb("xT", [P, 2, KD, P])
        h = m.sb("hidden", [P, 2, FF])
        hT = m.sb("hiddenT", [P, 2, 2, P])
        y = m.sb("y_rows", [P, 2, D])
        pb = m.psum("pb", [P, 8, 512])
        q = {k: m.sem(k) for k in "gu xt down_plus_1 ht silu h xca xcv hc ya yv loaded stored".split()}
        s_xs = [m.sem(f"x_rows{u}") for u in range(2)]
        s_st = [m.sem(f"stored{u}") for u in range(2)]
        block = m.block()
        pairs = NBLK // 2
        least = (2 * TT // P + 1) // 2

        def entry(eng, at, low, high):
            return eng.value_load(table[0:1, bass.ds(at, 1)], min_val=low, max_val=high)

        def steps(eng, body):
            last = entry(eng, T_LAST, least - 1, pairs - 1)
            for u in range(2):
                body(0, u, True)
            with eng.Fori(1, pairs) as i:
                with eng.If(i <= last):
                    for u in range(2):
                        body(i, u, False)
            return last

        @block.sync
        def _(sp):
            def load(e, u):
                sp.wait_ge(q["down_plus_1"], entry(sp, T_ENDS + e - SETS, 1, NBLK + 1))
                load_expert(sp, io, layer, e, u, weights)

            def arrived(i, u):
                sp.wait_ge(s_w[u], 48 * i + 48)
                sp.sem_inc(q["loaded"], 1)
            sp.wait_ge(s_xs[0], 16)
            for u in range(EARLY, SETS):
                load_expert(sp, io, layer, u, u, weights)
            for u in range(SETS):
                arrived(0, u)
            with sp.Fori(1, E // SETS) as i:
                for u in range(SETS):
                    load(SETS * i + u, u)
                    arrived(i, u)

        @block.gpsimd
        def _(pool):
            def load_rows(j, u):
                pool.dma_start(xs[:, u, :], io["slots_in"][bass.ds(j * P, P), :]).then_inc(s_xs[u], 16)

            def body(i, u, first):
                j = 2 * i + u
                if not (first and u == 0):
                    pool.wait_ge(q["xt"], j)
                load_rows(j + 1, 1 - u)
            load_rows(0, 0)
            steps(pool, body)

        @block.tensor
        def _(pe):
            mm = nc.tensor.matmul

            def transpose_x(i, u):
                pe.wait_ge(s_xs[u], 16 * i + 16)
                for k in range(KD):
                    t = nc.tensor.transpose(pb[:, k // 4, P * (k % 4):P * (k % 4) + P], xs[:, u, P * k:P * k + P],
                                            const["ident"][:, :])
                t.then_inc(q["xt"], 1)

            def down(i, u, c):
                j = 2 * i + u
                w = wd[:, bass.ds(c, 1), :, :].rearrange("p c k n -> p (c k) n")
                pe.wait_ge(q["hc"], j + 1)
                for half in range(2):
                    for k in range(2):
                        t = mm(pb[:, 5 + half, :], hT[:, u, k, :], w[:, k, 512 * half:512 * half + 512],
                               start=(k == 0), stop=(k == 1))
                t.then_inc(q["down_plus_1"], 1)

            def body(i, u, first):
                j = 2 * i + u
                c = entry(pe, T_SETS + j, 0, SETS - 1)
                expert = entry(pe, j, 0, E - 1)
                if not (first and u == 0):
                    c_before = entry(pe, T_SETS + j - 1, 0, SETS - 1)
                w = wgu[:, bass.ds(c, 1), :, :].rearrange("p c k n -> p (c k) n")
                pe.wait_ge(q["xca"], j + 1)
                pe.wait_ge(q["xcv"], j + 1)
                pe.wait_ge(q["loaded"], expert + 1)
                if not first:
                    pe.wait_ge(q["h"], j - 1)
                for k in range(KD):
                    t = mm(pb[:, 2 + u, :], xT[:, u, k, :], w[:, k, :], start=(k == 0), stop=(k == KD - 1))
                t.then_inc(q["gu"], 1)
                transpose_x(i + u, 1 - u)
                if not (first and u == 0):
                    if not first:
                        pe.wait_ge(q["ya"], j - 1)
                        pe.wait_ge(q["yv"], j - 1)
                    down(i - 1 + u, 1 - u, c_before)
                pe.wait_ge(q["h"], j + 1)
                if not (first and u == 0):
                    pe.wait_ge(q["hc"], j)
                for k in range(2):
                    t = nc.tensor.transpose(pb[:, 4, P * k:P * k + P], h[:, u, P * k:P * k + P], const["ident"][:, :])
                t.then_inc(q["ht"], 1)
            transpose_x(0, 0)
            pe.sem_inc(q["down_plus_1"], 1)
            last = steps(pe, body)
            c = entry(pe, 2 * last + (T_SETS + 1), 0, SETS - 1)
            pe.wait_ge(q["ya"], 2 * last + 1)
            pe.wait_ge(q["yv"], 2 * last + 1)
            down(last, 1, c)

        def copy_x(eng, copy, u, half, sem, j):
            eng.wait_ge(q["xt"], j + 1)
            copy(xT[:, u, 4 * half:4 * half + 4, :], pb[:, half, :].rearrange("p (k t) -> p k t", k=4)).then_inc(q[sem], 1)

        @block.scalar
        def _(act):
            def out(i, u, first):
                j = 2 * i + u
                act.wait_ge(q["down_plus_1"], j + 2)
                if not first:
                    act.wait_ge(s_st[u], 16 * i)
                nc.scalar.copy(y[:, u, 0:512], pb[:, 5, :]).then_inc(q["ya"], 1)
                act.wait_ge(q["ya"], j + 1)
                act.wait_ge(q["yv"], j + 1)
                act.dma_start(io["slots_out"][bass.ds(j * P, P), :], y[:, u, :]).then_inc(s_st[u], 16)

            def body(i, u, first):
                j = 2 * i + u
                act.wait_ge(q["gu"], j + 1)
                if not first:
                    act.wait_ge(q["ht"], j - 1)
                nc.scalar.activation(h[:, u, :], pb[:, 2 + u, 0:FF], ACT.Silu).then_inc(q["silu"], 1)
                copy_x(act, nc.scalar.copy, 1 - u, 0, "xca", j + 1)
                if not (first and u == 0):
                    out(i - 1 + u, 1 - u, first)
                act.wait_ge(q["ht"], j + 1)
                nc.scalar.copy(hT[:, u, :, :], pb[:, 4, 0:2 * P].rearrange("p (k t) -> p k t", k=2)).then_inc(q["hc"], 1)
            copy_x(act, nc.scalar.copy, 0, 0, "xca", 0)
            last = steps(act, body)
            out(last, 1, False)
            for u in range(2):
                act.wait_ge(s_st[u], 16 * last + 16)
            act.sem_inc(q["stored"], 1)

        @block.vector
        def _(dve):
            def out(i, u, first):
                j = 2 * i + u
                dve.wait_ge(q["down_plus_1"], j + 2)
                if not first:
                    dve.wait_ge(s_st[u], 16 * i)
                nc.vector.tensor_copy(y[:, u, 512:1024], pb[:, 6, :]).then_inc(q["yv"], 1)

            def body(i, u, first):
                j = 2 * i + u
                dve.wait_ge(q["silu"], j + 1)
                nc.vector.tensor_tensor(h[:, u, :], h[:, u, :], pb[:, 2 + u, FF:2 * FF], ALU.mult).then_inc(q["h"], 1)
                copy_x(dve, nc.vector.tensor_copy, 1 - u, 1, "xcv", j + 1)
                if not (first and u == 0):
                    out(i - 1 + u, 1 - u, first)
            copy_x(dve, nc.vector.tensor_copy, 0, 1, "xcv", 0)
            last = steps(dve, body)
            out(last, 1, False)


def combine(nc, io, layer, xr, gates, slots, const):
    with Memory(nc, f"cb{layer}") as m:
        r = m.sb("expert_rows", [P, TILES, 2, D])
        g = m.sb("ln_g", [P, D])
        b = m.sb("ln_b", [P, D])
        st = m.sb("stats", [P, 2, 18])
        eps = m.sb("eps", [P, 1])
        q = {k: m.sem(k) for k in "in eps first both res st var root rs nm n g x out".split()}
        s_r = [m.sem(f"rows{i}") for i in range(TILES)]
        AHEAD = 4
        block = m.block()

        @block.gpsimd
        def _(pool):
            nc.gpsimd.memset(eps[:, :], LN_EPS).then_inc(q["eps"], 1)
            for i in range(TILES + AHEAD):
                if i < TILES:
                    n = rows(i)
                    for c in range(2):
                        pool.indirect_dma_start(r[0:n, i, c, :], None, io["slots_out"],
                                                bass.IndirectOffsetOnAxis(ap=slots[0:n, i, c:c + 1], axis=0))\
                            .then_inc(s_r[i], 16)
                if i == AHEAD:
                    pool.wait_ge(q["in"], 32)
                if i >= AHEAD:
                    norm_shift(nc, pool, q, i - AHEAD, xr, b)

        @block.sync
        def _(sp):
            sp.dma_start(g[:, :], io["ln_ffn_g"][layer:layer + 1, :].to_broadcast([P, D])).then_inc(q["in"], 16)
            sp.dma_start(b[:, :], io["ln_ffn_b"][layer:layer + 1, :].to_broadcast([P, D])).then_inc(q["in"], 16)
            if layer == 1:
                for i in range(TILES):
                    sp.wait_ge(q["x"], i + 1)
                    dst = io["o_y_prompt"][0, P * i:P * i + P, :] if i < NT else io["o_y_sample"][:, 0, :]
                    sp.dma_start(dst, xr[0:rows(i), i, :]).then_inc(q["out"], 16)
                sp.wait_ge(q["out"], 16 * TILES)

        @block.scalar
        def _(act):
            act.wait_ge(q["eps"], 1)

            def first_gate(i):
                n = rows(i)
                act.wait_ge(s_r[i], 32)
                nc.scalar.activation(r[0:n, i, 0, :], r[0:n, i, 0, :], ACT.Identity,
                                     scale=gates[0:n, i, 0:1]).then_inc(q["first"], 1)
            first_gate(0)
            for i in range(TILES):
                if i + 1 < TILES:
                    first_gate(i + 1)
                norm_scalar(nc, act, q, i, xr, st, eps)

        @block.vector
        def _(dve):
            stt = nc.vector.scalar_tensor_tensor
            dve.wait_ge(q["in"], 32)
            for i in range(TILES):
                n = rows(i)
                x = xr[0:n, i, :]
                dve.wait_ge(q["first"], i + 1)
                r1, r2 = r[0:n, i, 0, :], r[0:n, i, 1, :]
                stt(out=r1, in0=r2, scalar=gates[0:n, i, 1:2], in1=r1, op0=ALU.mult, op1=ALU.add).then_inc(q["both"], 1)
                dve.wait_ge(q["both"], i + 1)
                stt(out=x, in0=x, scalar=ALPHA, in1=r1, op0=ALU.mult, op1=ALU.add).then_inc(q["res"], 1)
                norm_vector(nc, dve, q, i, xr, st, g)
            norm_gain(nc, dve, q, TILES - 1, xr, g)




def constants():
    i = np.arange(P)
    same = (i[:, None] // CH) == (i[None, :] // CH)
    up = (i[:, None] < i[None, :]) & same
    tabs = {"ident": np.eye(P), "low": up.T, "up": up, "up_incl": up | np.eye(P, dtype=bool),
            "head_ones": (i[:, None] // HD) == (i[None, :] // HD),
            "earlier": i[:, None] < i[None, :], "ones": np.ones((P, P))}
    for lev in range(6):
        b = 1 << lev
        off = ((i[:, None] // (2 * b)) == (i[None, :] // (2 * b))) & ((i[:, None] // b) % 2 == 1) & ((i[None, :] // b) % 2 == 0)
        if lev == 0:
            tabs["lev0"] = off
        tabs[f"lev{lev}T"] = off.T
    dist = 2 * WIN - 1 - np.arange(384)
    n = np.maximum(dist, 0)
    scaled = np.log(np.maximum(n, 16).astype(np.float32) / np.float32(16)) / np.float32(math.log(128 / 16))
    large = np.minimum(16 + (scaled * np.float32(16)).astype(np.int32), NBUCK - 1)
    bucket = np.where(n < 16, n, large)
    valid = (dist >= 0) & (dist <= WIN)
    onehot = np.zeros((NBUCK + 1, 384))
    onehot[np.where(valid, bucket, NBUCK), np.arange(384)] = 1
    r = np.arange(NS * 8)
    own = np.where((r[:, None] // 8) == np.arange(NS)[None, :], 0.0, NEG)
    cnt = np.minimum(np.array(POOLW)[:, None], np.arange(16)[None, :] + 1)
    tok = i[:, None] + P * np.arange(TILES)[None, :]
    out = {**{k: v for k, v in tabs.items()}, "onehot": onehot, "neg": np.full((1, 8), NEG), "own": own,
           "rowhead": np.tile(np.eye(8), (NS, 1)),
           "invcnt": np.tile((1.0 / cnt.astype(np.float32)).reshape(1, 64), (P, 1)),
           "valid": tok < TT, "blocks": np.tile(np.arange(NBLK)[None, :], (P, 1)),
           "set_steps": np.tile(np.where(np.arange(E) % SETS == SETS - 1, 1.0 - SETS, 1.0)[None, :], (P, 1))}
    return {f"c_{k}": np.ascontiguousarray(np.asarray(v).astype(np.float32)) for k, v in out.items()}


SQUARE = ("ident", "low", "up", "up_incl", "head_ones", "earlier", "ones", "lev0", "lev0T", "lev1T", "lev2T", "lev3T", "lev4T", "lev5T")

_INS = ['x_prompt', 'x_sample', 'state_rwkv', 'state_shift', 'cache_swa_k', 'cache_swa_v', 'state_pool', 'w_in',
        'tshift_mu', 'decay_w0', 'decay_w2', 'iclr_a0', 'iclr_a2', 'gate_w2', 'k_k', 'k_a', 'r_k', 'lnx_g', 'lnx_b',
        'attn_sinks', 'rel_bias', 'w_out', 'w_pool', 'pool_scale', 'ln_mix_g', 'ln_mix_b', 'ln_ffn_g', 'ln_ffn_b',
        'w_router', 'b_router', 'w_ex_gate', 'w_ex_up', 'w_ex_down']
_OUTS = [('y_prompt', (1, T, D)), ('y_sample', (NS, 1, D)), ('rwkv_prompt', (1, 1, HA, HD, HD)),
         ('rwkv_sample', (1, NS, HA, HD, HD)), ('shift_prompt', (1, 1, D)), ('shift_sample', (1, NS, D)),
         ('k_prompt', (1, 1, WIN, KVH, HD)), ('k_sample', (1, NS, WIN, KVH, HD)),
         ('v_prompt', (1, 1, WIN, KVH, HD)), ('v_sample', (1, NS, WIN, KVH, HD)),
         ('pool_prompt', (1, 1, KEEP, D)), ('pool_sample', (1, NS, KEEP, D))]


def build(nc, io):
    with ExitStack() as whole:
        sb = lambda ctx, name, shape, dt=F32: ctx.enter_context(nc.sbuf_tensor(name, shape, dt))
        const = {"ident": sb(whole, "k_ident", [P, P])}
        lg = sb(whole, "logits", [P, TILES, E])
        gates = sb(whole, "gates", [P, TILES, 2])
        slots = sb(whole, "slots", [P, TILES, 2], U32)
        table = sb(whole, "block_experts", [1, T_LEN], I32)
        with ExitStack() as layer0:
            yb = sb(layer0, "attention_out", [P, 4, TT])
            mix_const = {k: sb(layer0, f"k_{k}", [P, P]) for k in SQUARE if k not in ("ident", "earlier", "ones")}
            const.update(mix_const)
            const["lnx_eps"] = sb(layer0, "lnx_eps", [P, 1])
            pr = sb(layer0, "projected", [P, 14, PC])
            vec = {k: sb(layer0, f"v_{k}", [P, 4]) for k in ("decay_w0", "iclr_a0", "k_k", "k_a", "r_k", "lnx_g", "lnx_b")}
            vec["mu"] = sb(layer0, "v_mu", [P, 14])
            loads = {k: (t[:, :], io[f"c_{k}"]) for k, t in mix_const.items()}
            for k in ("decay_w0", "iclr_a0", "k_k", "k_a", "lnx_g", "lnx_b"):
                loads[k] = (vec[k][:, :], by_partition(io[k][0], 4))
            loads["r_k"] = (vec["r_k"][:, :], by_partition(io["r_k"][0].rearrange("h d -> (h d)"), 4))
            mu = io["tshift_mu"][0]
            loads["mu"] = (vec["mu"][:, 0:12], by_partition(mu[0:3 * DA], 12))
            lo = 3 * DA
            loads["mu_lora"] = (vec["mu"][0:WL + AL, 12:13], mu[lo:lo + WL + AL].rearrange("(p a) -> p a", a=1))
            loads["mu_gate"] = (vec["mu"][0:GL, 13:14], mu[lo + WL + AL:lo + WL + AL + GL].rearrange("(p a) -> p a", a=1))
            with ExitStack() as attention:
                pq = sb(attention, "projected_qkv", [P, 6, PC])
                project(nc, io, pr, pq, loads, const)
                attend(nc, io, pq, yb, const)
                attend_samples(nc, io, pq, yb, const)
            with ExitStack() as rwkv:
                mx = sb(rwkv, "mixed", [P, 12, TT])
                cumx = sb(rwkv, "log_decay_before", [P, 4, TT])
                shift_mix(nc, io, pr, mx, cumx, vec, const)
                rwkv_sample(nc, io, pr, mx, const)
                rwkv_chunks(nc, io, pr, mx, cumx, const)
                rwkv_norm(nc, io, pr, mx, vec, const)
            xr = whole.enter_context(nc.sbuf_tensor("x_rows", [P, TILES, D], F32, side="right"))
            mix_out(nc, io, 0, lambda k, i: (pr if k < 4 else yb)[:, k % 4, P * i:P * i + rows(i)], xr, lg, const)
        for layer in range(2):
            if layer == 1:
                with ExitStack() as pooled:
                    feats = sb(pooled, "pooled", [P, KD, TT])
                    pool_features(nc, io, xr, feats, const)
                    mix_out(nc, io, 1, lambda k, i: feats[:, k, P * i:P * i + rows(i)], xr, lg, const)
            with Memory(nc, f"ew{layer}") as m:
                weights = (m.sb("w_gate_up", [P, SETS, KD, 2 * FF]), m.sb("w_down", [P, SETS, 2, D]),
                           [m.sem(f"weights{u}") for u in range(SETS)])
                route(nc, io, layer, xr, lg, gates, slots, table, weights, const)
                experts(nc, io, layer, table, weights, const)
            combine(nc, io, layer, xr, gates, slots, const)


def declare(nc, inputs):
    arrays, io = {}, {}
    for name in _INS:
        a = np.ascontiguousarray(inputs[name])
        arrays[f"in_{name}"] = a
        io[name] = nc.dram_tensor(f"in_{name}", a.shape, F32, kind="ExternalInput").ap()
    for name, a in constants().items():
        arrays[f"in_{name}"] = a
        io[name] = nc.dram_tensor(f"in_{name}", a.shape, F32, kind="ExternalInput").ap()
    for name, shape in _OUTS:
        io["o_" + name] = nc.dram_tensor(f"out_{name}", shape, F32, kind="ExternalOutput").ap()
    for name, shape in (("bias_scratch", (8, P * 384)), ("sample_scratch", (6, NS, DA)), ("sample_y", (NS, DA)),
                        ("slots_in", (SLOTS, D)), ("slots_out", (NBLK * P, D))):
        io[name] = nc.dram_tensor(f"scratch_{name}", shape, F32, kind="Internal").ap()
    return arrays, io


def kernel(**inputs):
    import concourse.bacc as bacc
    from concourse.bass_utils import run_bass_kernel_spmd

    nc = bacc.Bacc("TRN2", target_bir_lowering=False, num_devices=1)
    arrays, io = declare(nc, inputs)
    build(nc, io)
    r = run_bass_kernel_spmd(nc, [arrays], core_ids=[0])
    return tuple(r.results[0][f"out_{name}"] for name, _ in _OUTS)
```
